# Optimizing a Trainium2 kernel written in Bass

```python
import jax
import jax.numpy as jnp
from jax import lax
import numpy as np

D_MODEL = 1024
BATCH = 1
SEQ = 1024
DEPTH = 2
DEC_BATCH = 1
DEC_SEQ = 64
PAST_LEN = 512

CHUNK = 64
QBLOCK = 128
N_BRANCH = 3
BRANCH_W = D_MODEL // 2
H_RET = 4
DV_RET = BRANCH_W // H_RET
DK_RET = DV_RET // 2
ROPE_BASE = 10000.0
H_FOX = 8
HD_FOX = BRANCH_W // H_FOX
H_GDN = 4
DK_GDN = BRANCH_W // H_GDN
DV_GDN = BRANCH_W // H_GDN
CONV_W = 4
CONV_CH = 2 * H_GDN * DK_GDN + H_GDN * DV_GDN
NORM_EPS = 1e-6
IN_SPLITS = (H_RET * DK_RET, H_RET * DK_RET, H_RET * DV_RET, BRANCH_W,
             H_FOX * HD_FOX, H_FOX * HD_FOX, H_FOX * HD_FOX, H_FOX, BRANCH_W,
             H_GDN * DK_GDN, H_GDN * DK_GDN, H_GDN * DV_GDN, H_GDN, H_GDN, BRANCH_W,
             N_BRANCH * D_MODEL)
IN_W = sum(IN_SPLITS)

kernel_name = 'hybrid_stream_encoder_step'

def rmsnorm(x, w):
    xf = x.astype(jnp.float32)
    xf = xf * lax.rsqrt(jnp.mean(xf * xf, axis=-1, keepdims=True) + NORM_EPS)
    return (xf * w.astype(jnp.float32)).astype(x.dtype)

def l2norm(x):
    return x * lax.rsqrt(jnp.sum(x * x, axis=-1, keepdims=True) + NORM_EPS)

def rotary(x, pos):
    half = x.shape[-1] // 2
    inv_freq = ROPE_BASE ** (-jnp.arange(half, dtype=jnp.float32) / half)
    ang = pos.astype(jnp.float32)[:, None] * inv_freq[None, :]
    cos = jnp.cos(ang)[None, :, None, :]
    sin = jnp.sin(ang)[None, :, None, :]
    xf = x.astype(jnp.float32)
    x1, x2 = xf[..., :half], xf[..., half:]
    return jnp.concatenate([x1 * cos - x2 * sin, x2 * cos + x1 * sin], axis=-1)

def retention(q, k, v, s0, chunk):
    B, S, H, DK = q.shape
    n = S // chunk
    log_g = jnp.log1p(-jnp.exp2(-5.0 - jnp.arange(H, dtype=jnp.float32)))
    i = jnp.arange(chunk, dtype=jnp.float32)
    d_intra = jnp.exp(jnp.abs(i[:, None] - i[None, :])[None] * log_g[:, None, None])
    d_q = jnp.exp((i[:, None] + 1.0) * log_g[None, :])
    d_k = jnp.exp((chunk - 1.0 - i)[:, None] * log_g[None, :])
    d_c = jnp.exp(chunk * log_g)

    def split(t):
        return t.reshape(B, n, chunk, H, t.shape[-1]).swapaxes(0, 1)

    def step(s, blk):
        qb, kb, vb = blk
        a = jnp.einsum('bihd,bjhd->bhij', qb, kb) * d_intra
        o = (jnp.einsum('bhij,bjhe->bihe', a, vb)
             + jnp.einsum('bihd,bhde->bihe', qb * d_q[None, :, :, None], s))
        s = s * d_c[:, None, None] + jnp.einsum('bjhd,bjhe->bhde', kb * d_k[None, :, :, None], vb)
        return s, o

    s, o = lax.scan(step, s0, (split(q), split(k), split(v)))
    return o.swapaxes(0, 1).reshape(B, S, H, v.shape[-1]), s

def fox_block(q, k, v, fq, fk, qpos, kpos):
    logits = jnp.einsum('bhqd,bhkd->bhqk', q, k).astype(jnp.float32) * (q.shape[-1] ** -0.5)
    logits = logits + fq[..., :, None] - fk[..., None, :]
    logits = jnp.where(qpos[:, None] >= kpos[None, :], logits, -jnp.inf)
    p = jax.nn.softmax(logits, axis=-1)
    return jnp.einsum('bhqk,bhkd->bhqd', p.astype(v.dtype), v)

def fox_prompt(q, k, v, fcum):
    B, H, S, Dh = q.shape
    nb = S // QBLOCK
    pos = jnp.arange(S)
    qb = q.reshape(B, H, nb, QBLOCK, Dh).transpose(2, 0, 1, 3, 4)
    fb = fcum.reshape(B, H, nb, QBLOCK).transpose(2, 0, 1, 3)
    pb = pos.reshape(nb, QBLOCK)
    o = lax.map(lambda blk: fox_block(blk[0], k, v, blk[1], fcum, blk[2], pos), (qb, fb, pb))
    return o.transpose(1, 2, 0, 3, 4).reshape(B, H, S, Dh)

def causal_conv_silu(u, buf, w):
    S = u.shape[1]
    full = jnp.concatenate([buf.astype(u.dtype), u], axis=1)
    y = full[:, 0:S] * w[0]
    for j in range(1, CONV_W):
        y = y + full[:, j:j + S] * w[j]
    return jax.nn.silu(y), full[:, -(CONV_W - 1):]

def gated_delta_rule(q, k, v, g, beta, s0, chunk):
    B, S, H, DK = q.shape
    n = S // chunk

    def split(t):
        return t.reshape(B, n, chunk, H, t.shape[-1]).transpose(1, 0, 3, 2, 4)

    gc = split(g[..., None])[..., 0]
    bc = split(beta[..., None])[..., 0]
    tri = jnp.tril(jnp.ones((chunk, chunk), bool))
    strict = jnp.tril(jnp.ones((chunk, chunk), bool), -1)
    eye = jnp.eye(chunk, dtype=jnp.float32)

    def step(s, blk):
        qb, kb, vb, gb, bb = blk
        G = jnp.cumsum(gb, axis=-1)
        decay = jnp.exp(jnp.where(tri, G[..., :, None] - G[..., None, :], -jnp.inf))
        a = jnp.where(strict, jnp.einsum('bhik,bhjk->bhij', kb, kb) * decay, 0.0) * bb[..., :, None]
        lower = eye + a
        u = lax.linalg.triangular_solve(lower, vb * bb[..., None], left_side=True,
                                        lower=True, unit_diagonal=True)
        w = lax.linalg.triangular_solve(lower, kb * (bb * jnp.exp(G))[..., None], left_side=True,
                                        lower=True, unit_diagonal=True)
        u = u - jnp.einsum('bhck,bhkv->bhcv', w, s)
        o = (jnp.einsum('bhck,bhkv->bhcv', qb * jnp.exp(G)[..., None], s)
             + jnp.einsum('bhij,bhjv->bhiv', jnp.einsum('bhik,bhjk->bhij', qb, kb) * decay, u))
        g_last = G[..., -1:]
        s = s * jnp.exp(g_last)[..., None] + jnp.einsum(
            'bhck,bhcv->bhkv', kb * jnp.exp(g_last - G)[..., None], u)
        return s, o

    s, o = lax.scan(step, s0, (split(q), split(k), split(v), gc, bc))
    return o.transpose(1, 0, 3, 2, 4).reshape(B, S, H, v.shape[-1]), s

def trunk_layer(x, c, pos, hist, norm_w, ada_w, ada_b, w_in, fox_f_bias, gdn_a_log,
                gdn_dt_bias, gdn_conv_w, ret_norm_w, gdn_norm_w, w_branch, w_out):
    B, S, _ = x.shape
    f32 = jnp.float32
    mod = jax.nn.silu(c) @ ada_w + ada_b
    shift, scale, gate = jnp.split(mod[:, None, :], 3, axis=-1)
    h = rmsnorm(x, norm_w) * (1.0 + scale) + shift
    proj = h @ w_in
    (rq, rk, rv, rz, fq, fk, fv, ff, fz, gq, gk, gv, ga, gb, gz, mg) = jnp.split(
        proj, np.cumsum(IN_SPLITS)[:-1].tolist(), axis=-1)

    if hist is None:
        ret_s0 = jnp.zeros((B, H_RET, DK_RET, DV_RET), f32)
        gdn_s0 = jnp.zeros((B, H_GDN, DK_GDN, DV_GDN), f32)
        conv_buf = jnp.zeros((B, CONV_W - 1, CONV_CH), proj.dtype)
        chunk = CHUNK
    else:
        fox_k_c, fox_v_c, fox_lf_c, ret_s0, gdn_s0, conv_buf = hist
        chunk = S

    q_r = rotary(rq.reshape(B, S, H_RET, DK_RET), pos)
    k_r = rotary(rk.reshape(B, S, H_RET, DK_RET), pos) * (DK_RET ** -0.5)
    v_r = rv.reshape(B, S, H_RET, DV_RET).astype(f32)
    o_r, ret_s = retention(q_r, k_r, v_r, ret_s0.astype(f32), chunk)
    o_ret = rmsnorm(o_r, ret_norm_w.reshape(H_RET, DV_RET)).reshape(B, S, BRANCH_W)
    o_ret = o_ret.astype(x.dtype) * jax.nn.silu(rz)

    q_f = fq.reshape(B, S, H_FOX, HD_FOX).transpose(0, 2, 1, 3)
    k_f = fk.reshape(B, S, H_FOX, HD_FOX).transpose(0, 2, 1, 3)
    v_f = fv.reshape(B, S, H_FOX, HD_FOX).transpose(0, 2, 1, 3)
    logf = jax.nn.log_sigmoid(ff.astype(f32) + fox_f_bias.astype(f32)).transpose(0, 2, 1)
    if hist is None:
        o_f = fox_prompt(q_f, k_f, v_f, jnp.cumsum(logf, axis=-1))
    else:
        past = fox_k_c.shape[2]
        k_all = jnp.concatenate([fox_k_c.astype(k_f.dtype), k_f], axis=2)
        v_all = jnp.concatenate([fox_v_c.astype(v_f.dtype), v_f], axis=2)
        fcum = jnp.cumsum(jnp.concatenate([fox_lf_c.astype(f32), logf], axis=-1), axis=-1)
        o_f = fox_block(q_f, k_all, v_all, fcum[..., past:], fcum, pos, jnp.arange(past + S))
    o_fox = o_f.transpose(0, 2, 1, 3).reshape(B, S, BRANCH_W) * jax.nn.silu(fz)

    qkv, conv_new = causal_conv_silu(jnp.concatenate([gq, gk, gv], axis=-1), conv_buf, gdn_conv_w)
    q_g, k_g, v_g = jnp.split(qkv.astype(f32), [H_GDN * DK_GDN, 2 * H_GDN * DK_GDN], axis=-1)
    q_g = l2norm(q_g.reshape(B, S, H_GDN, DK_GDN)) * (DK_GDN ** -0.5)
    k_g = l2norm(k_g.reshape(B, S, H_GDN, DK_GDN))
    v_g = v_g.reshape(B, S, H_GDN, DV_GDN)
    g = -jnp.exp(gdn_a_log.astype(f32)) * jax.nn.softplus(ga.astype(f32) + gdn_dt_bias.astype(f32))
    beta = jax.nn.sigmoid(gb.astype(f32))
    o_g, gdn_s = gated_delta_rule(q_g, k_g, v_g, g, beta, gdn_s0.astype(f32), chunk)
    o_gdn = rmsnorm(o_g, gdn_norm_w).reshape(B, S, BRANCH_W).astype(x.dtype) * jax.nn.silu(gz)

    br = jnp.einsum('bsnc,ncd->bsnd', jnp.stack([o_ret, o_fox, o_gdn], axis=2), w_branch)
    mg = jax.nn.sigmoid(mg.reshape(B, S, N_BRANCH, D_MODEL).astype(f32)).astype(x.dtype)
    out = jnp.sum(br * mg, axis=2) @ w_out
    x = x + gate * out
    new_state = (k_f, v_f, logf.astype(x.dtype), ret_s.astype(x.dtype),
                 gdn_s.astype(x.dtype), conv_new)
    return x, new_state

def setup_inputs(seed: int = 0) -> dict:
    key = jax.random.key(seed)
    ks = jax.random.split(key, 24)
    f32 = jnp.float32

    def nrm(k, shape, s):
        return jax.random.normal(k, shape, f32) * s

    dt = jnp.exp(jax.random.uniform(ks[15], (DEPTH, H_GDN), f32, np.log(1e-3), np.log(1e-1)))
    return {
        'x_prompt': nrm(ks[0], (BATCH, SEQ, D_MODEL), 1.0),
        'x_sample': nrm(ks[1], (DEC_BATCH, DEC_SEQ, D_MODEL), 1.0),
        'c_prompt': nrm(ks[2], (BATCH, D_MODEL), 1.0),
        'c_sample': nrm(ks[3], (DEC_BATCH, D_MODEL), 1.0),
        'cache_fox_k': nrm(ks[4], (DEPTH, DEC_BATCH, H_FOX, PAST_LEN, HD_FOX), 1.0),
        'cache_fox_v': nrm(ks[5], (DEPTH, DEC_BATCH, H_FOX, PAST_LEN, HD_FOX), 1.0),
        'cache_fox_logf': jax.nn.log_sigmoid(3.0 + nrm(ks[6], (DEPTH, DEC_BATCH, H_FOX, PAST_LEN), 1.0)),
        'state_ret': nrm(ks[7], (DEPTH, DEC_BATCH, H_RET, DK_RET, DV_RET), 1.0),
        'state_gdn': nrm(ks[8], (DEPTH, DEC_BATCH, H_GDN, DK_GDN, DV_GDN), 0.1),
        'state_gdn_conv': nrm(ks[9], (DEPTH, DEC_BATCH, CONV_W - 1, CONV_CH), 1.0),
        'norm_w': 1.0 + nrm(ks[10], (DEPTH, D_MODEL), 0.1),
        'ada_w': nrm(ks[11], (DEPTH, D_MODEL, 3 * D_MODEL), 0.5 * D_MODEL ** -0.5),
        'ada_b': nrm(ks[12], (DEPTH, 3 * D_MODEL), 0.02),
        'w_in': nrm(ks[13], (DEPTH, D_MODEL, IN_W), D_MODEL ** -0.5),
        'fox_f_bias': jax.random.uniform(ks[14], (DEPTH, H_FOX), f32, 1.0, 5.0),
        'gdn_a_log': jnp.log(jax.random.uniform(ks[16], (DEPTH, H_GDN), f32, 1.0, 16.0)),
        'gdn_dt_bias': dt + jnp.log(-jnp.expm1(-dt)),
        'gdn_conv_w': nrm(ks[17], (DEPTH, CONV_W, CONV_CH), CONV_W ** -0.5),
        'ret_norm_w': 1.0 + nrm(ks[18], (DEPTH, BRANCH_W), 0.1),
        'gdn_norm_w': 1.0 + nrm(ks[19], (DEPTH, DV_GDN), 0.1),
        'w_branch': nrm(ks[20], (DEPTH, N_BRANCH, BRANCH_W, D_MODEL), BRANCH_W ** -0.5),
        'w_out': nrm(ks[21], (DEPTH, D_MODEL, D_MODEL), D_MODEL ** -0.5),
        'final_norm_w': 1.0 + nrm(ks[22], (D_MODEL,), 0.1),
    }

def reference(x_prompt, x_sample, c_prompt, c_sample, cache_fox_k, cache_fox_v, cache_fox_logf,
              state_ret, state_gdn, state_gdn_conv, norm_w, ada_w, ada_b, w_in, fox_f_bias,
              gdn_a_log, gdn_dt_bias, gdn_conv_w, ret_norm_w, gdn_norm_w, w_branch, w_out,
              final_norm_w):
    past = cache_fox_k.shape[3]
    pos_p = jnp.arange(x_prompt.shape[1])
    pos_s = past + jnp.arange(x_sample.shape[1])
    xp, xs = x_prompt, x_sample
    p_states, s_states = [], []
    for l in range(DEPTH):
        wl = (norm_w[l], ada_w[l], ada_b[l], w_in[l], fox_f_bias[l], gdn_a_log[l], gdn_dt_bias[l],
              gdn_conv_w[l], ret_norm_w[l], gdn_norm_w[l], w_branch[l], w_out[l])
        xp, st_p = trunk_layer(xp, c_prompt, pos_p, None, *wl)
        p_states.append(st_p)
        hist = (cache_fox_k[l], cache_fox_v[l], cache_fox_logf[l], state_ret[l], state_gdn[l],
                state_gdn_conv[l])
        xs, st_s = trunk_layer(xs, c_sample, pos_s, hist, *wl)
        s_states.append(st_s)
    y_prompt = rmsnorm(xp, final_norm_w)
    y_sample = rmsnorm(xs, final_norm_w)

    def stacked(states, i):
        return jnp.stack([st[i] for st in states])

    return (y_prompt, y_sample,
            stacked(p_states, 0), stacked(p_states, 1), stacked(p_states, 2),
            stacked(p_states, 3), stacked(p_states, 4), stacked(p_states, 5),
            stacked(s_states, 0), stacked(s_states, 1), stacked(s_states, 2),
            stacked(s_states, 3), stacked(s_states, 4), stacked(s_states, 5))


_drawn_inputs = setup_inputs


def setup_inputs(seed=0):
    import zlib

    import numpy as np

    out = dict(_drawn_inputs(seed))
    spreads = {}
    factors = {'cache_fox_k': 5.094,
     'cache_fox_v': 3.835,
     'cache_fox_logf': 8.0,
     'ret_norm_w': 3.648,
     'gdn_norm_w': 3.593}
    for name, (base, spread) in spreads.items():
        noise = np.random.default_rng([zlib.crc32(name.encode()), seed]).standard_normal(out[name].shape)
        drawn = base * np.exp(spread * noise) if base else spread * noise
        out[name] = jnp.asarray(drawn.astype(out[name].dtype))
    for name, factor in factors.items():
        out[name] = (out[name] * factor).astype(out[name].dtype)
    return out
```

```python
from contextlib import ExitStack

import numpy as np
import concourse.bass as bass
from concourse import mybir

F32 = mybir.dt.float32
ALU = mybir.AluOpType
ACT = mybir.ActivationFunctionType
AXX = mybir.AxisListType.X

P = 128
D = 1024
DEPTH = 2
SEQ = 1024
DEC = 64
PAST = 512
TOK = SEQ + DEC
NTILE = SEQ // P + 1
PADTOK = NTILE * P
SEGS = [(0, 512), (512, 512), (SEQ, DEC)]
KC = D // P
EPS = 1e-6
N_BLOCKS = 76
FKEYS = SEQ + PAST + DEC
SCAN_OFF = SEQ + PAST
UW = 3 + SEQ + 3 + DEC
LEVELS = [2, 4, 8, 16, 32, 64]
GAMMA = [1.0 - 2.0 ** (-5.0 - h) for h in range(4)]


def shape_constants():
    i = np.arange(P)
    ident = np.eye(P)
    incl = (i[:, None] <= i[None, :]).astype(float)
    strict = (i[:, None] < i[None, :]).astype(float)
    lev = []
    for s in [1] + LEVELS:
        same = (i[:, None] // (2 * s)) == (i[None, :] // (2 * s))
        lev.append((same & ((i[:, None] // s) % 2 == 0) & ((i[None, :] // s) % 2 == 1)).astype(float))
    causal = np.where(i[None, :] > i[:, None], 1e30, 0.0)
    swap = np.zeros((P, P))
    for r in range(P):
        swap[(r // 64) * 64 + (r + 32) % 64, r] = 1.0
    masks = np.stack([ident, np.ones((P, P)), incl, strict, causal, swap] + lev, axis=1)
    half = 32
    inv = np.float32(10000.0) ** (-np.arange(half, dtype=np.float32) / np.float32(half))
    pos = np.concatenate([np.arange(SEQ), PAST + np.arange(DEC)]).astype(np.float32)
    ang = (inv.astype(np.float32)[:, None] * pos[None, :]).astype(np.float32)
    cos = np.cos(ang.astype(np.float64))
    sin = np.sin(ang.astype(np.float64))
    rot = np.stack([np.tile(cos, (4, 1)), np.concatenate([-sin, sin, -sin, sin])], axis=1)
    ret = []
    for g in range(2):
        gam = GAMMA[2 * g:2 * g + 2]
        dist = np.abs(i[:, None] - i[None, :])
        seen = (i[:, None] // 64) <= (i[None, :] // 64)
        dt = np.concatenate([np.where(seen, x ** dist, 0.0) for x in gam], axis=1)
        per = np.repeat(gam, 64)
        dq = per[:, None] ** (i[None, :] + 1)
        kd = per[None, :] ** (P - 1 - i)[:, None]
        kds = per[None, :] ** np.maximum(DEC - 1 - i, 0)[:, None]
        dc = np.stack([per ** P, per ** DEC], axis=1)
        ret.append(np.concatenate([dt, dq, kd, kds, dc], axis=1))
    f = np.float32
    return masks.astype(f), rot.astype(f), np.stack(ret).astype(f)


RETC = 2 * P + P + 2 * P + 2


def build(nc, A, O):
    with ExitStack() as ctx:
        def sb(name, shape):
            return ctx.enter_context(nc.sbuf_tensor("sb_" + name, shape, F32))

        sems = []

        def sem(name):
            s = ctx.enter_context(nc.semaphore(name))
            sems.append(s)
            return s

        xT = sb("xT", [P, KC, TOK])
        hT = sb("hT", [P, KC, TOK])
        oT = sb("oT", [P, 12, TOK])
        wt = sb("wt", [P, 6, KC, P])
        masks = sb("masks", [P, 13, P])
        cT = sb("cT", [P, KC, 2])
        consts = sb("consts", [P, 4])
        nwT = sb("nwT", [P, 4, KC])
        modT = sb("modT", [P, 24, 2])
        work = sb("work", [P, 14600])
        ident, ones, incl, strict = (masks[:, m, :] for m in range(4))
        causal, swap = masks[:, 4, :], masks[:, 5, :]
        eps_c, l2_c, one_c = consts[:, 0:1], consts[:, 1:2], consts[:, 2:3]
        ps = ctx.enter_context(nc.psum_tensor("ps", [P, 8, 512], F32))
        dfk = nc.dram_tensor("scratch_fcum", (8, FKEYS), F32, kind="Internal").ap()
        dg = nc.dram_tensor("scratch_g", (4, PADTOK), F32, kind="Internal").ap()
        db = nc.dram_tensor("scratch_beta", (4, PADTOK), F32, kind="Internal").ap()

        weights_loaded = sem("weights_loaded")
        params_loaded = sem("params_loaded")
        hist_loaded = sem("hist_loaded")
        bank_ready = sem("bank_ready")
        act_took = sem("act_took")
        dve_took = sem("dve_took")
        stored = sem("stored")
        act_step = sem("act_step")
        dve_step = sem("dve_step")
        squares = sem("squares")
        roots = sem("roots")
        raw_ready = sem("raw_ready")
        conv_done = sem("conv_done")
        silu_done = sem("silu_done")
        normed = sem("normed")
        decays = sem("decays")
        exps = sem("exps")
        tiles_made = sem("tiles_made")
        level_mask = sem("level_mask")
        level_x = sem("level_x")
        state_ready = sem("state_ready")
        chain_pe = sem("chain_pe")
        rhs_ready = sem("rhs_ready")
        upd_ready = sem("upd_ready")
        out_pe = sem("out_pe")
        out_took = sem("out_took")
        out_done = sem("out_done")
        scores_pe = sem("scores_pe")
        logits = sem("logits")
        probs = sem("probs")
        squares_used = sem("squares_used")
        cleared = sem("cleared")
        slot_used = sem("slot_used")
        slot_loaded = [sem(f"slot_loaded_{i}") for i in range(6)]
        branch_loaded = [sem(f"branch_loaded_{i}") for i in range(4)]
        nums = [s.num for s in sems]
        clear = range(min(nums), max(nums) + 1)
        assert len(clear) == len(sems)

        def barrier():
            nc.multi_engine_barrier(list(nc.engines), sems_to_clear=clear)

        def ln_chain(eng, ins, count, s):
            count[0] += 1
            ins.then_inc(s, 1)
            eng.wait_ge(s, count[0])

        class Ring:
            def __init__(self, owners, first, banks):
                self.owners, self.first, self.banks = owners, first, banks

            def bank(self, n):
                return self.first + n % self.banks

            def acquire(self, pe, n):
                m = n - self.banks
                if m >= 0 and not isinstance(self.owners[m], str):
                    pe.wait_ge(*self.owners[m])
                elif m >= 0:
                    who = self.owners[m]
                    pe.wait_ge(act_took if who == "act" else dve_took,
                               sum(o == who for o in self.owners[:m + 1]))

        def project(pe, ring, n, slot):
            for s, (a, w) in enumerate(SEGS):
                ring.acquire(pe, n + s)
                for k in range(KC):
                    mm = pe.matmul(ps[:, ring.bank(n + s), 0:w], wt[:, slot, k, :], hT[:, k, a:a + w],
                                   start=(k == 0), stop=(k == KC - 1))
                mm.then_inc(bank_ready, 1)

        def sum_features(pe, ring, n, sq):
            for s, (a, w) in enumerate(SEGS):
                ring.acquire(pe, n + s)
                pe.matmul(ps[:, ring.bank(n + s), 0:w], ones, sq[:, a:a + w],
                          start=True, stop=True).then_inc(bank_ready, 1)

        def reload_weights(sp, base, after, count):
            for i in range(count):
                if after[i]:
                    sp.wait_ge(bank_ready, after[i])
                sp.dma_start(wt[:, i, :, :], A["wblk"][bass.ds(base + i, 1)]
                             .rearrange("a p k c -> (a p) k c")).then_inc(weights_loaded, 16)

        def row(name, idx):
            ap = A[name] if name in A else O[name]
            dims = " ".join("bcdef"[:len(ap.shape) - 2])
            return ap[bass.ds(idx, 1)].rearrange(f"a p {dims} -> (a p) {dims}" if dims else "a p -> (a p)")

        with nc.Block() as block:
            @block.sync
            def _(sp):
                sp.dma_start(masks[:, :, :], A["masks"]).then_inc(params_loaded, 16)
                sp.dma_start(cT[:, :, :], A["cT"]).then_inc(params_loaded, 16)
                sp.dma_start(xT[:, :, :], A["xT"]).then_inc(params_loaded, 16)
                sp.wait_ge(params_loaded, 48)

            @block.scalar
            def _(act):
                act.wait_ge(params_loaded, 48)
                act.activation(cT[:, :, :], cT[:, :, :], ACT.Silu)

            @block.vector
            def _(dve):
                dve.memset(eps_c, EPS)
                dve.memset(l2_c, EPS * P)
                dve.memset(one_c, 1.0)
        barrier()

        def norm_block(final, L):
            sq = work[:, 0:2 * TOK].rearrange("p (b t) -> p b t", b=2)
            rstd = work[:, 2176:2176 + TOK]
            NADA = 3
            ada = work[:, 3264:3264 + NADA * 1024].rearrange("p (b k c) -> p b k c", b=NADA, k=KC)
            wsm = work[:, 6336:7104].rearrange("p (k c) -> p k c", k=KC)
            gz = work[0:96, 7104:7104 + PADTOK]
            ga = work[0:96, 8256:8256 + PADTOK]
            gl = work[0:96, 9408:9408 + PADTOK]
            lfx = work[0:8, 10560:10560 + FKEYS]
            fre = work[0:8, 12160:12160 + FKEYS]
            gre = work[0:96, 3264:3264 + PADTOK]
            colsA = work[:, 13760:13760 + 24 + 4 + 16]
            adab, gcols, scw = colsA[:, 0:24], colsA[0:96, 24:28], colsA[:, 28:44].rearrange("p (k c) -> p k c", k=KC)
            ring = Ring(["act"] * 3, 0, 8)
            with nc.Block() as block:
                @block.sync
                def _(sp):
                    if final:
                        sp.dma_start(nwT[:, 0, :], A["fnwT"]).then_inc(params_loaded, 16)
                        for k in range(KC):
                            sp.wait_ge(out_done, k + 1)
                            sp.dma_start(O["yT"][k], hT[:, k, :]).then_inc(stored, 16)
                        sp.wait_ge(stored, 16 * KC)
                        return
                    sp.dma_start(nwT[:, 0, :], row("nwT", L)).then_inc(params_loaded, 16)
                    sp.dma_start(adab, row("adabT", L)).then_inc(params_loaded, 16)
                    sp.dma_start(gcols, row("gcols", L)).then_inc(params_loaded, 16)
                    sp.dma_start(wsm, row("wsm", L)).then_inc(params_loaded, 16)
                    sp.dma_start(lfx[:, SEQ:SEQ + PAST], row("lfc", L)).then_inc(params_loaded, 16)
                    for n in range(24):
                        if n >= NADA:
                            sp.wait_ge(slot_used, n - NADA + 1)
                        sp.dma_start(ada[:, n % NADA], row("adaw", L * 24 + n))\
                            .then_inc(slot_loaded[n % NADA], 16)
                    reload_weights(sp, L * N_BLOCKS, [0] * 6, 6)
                    sp.wait_ge(decays, 1)
                    sp.dma_start(row("p_logf", L), lfx[:, 0:SEQ]).then_inc(stored, 16)
                    sp.dma_start(row("s_logf", L), lfx[:, SCAN_OFF:FKEYS]).then_inc(stored, 16)
                    sp.wait_ge(decays, 2)
                    sp.dma_start(dfk, fre).then_inc(stored, 16)
                    sp.wait_ge(decays, 3)
                    sp.dma_start(dg, ga[32:36, :]).then_inc(stored, 16)
                    sp.wait_ge(exps, 1)
                    sp.dma_start(db, gz[64:68, :]).then_inc(stored, 16)
                    sp.wait_ge(stored, 80)
                    sp.wait_ge(weights_loaded, 96)

                @block.tensor
                def _(pe):
                    for k in range(KC):
                        pe.wait_ge(squares, k + 1)
                        for s, (a, w) in enumerate(SEGS):
                            mm = pe.matmul(ps[:, s, 0:w], ones, sq[:, k % 2, a:a + w],
                                           start=(k == 0), stop=(k == KC - 1))
                        mm.then_inc(squares_used, 1)
                    if final:
                        return
                    for n in range(24):
                        pe.wait_ge(slot_loaded[n % NADA], 16 * (n // NADA + 1))
                        for k in range(KC):
                            mm = pe.matmul(ps[:, 3, 2 * n:2 * n + 2], ada[:, n % NADA, k, :], cT[:, k, :],
                                           start=(k == 0), stop=(k == KC - 1))
                        mm.then_inc(slot_used, 1)
                    pe.wait_ge(params_loaded, 80)
                    pe.wait_ge(out_done, KC)
                    for s, (a, w) in enumerate(SEGS):
                        for k in range(KC):
                            mm = pe.matmul(ps[0:96, 4 + s, 0:w], wsm[:, k, :], hT[:, k, a:a + w],
                                           start=(k == 0), stop=(k == KC - 1))
                        mm.then_inc(out_pe, 1)

                @block.scalar
                def _(act):
                    for k in range(KC):
                        if k >= 2:
                            act.wait_ge(squares_used, k - 1)
                        act.activation(sq[:, k % 2, :], xT[:, k, :], ACT.Square).then_inc(squares, 1)
                    act.wait_ge(squares_used, KC)
                    for s, (a, w) in enumerate(SEGS):
                        act.activation(rstd[:, a:a + w], ps[:, s, 0:w], ACT.Sqrt, bias=eps_c,
                                       scale=1.0 / D).then_inc(roots, 1)
                    if final:
                        return
                    for k in range(KC):
                        act.wait_ge(normed, k + 1)
                        for c, (a, w) in enumerate(((0, SEQ), (SEQ, DEC))):
                            ins = act.activation(hT[:, k, a:a + w], hT[:, k, a:a + w], ACT.Identity,
                                                 bias=modT[:, k, c:c + 1])
                        ins.then_inc(out_done, 1)
                    act.wait_ge(params_loaded, 80)
                    act.activation(gcols[:, 2:3], gcols[:, 1:2], ACT.Exp).then_inc(act_step, 1)
                    act.wait_ge(raw_ready, 4)
                    act.activation(gl, ga, ACT.Exp, scale=-1.0).then_inc(act_step, 1)
                    act.wait_ge(act_step, 2)
                    act.activation(gl, gl, ACT.Ln, bias=one_c[0:96]).then_inc(act_took, 1)
                    act.wait_ge(conv_done, 1)
                    act.activation(gz[64:68, 0:TOK], gl[64:68, 0:TOK], ACT.Exp).then_inc(exps, 1)

                @block.vector
                def _(dve):
                    st = [0]

                    def link(ins):
                        ln_chain(dve, ins, st, dve_step)
                    if not final:
                        link(dve.memset(gz, 0.0))
                        link(dve.memset(ga, 0.0))
                        dve.wait_ge(params_loaded, 80)
                        dve.wait_ge(slot_used, 24)
                        link(dve.tensor_tensor(modT[:, :, :], ps[:, 3, 0:48].rearrange("p (n c) -> p n c", c=2),
                                               adab.unsqueeze(2).to_broadcast([P, 24, 2]), ALU.add))
                        link(dve.tensor_scalar(scw, modT[:, 8:16, :], 1.0, None, ALU.add))
                        link(dve.tensor_tensor(scw, scw, nwT[:, 0, :].unsqueeze(2).to_broadcast([P, KC, 2]),
                                               ALU.mult))
                    else:
                        dve.wait_ge(params_loaded, 16)
                    dve.wait_ge(roots, 3)
                    link(dve.reciprocal(rstd, rstd))
                    for k in range(KC):
                        for c, (a, w) in enumerate(((0, SEQ), (SEQ, DEC))):
                            col = nwT[:, 0, k:k + 1] if final else scw[:, k, c:c + 1]
                            ins = dve.scalar_tensor_tensor(hT[:, k, a:a + w], xT[:, k, a:a + w], col,
                                                           rstd[:, a:a + w], ALU.mult, ALU.mult)
                        ins.then_inc(out_done if final else normed, 1)
                    if final:
                        return
                    for s, (a, w) in enumerate(SEGS):
                        dve.wait_ge(out_pe, s + 1)
                        dve.tensor_scalar(gz[:, a:a + w], ps[0:96, 4 + s, 0:w], gcols[:, 0:1], None,
                                          ALU.add).then_inc(raw_ready, 1)
                    dve.wait_ge(raw_ready, 3)
                    dve.scalar_tensor_tensor(ga, gz, -1.0, gz, ALU.mult, ALU.max).then_inc(raw_ready, 1)
                    dve.wait_ge(act_took, 1)
                    link(dve.scalar_tensor_tensor(ga, gz, 0.0, gl, ALU.max, ALU.add))
                    dve.wait_ge(act_step, 2)
                    link(dve.tensor_scalar(ga, ga, gcols[:, 2:3], -1.0, ALU.mult, ALU.mult))
                    dve.scalar_tensor_tensor(gl, gz, 0.0, gl, ALU.min, ALU.subtract).then_inc(conv_done, 1)
                    dve.wait_ge(conv_done, 1)
                    dve.tensor_copy(lfx[:, 0:SEQ], gl[0:8, 0:SEQ])
                    link(dve.tensor_copy(lfx[:, SCAN_OFF:FKEYS], gl[0:8, SEQ:TOK]))
                    link(dve.memset(fre, 1.0))
                    link(dve.memset(fre[:, SEQ:SEQ + 1], 0.0))
                    dve.memset(gre, 1.0).then_inc(decays, 1)
                    dve.wait_ge(decays, 1)
                    link(dve.memset(gre.rearrange("p (t c) -> p t c", c=P)[:, :, 0:1], 0.0))
                    dve.tensor_tensor_scan(fre, fre, lfx, 0.0, ALU.mult, ALU.add).then_inc(decays, 1)
                    dve.memset(ga[:, TOK:PADTOK], 0.0).then_inc(cleared, 1)
                    dve.wait_ge(cleared, 1)
                    dve.tensor_tensor_scan(ga[32:36, :], gre[32:36, :], ga[32:36, :], 0.0, ALU.mult,
                                           ALU.add).then_inc(decays, 1)
            barrier()

        def head_norm_gate(eng_name, ring, n, eng, raw, sq, r, w_col=None, out_ap=None, link=None, need=None):
            if eng_name == "act":
                eng.activation(sq, raw, ACT.Square).then_inc(squares, 1)
                for s, (a, w) in enumerate(SEGS):
                    eng.wait_ge(bank_ready, n + s + 1)
                    eng.activation(r[:, a:a + w], ps[:, ring.bank(n + s), 0:w], ACT.Sqrt, bias=eps_c,
                                   scale=1.0 / P).then_inc(act_took, 1)
            else:
                eng.wait_ge(act_took, need)
                link(eng.reciprocal(r, r))
                link(eng.scalar_tensor_tensor(raw, raw, w_col, r, ALU.mult, ALU.mult))
                eng.tensor_tensor(out_ap, out_ap, raw, ALU.mult).then_inc(out_done, 1)

        def slab(i):
            return work[:, i * PADTOK:(i + 1) * PADTOK]

        def tiles(ap):
            return ap.rearrange("p (t c) -> p t c", c=P)

        G3 = [(0, 4), (4, 4), (8, 1)]
        Q4 = lambda ap: ap.rearrange("p (t c) -> p t c", c=P)

        def retention_group(L, g):
            q, k_, V = slab(0), slab(1), work[:, 2 * PADTOK:4 * PADTOK].rearrange("p (t c) -> p t c", c=2 * P)
            cos, sin, tmp, Kd = slab(4)[:, 0:TOK], slab(5)[:, 0:TOK], slab(6), slab(7)
            AT = [slab(8), slab(9)]
            raw, sq, r = [slab(4), slab(5)], slab(6), slab(7)
            base = 10 * PADTOK
            S = work[:, base:base + 11 * P].rearrange("p (t c) -> p t c", c=P)
            rc = work[:, base + 11 * P:base + 11 * P + RETC]
            DT = [rc[:, 0:P], rc[:, P:2 * P]]
            dq, kd = rc[:, 2 * P:3 * P], rc[:, 3 * P:5 * P]
            dc = rc[:, 5 * P:5 * P + 2]
            nw = work[:, base + 11 * P + RETC:base + 11 * P + RETC + 2]
            gi = L * 2 + g
            VN = [(0, 2), (2, 2), (4, 2), (6, 2), (8, 1)]
            owners = (["act"] * 11 + ["dve"] * 6 + ["act"] * 6 + ["dve"] * 9
                      + [(state_ready, 4), (state_ready, 8), (state_ready, 9)] + ["act"] * 6 + ["act"] * 6)
            ring = Ring(owners, 0, 8)
            with nc.Block() as block:
                @block.sync
                def _(sp):
                    sp.dma_start(work[:, 4 * PADTOK:4 * PADTOK + TOK], A["rot"][:, 0, :]).then_inc(params_loaded, 16)
                    sp.dma_start(work[:, 5 * PADTOK:5 * PADTOK + TOK], A["rot"][:, 1, :]).then_inc(params_loaded, 16)
                    sp.dma_start(rc, row("retc", g)).then_inc(params_loaded, 16)
                    sp.dma_start(nw, row("rnwT", gi)).then_inc(params_loaded, 16)
                    sp.dma_start(S[:, 9, :], row("sret", gi)).then_inc(params_loaded, 16)
                    reload_weights(sp, L * N_BLOCKS + g * 6 + 6, [3, 6, 11, 11, 20, 23], 6)
                    sp.wait_ge(state_ready, 9)
                    sp.dma_start(row("p_ret", gi), S[:, 8, :]).then_inc(stored, 16)
                    sp.dma_start(row("s_ret", gi), S[:, 10, :]).then_inc(stored, 16)
                    sp.wait_ge(stored, 32)
                    sp.wait_ge(weights_loaded, 96)

                @block.tensor
                def _(pe):
                    project(pe, ring, 0, 0)
                    project(pe, ring, 3, 1)
                    for n, (t, c) in enumerate(VN):
                        ring.acquire(pe, 6 + n)
                        for j in range(c):
                            rows = P if t + j < 8 else DEC
                            for k in range(KC):
                                mm = pe.matmul(ps[0:rows, ring.bank(6 + n), 256 * j:256 * j + 256],
                                               hT[:, k, (t + j) * P:(t + j) * P + rows],
                                               wt[:, 2:4, k, :], start=(k == 0), stop=(k == KC - 1))
                        mm.then_inc(bank_ready, 1)
                    for x, src in enumerate((q, k_)):
                        pe.wait_ge(act_took, 3 * (x + 1))
                        for s, (a, w) in enumerate(SEGS):
                            ring.acquire(pe, 11 + 3 * x + s)
                            pe.matmul(ps[:, ring.bank(11 + 3 * x + s), 0:w], swap, src[:, a:a + w],
                                      start=True, stop=True).then_inc(bank_ready, 1)
                    project(pe, ring, 17, 4)
                    project(pe, ring, 20, 5)
                    pe.wait_ge(normed, 2)
                    for n, (t, c) in enumerate(G3):
                        ring.acquire(pe, 23 + n)
                        for j in range(c):
                            mm = pe.transpose(ps[:, ring.bank(23 + n), P * j:P * j + P],
                                              Q4(k_)[:, t + j, :], ident)
                        mm.then_inc(bank_ready, 1)
                    for h in range(2):
                        for n, (t, c) in enumerate(G3):
                            e = 26 + 3 * h + n
                            ring.acquire(pe, e)
                            for j in range(c):
                                mm = pe.matmul(ps[:, ring.bank(e), P * j:P * j + P],
                                               Q4(k_)[64 * h:64 * h + 64, t + j, :],
                                               Q4(q)[64 * h:64 * h + 64, t + j, :], start=True, stop=True)
                            mm.then_inc(bank_ready, 1)
                    pe.wait_ge(dve_took, 9)
                    pe.wait_ge(act_took, 11)
                    pe.wait_ge(cleared, 2)
                    for n, (t, c) in enumerate(G3):
                        ring.acquire(pe, 32 + n)
                        for j in range(c):
                            for h in range(2):
                                mm = pe.matmul(ps[64 * h:64 * h + 64, ring.bank(32 + n), P * j:P * j + P],
                                               Q4(Kd)[:, t + j, 64 * h:64 * h + 64],
                                               V[:, t + j, P * h:P * h + P], start=True, stop=True)
                        mm.then_inc(bank_ready, 1)
                    for h in range(2):
                        pe.wait_ge(dve_took, 9 + 3 * (h + 1))
                        pe.wait_ge(conv_done, 1)
                        for n, (t, c) in enumerate(G3):
                            e = 35 + 3 * h + n
                            ring.acquire(pe, e)
                            pe.wait_ge(state_ready, min(t + c - 1, 9) if t < 8 else 8)
                            for j in range(c):
                                tt = t + j
                                out = ps[:, ring.bank(e), P * j:P * j + P]
                                mm = pe.matmul(out, V[:, tt, P * h:P * h + P], Q4(AT[h])[:, tt, :],
                                               start=True, stop=(tt == 0))
                                if tt:
                                    mm = pe.matmul(out, S[64 * h:64 * h + 64, 9 if tt == 8 else tt, :],
                                                   Q4(q)[64 * h:64 * h + 64, tt, :], start=False, stop=True)
                            mm.then_inc(bank_ready, 1)
                    for h in range(2):
                        pe.wait_ge(squares, h + 1)
                        sum_features(pe, ring, 41 + 3 * h, sq)

                @block.scalar
                def _(act):
                    for s, (a, w) in enumerate(SEGS):
                        act.wait_ge(bank_ready, s + 1)
                        act.activation(q[:, a:a + w], ps[:, ring.bank(s), 0:w], ACT.Copy)\
                            .then_inc(act_took, 1)
                    for s, (a, w) in enumerate(SEGS):
                        act.wait_ge(bank_ready, s + 4)
                        act.activation(k_[:, a:a + w], ps[:, ring.bank(3 + s), 0:w], ACT.Copy, scale=0.125)\
                            .then_inc(act_took, 1)
                    act.wait_ge(cleared, 2)
                    for n, (t, c) in enumerate(VN):
                        act.wait_ge(bank_ready, 7 + n)
                        rows = P if t < 8 else DEC
                        act.activation(V[0:rows, t:t + c, :],
                                       ps[0:rows, ring.bank(6 + n), 0:256 * c].rearrange("p (t c) -> p t c", t=c),
                                       ACT.Copy).then_inc(act_took, 1)
                    for x in range(2):
                        for s, (a, w) in enumerate(SEGS):
                            n = 17 + 3 * x + s
                            act.wait_ge(bank_ready, n + 1)
                            act.activation(oT[:, bass.ds(2 * g + x, 1), a:a + w].rearrange("p a t -> p (a t)"),
                                           ps[:, ring.bank(n), 0:w], ACT.Silu).then_inc(act_took, 1)
                    act.wait_ge(normed, 2)
                    for h in range(2):
                        for n, (t, c) in enumerate(G3):
                            e = 35 + 3 * h + n
                            act.wait_ge(bank_ready, e + 1)
                            act.activation(Q4(raw[h])[:, t:t + c, :],
                                           Q4(ps[:, ring.bank(e), 0:P * c]), ACT.Copy)\
                                .then_inc(act_took, 1)
                    for h in range(2):
                        act.wait_ge(act_took, 20 + 3 * h)
                        if h:
                            act.wait_ge(bank_ready, 44)
                            act.wait_ge(out_done, 1)
                        head_norm_gate("act", ring, 41 + 3 * h, act, raw[h], sq, r)

                @block.vector
                def _(dve):
                    st = [0]

                    def link(ins):
                        ln_chain(dve, ins, st, dve_step)
                    dve.memset(V[64:128, 8, :], 0.0).then_inc(cleared, 1)
                    link(dve.memset(q[:, TOK:PADTOK], 0.0))
                    dve.memset(k_[:, TOK:PADTOK], 0.0).then_inc(cleared, 1)
                    dve.wait_ge(cleared, 2)
                    dve.wait_ge(params_loaded, 80)
                    for x, dst in enumerate((q, k_)):
                        for s, (a, w) in enumerate(SEGS):
                            dve.wait_ge(bank_ready, 12 + 3 * x + s)
                            dve.tensor_tensor(tmp[:, a:a + w], ps[:, ring.bank(11 + 3 * x + s), 0:w],
                                              sin[:, a:a + w], ALU.mult).then_inc(dve_took, 1)
                        link(dve.tensor_tensor(dst[:, 0:TOK], dst[:, 0:TOK], cos, ALU.mult))
                        dve.wait_ge(dve_took, 3 * (x + 1))
                        dve.tensor_tensor(dst[:, 0:TOK], dst[:, 0:TOK], tmp[:, 0:TOK], ALU.add)\
                            .then_inc(normed, 1)
                        dve.wait_ge(normed, x + 1)
                    for n, (t, c) in enumerate(G3):
                        dve.wait_ge(bank_ready, 24 + n)
                        col = kd[:, 0:P] if t < 8 else kd[:, P:2 * P]
                        dve.tensor_tensor(Q4(Kd)[:, t:t + c, :], Q4(ps[:, ring.bank(23 + n), 0:P * c]),
                                          col.unsqueeze(1).to_broadcast([P, c, P]), ALU.mult)\
                            .then_inc(dve_took, 1)
                    for h in range(2):
                        for n, (t, c) in enumerate(G3):
                            e = 26 + 3 * h + n
                            dve.wait_ge(bank_ready, e + 1)
                            dve.tensor_tensor(Q4(AT[h])[:, t:t + c, :], Q4(ps[:, ring.bank(e), 0:P * c]),
                                              DT[h].unsqueeze(1).to_broadcast([P, c, P]), ALU.mult)\
                                .then_inc(dve_took, 1)
                    dve.tensor_tensor(Q4(q), Q4(q), dq.unsqueeze(1).to_broadcast([P, NTILE, P]), ALU.mult)\
                        .then_inc(conv_done, 1)
                    dve.wait_ge(params_loaded, 80)
                    for t in range(NTILE):
                        n = 32 + t // 4
                        dve.wait_ge(bank_ready, n + 1)
                        upd = ps[:, ring.bank(n), P * (t % 4):P * (t % 4) + P]
                        if t == 0:
                            ins = dve.tensor_copy(S[:, 1, :], upd)
                        elif t < 8:
                            ins = dve.scalar_tensor_tensor(S[:, t + 1, :], S[:, t, :], dc[:, 0:1], upd,
                                                           ALU.mult, ALU.add)
                        else:
                            ins = dve.scalar_tensor_tensor(S[:, 10, :], S[:, 9, :], dc[:, 1:2], upd,
                                                           ALU.mult, ALU.add)
                        ins.then_inc(state_ready, 1)
                        dve.wait_ge(state_ready, t + 1)
                    for h in range(2):
                        head_norm_gate("dve", ring, 41 + 3 * h, dve, raw[h][:, 0:TOK], sq, r[:, 0:TOK],
                                       nw[:, h:h + 1],
                                       oT[:, bass.ds(2 * g + h, 1), :].rearrange("p a t -> p (a t)"),
                                       link, 26 + 3 * h)
            barrier()

        def fox_group(L, g):
            qT = work[:, 0:TOK]
            at = TOK
            kT = work[:, at:at + FKEYS]
            at += FKEYS
            V = work[:, at:at + 13 * P].rearrange("p (t c) -> p t c", c=P)
            at += 13 * P
            fk = work[:, at:at + 2 * FKEYS].rearrange("p (h c) -> p h c", h=2)
            at += 2 * FKEYS
            fd = work[:, at:at + 2 * 9 * P].rearrange("p (h t c) -> p h t c", h=2, t=9)
            at += 18 * P
            lg = work[:, at:at + 2048].rearrange("p (b c) -> p b c", b=2)
            at += 2048
            PT = work[:, at:at + 2048].rearrange("p (b c) -> p b c", b=2)
            at += 2048
            otok = work[:, at:at + 2 * P].rearrange("p (b c) -> p b c", b=2)
            at += 2 * P
            mx = work[:, at:at + 18 * 5].rearrange("p (s c) -> p s c", c=5)
            gi = L * 4 + g
            VN = [(0, 4), (4, 4), (8, 1)]
            ring = Ring(["act"] * 12, 0, 8)
            with nc.Block() as block:
                @block.sync
                def _(sp):
                    sp.dma_start(fk.rearrange("p h c -> p (h c)"),
                                 dfk[bass.ds(2 * g, 2), :].rearrange("a c -> (a c)").partition_broadcast(P))\
                        .then_inc(params_loaded, 16)
                    sp.dma_start(kT[:, SEQ:SEQ + PAST], row("kcT", gi)).then_inc(params_loaded, 16)
                    sp.dma_start(V[:, 8:12, :], row("vc", gi)).then_inc(params_loaded, 16)
                    reload_weights(sp, L * N_BLOCKS + 12 + g * 4 + 4, [3, 6, 9, 12], 4)
                    sp.wait_ge(act_took, 12)
                    sp.dma_start(row("p_k", gi), kT[:, 0:SEQ]).then_inc(stored, 16)
                    sp.dma_start(row("s_k", gi), kT[:, SCAN_OFF:FKEYS]).then_inc(stored, 16)
                    sp.dma_start(row("p_v", gi), V[:, 0:8, :]).then_inc(stored, 16)
                    sp.dma_start(row("s_v", gi), V[0:DEC, 12, :]).then_inc(stored, 16)
                    sp.wait_ge(stored, 64)
                    sp.wait_ge(params_loaded, 48)
                    sp.wait_ge(weights_loaded, 64)

                @block.tensor
                def _(pe):
                    project(pe, ring, 0, 0)
                    project(pe, ring, 3, 1)
                    for n, (t, c) in enumerate(VN):
                        ring.acquire(pe, 6 + n)
                        for j in range(c):
                            rows = P if t + j < 8 else DEC
                            for k in range(KC):
                                mm = pe.matmul(ps[0:rows, ring.bank(6 + n), P * j:P * j + P],
                                               hT[:, k, (t + j) * P:(t + j) * P + rows],
                                               wt[:, 2, k, :], start=(k == 0), stop=(k == KC - 1))
                        mm.then_inc(bank_ready, 1)
                    project(pe, ring, 9, 3)

                @block.scalar
                def _(act):
                    for x, (dst, sc) in enumerate(((qT, 0.125), (kT, 1.0))):
                        for s, (a, w) in enumerate(SEGS):
                            n = 3 * x + s
                            b = SCAN_OFF if x == 1 and s == 2 else a
                            act.wait_ge(bank_ready, n + 1)
                            act.activation(dst[:, b:b + w], ps[:, ring.bank(n), 0:w], ACT.Copy, scale=sc)\
                                .then_inc(act_took, 1)
                    for n, (t, c) in enumerate(VN):
                        act.wait_ge(bank_ready, 7 + n)
                        rows, to = (P, t) if t < 8 else (DEC, 12)
                        act.activation(V[0:rows, to:to + c, :], Q4(ps[0:rows, ring.bank(6 + n), 0:P * c]),
                                       ACT.Copy).then_inc(act_took, 1)
                    for s, (a, w) in enumerate(SEGS):
                        act.wait_ge(bank_ready, 10 + s)
                        act.activation(oT[:, bass.ds(4 + g, 1), a:a + w].rearrange("p a t -> p (a t)"),
                                       ps[:, ring.bank(9 + s), 0:w], ACT.Silu).then_inc(act_took, 1)

                @block.vector
                def _(dve):
                    dve.wait_ge(params_loaded, 48)
                    for h in range(2):
                        dve.tensor_tensor(fd[:, h, 0:8, :], Q4(fk[:, h, 0:SEQ]),
                                          causal.unsqueeze(1).to_broadcast([P, 8, P]), ALU.add)
                        dve.tensor_tensor(fd[:, h, 8, 0:DEC], fk[:, h, SCAN_OFF:FKEYS], causal[:, 0:DEC],
                                          ALU.add)
            barrier()
            steps = [(t, h) for t in range(9) for h in range(2)]

            def blocks_of(t):
                if t < 8:
                    return [(P * b, P, b) for b in range(t + 1)]
                return [(SEQ + P * b, P, 8 + b) for b in range(4)] + [(SCAN_OFF, DEC, 12)]

            entry = {}
            order = 0
            for s, (t, h) in enumerate(steps):
                for c in range((len(blocks_of(t)) + 3) // 4):
                    entry[("p", s, c)] = order
                    order += 1
                if h == 0 and t:
                    entry[("o", t - 1)] = order
                    order += 1
            entry[("o", 8)] = order
            order += 1
            last_p = [max(v for e, v in entry.items() if e[0] == "p" and e[1] == s) for s in range(18)]
            with nc.Block() as block:
                @block.tensor
                def _(pe):
                    def qk(s):
                        t, h = steps[s]
                        rows = P if t < 8 else DEC
                        blk = blocks_of(t)
                        lo, n = blk[0][0], sum(b[1] for b in blk)
                        if s >= 2:
                            pe.wait_ge(logits, s - 1)
                        for a in range(0, n, 512):
                            w = min(512, n - a)
                            mm = pe.matmul(ps[0:rows, 2 * (s % 2) + a // 512, 0:w],
                                           qT[64 * h:64 * h + 64, P * t:P * t + rows],
                                           kT[64 * h:64 * h + 64, lo + a:lo + a + w], start=True, stop=True)
                        mm.then_inc(scores_pe, 1)

                    def get(n):
                        if n >= 2:
                            pe.wait_ge(dve_took, n - 1)
                        return 4 + n % 2

                    def turn_out(t):
                        rows = P if t < 8 else DEC
                        n = entry[("o", t)]
                        b = get(n)
                        pe.wait_ge(out_done, 2 * t + 2)
                        pe.transpose(ps[:, b, 0:rows], otok[0:rows, t % 2, :], ident[0:rows, 0:rows])\
                            .then_inc(bank_ready, 1)

                    qk(0)
                    for s, (t, h) in enumerate(steps):
                        if s + 1 < len(steps):
                            qk(s + 1)
                        rows = P if t < 8 else DEC
                        blk = blocks_of(t)
                        pe.wait_ge(probs, s + 1)
                        for c in range(0, len(blk), 4):
                            b = get(entry[("p", s, c // 4)])
                            for j, (col, w, _) in enumerate(blk[c:c + 4]):
                                mm = pe.transpose(ps[0:w, b, P * j:P * j + rows],
                                                  lg[0:rows, s % 2, (c + j) * P:(c + j) * P + w],
                                                  ident[0:rows, 0:rows])
                            mm.then_inc(bank_ready, 1)
                        if h == 0 and t:
                            turn_out(t - 1)
                        pe.wait_ge(dve_took, last_p[s] + 1)
                        if s >= 2:
                            pe.wait_ge(out_done, s - 1)
                        for c, (col, w, vt) in enumerate(blk):
                            mm = pe.matmul(ps[0:rows, 6 + s % 2, 0:64], PT[0:w, s % 2, P * c:P * c + rows],
                                           V[0:w, vt, 64 * h:64 * h + 64],
                                           start=(c == 0), stop=(c == len(blk) - 1))
                        mm.then_inc(out_pe, 1)
                    turn_out(8)

                @block.scalar
                def _(act):
                    for s, (t, h) in enumerate(steps):
                        rows = P if t < 8 else DEC
                        n = sum(b[1] for b in blocks_of(t))
                        act.wait_ge(exps, s + 1)
                        act.activation(lg[0:rows, s % 2, 0:n], lg[0:rows, s % 2, 0:n], ACT.Exp,
                                       bias=mx[0:rows, s, 2:3], accum_out=mx[0:rows, s, 3:4])\
                            .then_inc(probs, 1)

                @block.vector
                def _(dve):
                    st = [0]

                    def link(ins):
                        ln_chain(dve, ins, st, dve_step)

                    def maxima(s):
                        t, h = steps[s]
                        rows = P if t < 8 else DEC
                        blk = blocks_of(t)
                        lo, w = blk[0][0], blk[-1][1]
                        n = P * (len(blk) - 1)
                        dve.wait_ge(scores_pe, s + 1)
                        if s >= 2:
                            dve.wait_ge(bank_ready, last_p[s - 2] + 1)
                        src = ps[0:rows, 2 * (s % 2):2 * (s % 2) + 2, :].rearrange("p b c -> p (b c)")
                        if n:
                            dve.tensor_tensor_reduce(out=lg[0:rows, s % 2, 0:n], in0=src[:, 0:n],
                                                     in1=fk[0:rows, h, lo:lo + n], scale=1.0, scalar=-3e38,
                                                     op0=ALU.subtract, op1=ALU.max,
                                                     accum_out=mx[0:rows, s, 0:1])
                        dve.tensor_tensor_reduce(out=lg[0:rows, s % 2, n:n + w], in0=src[:, n:n + w],
                                                 in1=fd[0:rows, h, t, 0:w], scale=1.0, scalar=-3e38,
                                                 op0=ALU.subtract, op1=ALU.max,
                                                 accum_out=mx[0:rows, s, 1:2]).then_inc(logits, 1)
                        dve.wait_ge(logits, s + 1)
                        other = mx[0:rows, s, 0:1] if n else mx[0:rows, s, 1:2]
                        dve.tensor_scalar(mx[0:rows, s, 2:3], mx[0:rows, s, 1:2], other, -1.0,
                                          ALU.max, ALU.mult).then_inc(exps, 1)

                    def gate(t):
                        n = entry[("o", t)]
                        rows = P if t < 8 else DEC
                        dst = oT[:, bass.ds(4 + g, 1), P * t:P * t + rows].rearrange("p a t -> p (a t)")
                        dve.wait_ge(bank_ready, n + 1)
                        dve.tensor_tensor(dst, ps[:, 4 + n % 2, 0:rows], dst, ALU.mult).then_inc(dve_took, 1)

                    maxima(0)
                    for s, (t, h) in enumerate(steps):
                        if s + 1 < len(steps):
                            maxima(s + 1)
                        rows = P if t < 8 else DEC
                        blk = blocks_of(t)
                        if s >= 2:
                            dve.wait_ge(out_pe, s - 1)
                        for c in range(0, len(blk), 4):
                            part = blk[c:c + 4]
                            n = entry[("p", s, c // 4)]
                            full = sum(1 for b in part if b[1] == P)
                            dve.wait_ge(bank_ready, n + 1)
                            src = ps[:, 4 + n % 2, 0:P * len(part)].rearrange("p (b c) -> p b c", c=P)
                            dst = PT[:, s % 2, P * c:P * (c + len(part))].rearrange("p (b c) -> p b c", c=P)
                            if full:
                                ins = dve.tensor_copy(dst[:, 0:full, 0:rows], src[:, 0:full, 0:rows])
                            else:
                                ins = dve.tensor_copy(dst[0:DEC, 0, 0:rows], src[0:DEC, 0, 0:rows])
                            ins.then_inc(dve_took, 1)
                        if h == 0 and t:
                            gate(t - 1)
                        dve.wait_ge(probs, s + 1)
                        link(dve.reciprocal(mx[0:rows, s, 4:5], mx[0:rows, s, 3:4]))
                        dve.wait_ge(out_pe, s + 1)
                        if h == 0 and t >= 2:
                            dve.wait_ge(bank_ready, entry[("o", t - 2)] + 1)
                        dve.tensor_scalar(otok[0:rows, t % 2, 64 * h:64 * h + 64], ps[0:rows, 6 + s % 2, 0:64],
                                          mx[0:rows, s, 4:5], None, ALU.mult).then_inc(out_done, 1)
                    gate(8)
            barrier()

        def delta_group(L, g):
            ub = [work[:, 0:UW], work[:, PADTOK:PADTOK + UW]]
            cv = [slab(2), slab(3), slab(4)]
            qT, kT, vT = cv
            AT = vT
            Grow, brow, E, LT, XT, Kd, Vb = (slab(i) for i in (5, 6, 7, 8, 9, 10, 11))
            X, T, LM = slab(6), slab(0), slab(1)
            sq = [slab(8), slab(9)]
            rt = [slab(10), slab(11)]
            raw, sqo, ro = slab(8), slab(0), slab(1)
            at = 12 * PADTOK
            gcol, bcol, nbg, kdc = (work[:, at + 9 * i:at + 9 * i + 9] for i in range(4))
            at += 36
            egl = work[:, at:at + 9]
            at += 9
            cw, nw = work[:, at:at + 12], work[:, at + 12:at + 13]
            at += 13
            S = work[:, 13 * 0 + at:at + 3 * P].rearrange("p (b c) -> p b c", b=3)
            R, U = LM[:, 0:4 * P], LM[:, 4 * P:8 * P]
            gi = L * 4 + g
            owners = ["act"] * 12 + ["dve"] * 3 + ["act"] * 6 + ["dve"] * 9
            lev_first = []
            for i in range(len(LEVELS)):
                lev_first.append(len(owners))
                owners += ["act"] * 3 + ["dve"] * (6 if i < len(LEVELS) - 1 else 3)
            norm_first = len(owners)
            owners += ["act"] * 3
            ring = Ring(owners, 0, 8)

            def taken(who, n):
                return sum(o == who for o in owners[:n + 1])

            def level_out(eng, i, n):
                if i < 0:
                    eng.wait_ge(level_x, 1)
                else:
                    eng.wait_ge(dve_took, taken("dve", lev_first[i] + 3 + 2 * n + 1))

            with nc.Block() as block:
                @block.sync
                def _(sp):
                    sp.wait_ge(cleared, 4)
                    for x in range(2):
                        sp.dma_start(ub[x][:, 3 + SEQ:6 + SEQ], row("hist", gi * 3 + x)).then_inc(hist_loaded, 16)
                    sp.dma_start(cw, row("cwT", gi)).then_inc(params_loaded, 16)
                    sp.dma_start(nw, row("gnwT", L)).then_inc(params_loaded, 16)
                    sp.dma_start(Grow, dg[bass.ds(g, 1), :].rearrange("a c -> (a c)").partition_broadcast(P))\
                        .then_inc(params_loaded, 16)
                    sp.dma_start(brow, db[bass.ds(g, 1), :].rearrange("a c -> (a c)").partition_broadcast(P))\
                        .then_inc(params_loaded, 16)
                    with nc.allow_non_contiguous_dma(reason="a small turn of gates"):
                        sp.dma_start(gcol, dg[bass.ds(g, 1), :].rearrange("a (t p) -> (a p) t", p=P))\
                            .then_inc(params_loaded, 16)
                        sp.dma_start(bcol, db[bass.ds(g, 1), :].rearrange("a (t p) -> (a p) t", p=P))\
                            .then_inc(params_loaded, 16)
                    sp.dma_start(S[:, 2, :], row("sgdn", gi)).then_inc(params_loaded, 16)
                    for x in range(3):
                        if x == 2:
                            sp.wait_ge(conv_done, 1)
                            sp.wait_ge(stored, 64)
                            sp.dma_start(ub[0][:, 3 + SEQ:6 + SEQ], row("hist", gi * 3 + 2))\
                                .then_inc(hist_loaded, 16)
                        sp.wait_ge(act_took, 3 * (x + 1))
                        sp.dma_start(row("p_conv", gi * 3 + x), ub[x % 2][:, SEQ:SEQ + 3]).then_inc(stored, 16)
                        sp.dma_start(row("s_conv", gi * 3 + x), ub[x % 2][:, UW - 3:UW]).then_inc(stored, 16)
                    reload_weights(sp, L * N_BLOCKS + 28 + g * 4 + 4, [3, 6, 9, 12], 4)
                    sp.wait_ge(state_ready, 9)
                    sp.dma_start(row("p_gdn", gi), S[:, 0, :]).then_inc(stored, 16)
                    sp.dma_start(row("s_gdn", gi), S[:, 2, :]).then_inc(stored, 16)
                    sp.wait_ge(stored, 128)
                    sp.wait_ge(weights_loaded, 64)

                @block.tensor
                def _(pe):
                    for b in range(4):
                        project(pe, ring, 3 * b, b)

                    def turn(first, src):
                        for n, (t, c) in enumerate(G3):
                            ring.acquire(pe, first + n)
                            for j in range(c):
                                mm = pe.transpose(ps[:, ring.bank(first + n), P * j:P * j + P],
                                                  Q4(src)[:, t + j, :], ident)
                            mm.then_inc(bank_ready, 1)

                    def products(first, lhs, rhs, group):
                        n, (t, c) = group, G3[group]
                        ring.acquire(pe, first + n)
                        for j in range(c):
                            mm = pe.matmul(ps[:, ring.bank(first + n), P * j:P * j + P],
                                           Q4(lhs)[:, t + j, :], Q4(rhs)[:, t + j, :], start=True, stop=True)
                        mm.then_inc(bank_ready, 1)

                    pe.wait_ge(silu_done, 3)
                    turn(12, vT)
                    for x in range(2):
                        pe.wait_ge(squares, x + 1)
                        sum_features(pe, ring, 15 + 3 * x, sq[x])
                    pe.wait_ge(normed, 2)
                    turn(21, kT)
                    for n in range(3):
                        products(24, kT, kT, n)
                    for n in range(3):
                        products(27, kT, qT, n)
                    for i in range(len(LEVELS)):
                        f = lev_first[i]
                        pe.wait_ge(level_mask, i + 1)
                        for n in range(3):
                            level_out(pe, i - 1, n)
                            products(f, LM, X, n)
                        for n in range(3):
                            pe.wait_ge(act_took, taken("act", f + n))
                            products(f + 3 + (n if i < len(LEVELS) - 1 else 0), T, XT, n)
                            if i < len(LEVELS) - 1:
                                products(f + 4 + n, XT, T, n)
                    pe.wait_ge(act_took, taken("act", norm_first - 1))
                    pe.wait_ge(dve_took, taken("dve", norm_first - 1))
                    pe.wait_ge(decays, 3)
                    for i, t in enumerate([8] + list(range(8))):
                        src = S[:, 2 if t == 8 else t % 2, :]
                        if i:
                            pe.wait_ge(state_ready, i)
                        else:
                            pe.wait_ge(params_loaded, 112)
                        pe.wait_ge(cleared, 6)
                        pe.matmul(ps[:, 0, 0:P], Q4(kT)[:, t, :], src, start=True, stop=True)\
                            .then_inc(chain_pe, 1)
                        pe.wait_ge(rhs_ready, i + 1)
                        pe.matmul(ps[:, 1, 0:P], Q4(XT)[:, t, :], R[:, P * (i % 4):P * (i % 4) + P],
                                  start=True, stop=True).then_inc(chain_pe, 1)
                        if i >= 2:
                            pe.wait_ge(out_took, i - 1)
                        pe.matmul(ps[:, 4 + i % 2, 0:P], src, Q4(qT)[:, t, :], start=True, stop=False)
                        pe.wait_ge(upd_ready, i + 1)
                        Ui = U[:, P * (i % 4):P * (i % 4) + P]
                        pe.matmul(ps[:, 2, 0:P], Q4(Kd)[:, t, :], Ui, start=True, stop=True)\
                            .then_inc(chain_pe, 1)
                        pe.matmul(ps[:, 4 + i % 2, 0:P], Ui, Q4(AT)[:, t, :], start=False, stop=True)\
                            .then_inc(out_pe, 1)
                    pe.wait_ge(squares, 3)
                    pe.wait_ge(state_ready, 9)
                    sum_features(pe, ring, norm_first, sqo)

                @block.scalar
                def _(act):
                    for x in range(3):
                        for s, (a, w) in enumerate(SEGS):
                            n = 3 * x + s
                            act.wait_ge(bank_ready, n + 1)
                            if x == 0 and s == 0:
                                act.wait_ge(cleared, 4)
                            if x == 2 and s == 0:
                                act.wait_ge(conv_done, 1)
                                act.wait_ge(stored, 64)
                            b = 3 + a if s < 2 else 6 + SEQ
                            act.activation(ub[x % 2][:, b:b + w], ps[:, ring.bank(n), 0:w], ACT.Copy)\
                                .then_inc(act_took, 1)
                        if x:
                            act.wait_ge(conv_done, x)
                            act.activation(cv[x - 1][:, 0:TOK], cv[x - 1][:, 0:TOK], ACT.Silu)\
                                .then_inc(silu_done, 1)
                    for s, (a, w) in enumerate(SEGS):
                        act.wait_ge(bank_ready, 10 + s)
                        act.activation(oT[:, bass.ds(8 + g, 1), a:a + w].rearrange("p a t -> p (a t)"),
                                       ps[:, ring.bank(9 + s), 0:w], ACT.Silu).then_inc(act_took, 1)
                    act.wait_ge(conv_done, 3)
                    act.activation(vT[:, 0:TOK], vT[:, 0:TOK], ACT.Silu).then_inc(silu_done, 1)
                    for x in range(2):
                        act.wait_ge(silu_done, x + 1)
                        act.activation(sq[x][:, 0:TOK], cv[x][:, 0:TOK], ACT.Square).then_inc(squares, 1)
                    for x in range(2):
                        for s, (a, w) in enumerate(SEGS):
                            n = 15 + 3 * x + s
                            act.wait_ge(bank_ready, n + 1)
                            dst = (rt[0] if x == 0 else LM)[:, a:a + w]
                            if x == 1 and s == 0:
                                act.wait_ge(conv_done, 3)
                                act.wait_ge(stored, 96)
                            act.activation(dst, ps[:, ring.bank(n), 0:w], ACT.Sqrt,
                                           bias=l2_c if x == 0 else eps_c,
                                           scale=float(P) if x == 0 else 1.0).then_inc(act_took, 1)
                    act.wait_ge(decays, 1)
                    act.activation(E, E, ACT.Exp).then_inc(exps, 1)
                    act.activation(kdc, kdc, ACT.Exp).then_inc(exps, 1)
                    act.activation(Grow, Grow, ACT.Exp).then_inc(exps, 1)
                    act.activation(gcol, gcol, ACT.Exp).then_inc(exps, 1)
                    for i in range(len(LEVELS)):
                        for n, (t, c) in enumerate(G3):
                            e = lev_first[i] + n
                            act.wait_ge(bank_ready, e + 1)
                            act.activation(Q4(T)[:, t:t + c, :], Q4(ps[:, ring.bank(e), 0:P * c]), ACT.Copy)\
                                .then_inc(act_took, 1)
                    for i, t in enumerate([8] + list(range(8))):
                        act.wait_ge(out_pe, i + 1)
                        if i == 0:
                            act.wait_ge(level_mask, len(LEVELS))
                        act.activation(Q4(raw)[:, t, :], ps[:, 4 + i % 2, 0:P], ACT.Copy).then_inc(out_took, 1)
                    act.wait_ge(out_took, 9)
                    head_norm_gate("act", ring, norm_first, act, raw, sqo, ro)

                @block.vector
                def _(dve):
                    st = [0]

                    def link(ins):
                        ln_chain(dve, ins, st, dve_step)
                    dve.memset(ub[0][:, 0:3], 0.0).then_inc(cleared, 1)
                    dve.memset(ub[1][:, 0:3], 0.0).then_inc(cleared, 1)
                    dve.memset(qT[:, TOK:PADTOK], 0.0).then_inc(cleared, 1)
                    dve.memset(kT[:, TOK:PADTOK], 0.0).then_inc(cleared, 1)
                    dve.memset(vT[:, TOK:PADTOK], 0.0).then_inc(cleared, 1)
                    dve.memset(S[:, 0, :], 0.0).then_inc(cleared, 1)
                    dve.wait_ge(cleared, 6)
                    dve.wait_ge(params_loaded, 112)
                    for x in range(3):
                        u, c = ub[x % 2], cv[x]
                        dve.wait_ge(hist_loaded, 16 * (x + 1) if x == 2 else 32)
                        dve.wait_ge(act_took, 3 * (x + 1))
                        for a, b, w in ((0, 0, SEQ), (3 + SEQ, SEQ, DEC)):
                            link(dve.tensor_scalar(c[:, b:b + w], u[:, a:a + w], cw[:, 4 * x:4 * x + 1], None,
                                                   ALU.mult))
                            for j in range(1, 4):
                                ins = dve.scalar_tensor_tensor(c[:, b:b + w], u[:, a + j:a + j + w],
                                                               cw[:, 4 * x + j:4 * x + j + 1], c[:, b:b + w],
                                                               ALU.mult, ALU.add)
                                if b and j == 3:
                                    ins.then_inc(conv_done, 1)
                                    dve.wait_ge(conv_done, x + 1)
                                else:
                                    link(ins)
                    link(dve.tensor_tensor(Q4(E), Q4(Grow), gcol.unsqueeze(2).to_broadcast([P, NTILE, P]),
                                           ALU.subtract))
                    link(dve.tensor_tensor(kdc.unsqueeze(2), Q4(Grow)[:, :, P - 1:P], gcol.unsqueeze(2),
                                           ALU.subtract))
                    dve.tensor_scalar(E, E, 0.0, None, ALU.min).then_inc(decays, 1)
                    for n, (t, c) in enumerate(G3):
                        dve.wait_ge(bank_ready, 13 + n)
                        dve.tensor_tensor(Q4(Vb)[:, t:t + c, :], Q4(ps[:, ring.bank(12 + n), 0:P * c]),
                                          bcol[:, t:t + c].unsqueeze(2).to_broadcast([P, c, P]), ALU.mult)\
                            .then_inc(dve_took, 1)
                    for x in range(2):
                        dve.wait_ge(act_took, taken("act", 17 + 3 * x))
                        r = (rt[0] if x == 0 else LM)[:, 0:TOK]
                        link(dve.reciprocal(r, r))
                        dve.tensor_tensor(cv[x][:, 0:TOK], cv[x][:, 0:TOK], r, ALU.mult).then_inc(normed, 1)
                        dve.wait_ge(normed, x + 1)
                    dve.wait_ge(exps, 4)
                    link(dve.tensor_tensor(Q4(E), Q4(E), incl.unsqueeze(1).to_broadcast([P, NTILE, P]), ALU.mult))
                    link(dve.tensor_copy(egl.unsqueeze(2), Q4(Grow)[:, :, P - 1:P]))
                    link(dve.scalar_tensor_tensor(nbg, bcol, -1.0, gcol, ALU.mult, ALU.mult))
                    for n, (t, c) in enumerate(G3):
                        dve.wait_ge(bank_ready, 22 + n)
                        dve.tensor_tensor(Q4(Kd)[:, t:t + c, :], Q4(ps[:, ring.bank(21 + n), 0:P * c]),
                                          kdc[:, t:t + c].unsqueeze(2).to_broadcast([P, c, P]), ALU.mult)\
                            .then_inc(dve_took, 1)
                    link(dve.tensor_tensor(Q4(brow), Q4(brow), strict.unsqueeze(1).to_broadcast([P, NTILE, P]),
                                           ALU.mult))
                    for x, dst in enumerate((LT, AT)):
                        for n, (t, c) in enumerate(G3):
                            e = 24 + 3 * x + n
                            dve.wait_ge(bank_ready, e + 1)
                            dve.tensor_tensor(Q4(dst)[:, t:t + c, :], Q4(ps[:, ring.bank(e), 0:P * c]),
                                              Q4(E)[:, t:t + c, :], ALU.mult).then_inc(dve_took, 1)
                    dve.wait_ge(dve_took, taken("dve", 29))
                    link(dve.tensor_tensor(LT, LT, brow, ALU.mult))
                    link(dve.tensor_tensor(Q4(XT), Q4(LT), masks[:, 6, :].unsqueeze(1).to_broadcast([P, NTILE, P]),
                                           ALU.mult))
                    link(dve.tensor_tensor(Q4(XT), ident.unsqueeze(1).to_broadcast([P, NTILE, P]), Q4(XT),
                                           ALU.subtract))
                    dve.transpose(X, XT).then_inc(level_x, 1)
                    dve.tensor_tensor(qT, qT, Grow, ALU.mult).then_inc(decays, 2)
                    for i in range(len(LEVELS)):
                        f = lev_first[i]
                        if i:
                            dve.wait_ge(bank_ready, lev_first[i - 1] + 3)
                        dve.tensor_tensor(Q4(LM), Q4(LT),
                                          masks[:, 7 + i, :].unsqueeze(1).to_broadcast([P, NTILE, P]),
                                          ALU.mult).then_inc(level_mask, 1)
                        last = i == len(LEVELS) - 1
                        for n, (t, c) in enumerate(G3):
                            e = f + 3 + (n if last else 2 * n)
                            dve.wait_ge(bank_ready, e + (1 if last else 2))
                            ins = dve.tensor_tensor(Q4(XT)[:, t:t + c, :], Q4(XT)[:, t:t + c, :],
                                                    Q4(ps[:, ring.bank(e), 0:P * c]), ALU.subtract)
                            ins.then_inc(dve_took, 1)
                            if not last:
                                ins = dve.tensor_tensor(Q4(X)[:, t:t + c, :], Q4(X)[:, t:t + c, :],
                                                        Q4(ps[:, ring.bank(e + 1), 0:P * c]), ALU.subtract)
                                ins.then_inc(dve_took, 1)
                        dve.wait_ge(dve_took, taken("dve", f + (5 if last else 8)))
                    for i, t in enumerate([8] + list(range(8))):
                        Ri, Ui = (b[:, P * (i % 4):P * (i % 4) + P] for b in (R, U))
                        dve.wait_ge(chain_pe, 3 * i + 1)
                        dve.scalar_tensor_tensor(Ri, ps[:, 0, 0:P], nbg[:, t:t + 1], Q4(Vb)[:, t, :],
                                                 ALU.mult, ALU.add).then_inc(rhs_ready, 1)
                        dve.wait_ge(chain_pe, 3 * i + 2)
                        if i >= 4:
                            dve.wait_ge(out_pe, i - 3)
                        dve.tensor_copy(Ui, ps[:, 1, 0:P]).then_inc(upd_ready, 1)
                        src = S[:, 2 if t == 8 else t % 2, :]
                        dst = S[:, 2 if t == 8 else (t + 1) % 2, :]
                        dve.wait_ge(chain_pe, 3 * i + 3)
                        if t == 8:
                            dve.wait_ge(out_pe, 1)
                        elif i >= 2:
                            dve.wait_ge(out_pe, i)
                        dve.scalar_tensor_tensor(dst, src, egl[:, t:t + 1], ps[:, 2, 0:P], ALU.mult, ALU.add)\
                            .then_inc(state_ready, 1)
                        dve.wait_ge(state_ready, i + 1)
                    head_norm_gate("dve", ring, norm_first, dve, raw[:, 0:TOK], sqo, ro[:, 0:TOK], nw,
                                   oT[:, bass.ds(8 + g, 1), :].rearrange("p a t -> p (a t)"),
                                   link, taken("act", norm_first + 2))
            barrier()

        def merge(L):
            NB = 24
            mg = work[:, 0:KC * TOK].rearrange("p (k t) -> p k t", k=KC)
            at = KC * TOK
            wb = work[:, at:at + 4 * 512].rearrange("p (b k c) -> p b k c", b=4, k=4)
            at += 2048
            sg = work[:, at:at + 1024].rearrange("p (b c) -> p b c", b=2)
            at += 1024
            pr = work[:, at:at + 1024].rearrange("p (b c) -> p b c", b=2)

            def loads(u):
                return len(range(u, 3, -6))

            with nc.Block() as block:
                @block.sync
                def _(sp):
                    for u in range(NB + KC):
                        if u < NB:
                            if u >= 4:
                                sp.wait_ge(out_pe, 3 * (u - 3))
                            sp.dma_start(wb[:, u % 4], row("wbr", L * NB + u))\
                                .then_inc(branch_loaded[u % 4], 16)
                        if u >= 4:
                            if u >= 6:
                                if u - 6 < NB:
                                    sp.wait_ge(out_pe, 3 * (u - 5))
                                else:
                                    sp.wait_ge(bank_ready, 3 * (u - 5 - NB))
                            sp.dma_start(wt[:, u % 6, :, :], row("wblk", L * N_BLOCKS + 44 + u))\
                                .then_inc(slot_loaded[u % 6], 16)

                @block.tensor
                def _(pe):
                    n = 0
                    for u in range(NB):
                        dbk, br = u // 3, u % 3
                        if u >= 4:
                            pe.wait_ge(slot_loaded[u % 6], 16 * loads(u))
                        pe.wait_ge(branch_loaded[u % 4], 16 * (u // 4 + 1))
                        for s, (a, w) in enumerate(SEGS):
                            if n >= 4:
                                pe.wait_ge(logits, n - 3)
                            for k in range(KC):
                                mm = pe.matmul(ps[:, 2 * (n % 4), 0:w], wt[:, u % 6, k, :], hT[:, k, a:a + w],
                                               start=(k == 0), stop=(k == KC - 1))
                            mm.then_inc(scores_pe, 1)
                            for k in range(4):
                                mm = pe.matmul(ps[:, 2 * (n % 4) + 1, 0:w], wb[:, u % 4, k, :],
                                               oT[:, 4 * br + k, a:a + w], start=(k == 0), stop=(k == 3))
                            mm.then_inc(out_pe, 1)
                            n += 1
                    pe.wait_ge(tiles_made, 2 * NB)
                    m = 0
                    for u in range(NB, NB + KC):
                        pe.wait_ge(slot_loaded[u % 6], 16 * loads(u))
                        for s, (a, w) in enumerate(SEGS):
                            if m >= 8:
                                pe.wait_ge(dve_took, m - 7)
                            for k in range(KC):
                                mm = pe.matmul(ps[:, m % 8, 0:w], wt[:, u % 6, k, :], mg[:, k, a:a + w],
                                               start=(k == 0), stop=(k == KC - 1))
                            mm.then_inc(bank_ready, 1)
                            m += 1

                @block.scalar
                def _(act):
                    for n in range(3 * NB):
                        w = SEGS[n % 3][1]
                        act.wait_ge(scores_pe, n + 1)
                        if n >= 2:
                            act.wait_ge(logits, n - 1)
                        act.activation(sg[:, n % 2, 0:w], ps[:, 2 * (n % 4), 0:w], ACT.Sigmoid).then_inc(probs, 1)

                @block.vector
                def _(dve):
                    def adds(n):
                        return sum(1 for m in range(n) if (m // 3) % 3)

                    for n in range(3 * NB):
                        dbk, br = n // 9, (n // 3) % 3
                        a, w = SEGS[n % 3]
                        dst = mg[:, dbk, a:a + w]
                        dve.wait_ge(probs, n + 1)
                        dve.wait_ge(out_pe, n + 1)
                        to = pr[:, n % 2, 0:w] if br else dst
                        if br and adds(n - 1):
                            dve.wait_ge(tiles_made, adds(n - 1))
                        dve.tensor_tensor(to, ps[:, 2 * (n % 4) + 1, 0:w], sg[:, n % 2, 0:w], ALU.mult)\
                            .then_inc(logits, 1)
                        dve.wait_ge(logits, n + 1)
                        if br:
                            dve.tensor_tensor(dst, dst, to, ALU.add).then_inc(tiles_made, 1)
                    for m in range(3 * KC):
                        dbk, s = m // 3, m % 3
                        a, w = SEGS[s]
                        c = 0 if s < 2 else 1
                        dve.wait_ge(bank_ready, m + 1)
                        dve.scalar_tensor_tensor(xT[:, dbk, a:a + w], ps[:, m % 8, 0:w],
                                                 modT[:, 16 + dbk, c:c + 1], xT[:, dbk, a:a + w],
                                                 ALU.mult, ALU.add).then_inc(dve_took, 1)
            barrier()

        with nc.Fori(0, DEPTH) as L:
            norm_block(False, L)
            with nc.Fori(0, 2) as g:
                retention_group(L, g)
            with nc.Fori(0, 4) as g:
                fox_group(L, g)
            with nc.Fori(0, 4) as g:
                delta_group(L, g)
            merge(L)
        norm_block(True, None)


OUTS = {
    "yT": (KC, P, TOK),
    "p_k": (8, P, SEQ), "p_v": (8, P, 8, P), "p_logf": (2, 8, SEQ), "p_ret": (4, P, P), "p_gdn": (8, P, P),
    "p_conv": (24, P, 3),
    "s_k": (8, P, DEC), "s_v": (8, DEC, P), "s_logf": (2, 8, DEC), "s_ret": (4, P, P), "s_gdn": (8, P, P),
    "s_conv": (24, P, 3),
}


def column_blocks():
    ret, fox, gdn, gates = 0, 1536, 3592, 5648
    cols = []
    for g in range(2):
        cols += [ret + g * 128, ret + 256 + g * 128, ret + 512 + g * 256, ret + 640 + g * 256,
                 ret + 1024 + g * 256, ret + 1152 + g * 256]
    for g in range(4):
        cols += [fox + g * 128, fox + 512 + g * 128, fox + 1024 + g * 128, fox + 1544 + g * 128]
    for g in range(4):
        cols += [gdn + g * 128, gdn + 512 + g * 128, gdn + 1024 + g * 128, gdn + 1544 + g * 128]
    for d in range(8):
        cols += [gates + n * 1024 + d * 128 for n in range(3)]
    return cols


def kernel(**inputs):
    import concourse.bacc as _bacc
    from concourse.bass_utils import run_bass_kernel_spmd as _run

    a = {n: np.asarray(v) for n, v in inputs.items()}
    w_in = a["w_in"]

    def blocked(w):
        return w.reshape(KC, P, -1, P).transpose(2, 1, 0, 3)

    stream = [np.concatenate([blocked(w_in[l][:, c:c + P]) for c in column_blocks()]
                             + [blocked(a["w_out"][l])]) for l in range(DEPTH)]
    wsm = np.zeros((DEPTH, D, 96), np.float32)
    wsm[:, :, 0:8] = w_in[:, :, 3072:3080]
    wsm[:, :, 32:36] = w_in[:, :, 5128:5132]
    wsm[:, :, 64:68] = w_in[:, :, 5132:5136]
    gcols = np.zeros((DEPTH, 96, 4), np.float32)
    gcols[:, 0:8, 0] = a["fox_f_bias"]
    gcols[:, 32:36, 0] = a["gdn_dt_bias"]
    gcols[:, 32:36, 1] = a["gdn_a_log"]
    masks, rot, retc = shape_constants()
    x = np.concatenate([a["x_prompt"][0], a["x_sample"][0]])
    cvec = np.stack([a["c_prompt"][0], a["c_sample"][0]])
    conv_w = a["gdn_conv_w"].reshape(DEPTH, 4, 3, 4, P).transpose(0, 3, 4, 2, 1)
    hist = a["state_gdn_conv"].reshape(DEPTH, 3, 3, 4, P).transpose(0, 3, 2, 4, 1)
    arrays = {
        "xT": x.T.reshape(KC, P, TOK).transpose(1, 0, 2),
        "cT": cvec.T.reshape(KC, P, 2).transpose(1, 0, 2),
        "masks": masks, "rot": rot, "retc": retc,
        "wblk": np.concatenate(stream),
        "wbr": a["w_branch"].reshape(DEPTH, 3, 4, P, 8, P).transpose(0, 4, 1, 3, 2, 5).reshape(48, P, 4, P),
        "adaw": np.concatenate([blocked(a["ada_w"][l]) for l in range(DEPTH)]),
        "adabT": a["ada_b"].reshape(DEPTH, 24, P).transpose(0, 2, 1),
        "nwT": a["norm_w"].reshape(DEPTH, KC, P).transpose(0, 2, 1),
        "fnwT": a["final_norm_w"].reshape(KC, P).T,
        "wsm": wsm.reshape(DEPTH, KC, P, 96).transpose(0, 2, 1, 3),
        "gcols": gcols,
        "lfc": a["cache_fox_logf"][:, 0],
        "rnwT": a["ret_norm_w"].reshape(DEPTH * 2, 2, P).transpose(0, 2, 1),
        "gnwT": a["gdn_norm_w"].reshape(DEPTH, P, 1),
        "sret": a["state_ret"].reshape(DEPTH * 2, P, P),
        "sgdn": a["state_gdn"].reshape(DEPTH * 4, P, P),
        "kcT": a["cache_fox_k"].reshape(DEPTH * 4, 2, PAST, 64).transpose(0, 1, 3, 2).reshape(8, P, PAST),
        "vc": a["cache_fox_v"].reshape(DEPTH * 4, 2, 4, P, 64).transpose(0, 3, 2, 1, 4).reshape(8, P, 4, P),
        "cwT": conv_w.reshape(8, P, 12),
        "hist": hist.reshape(24, P, 3),
    }
    arrays = {n: np.ascontiguousarray(v) for n, v in arrays.items()}
    nc = _bacc.Bacc("TRN2", target_bir_lowering=False, num_devices=1)
    A = {n: nc.dram_tensor("in_" + n, v.shape, F32, kind="ExternalInput").ap() for n, v in arrays.items()}
    O = {n: nc.dram_tensor("out_" + n, s, F32, kind="ExternalOutput").ap() for n, s in OUTS.items()}
    build(nc, A, O)
    r = _run(nc, [{"in_" + n: v for n, v in arrays.items()}], core_ids=[0])
    o = {n: np.asarray(r.results[0]["out_" + n]) for n in OUTS}
    y = o["yT"].reshape(D, TOK).T

    def heads_k(v, n):
        return v.reshape(DEPTH, 1, 8, 64, n).transpose(0, 1, 2, 4, 3)

    def conv(v):
        return v.reshape(DEPTH, 4, 3, P, 3).transpose(0, 4, 2, 1, 3).reshape(DEPTH, 1, 3, 1536)

    p_v = o["p_v"].reshape(DEPTH, 4, P, 8, 2, 64).transpose(0, 1, 4, 3, 2, 5).reshape(DEPTH, 1, 8, SEQ, 64)
    s_v = o["s_v"].reshape(DEPTH, 4, DEC, 2, 64).transpose(0, 1, 3, 2, 4).reshape(DEPTH, 1, 8, DEC, 64)
    out = (y[None, :SEQ], y[None, SEQ:],
           heads_k(o["p_k"], SEQ), p_v, o["p_logf"].reshape(DEPTH, 1, 8, SEQ),
           o["p_ret"].reshape(DEPTH, 1, 4, 64, P), o["p_gdn"].reshape(DEPTH, 1, 4, P, P), conv(o["p_conv"]),
           heads_k(o["s_k"], DEC), s_v, o["s_logf"].reshape(DEPTH, 1, 8, DEC),
           o["s_ret"].reshape(DEPTH, 1, 4, 64, P), o["s_gdn"].reshape(DEPTH, 1, 4, P, P), conv(o["s_conv"]))
    return tuple(np.ascontiguousarray(v) for v in out)
```

```python
from contextlib import ExitStack

import numpy as np
import concourse.bass as bass
from concourse import mybir

F32 = mybir.dt.float32
F32R = mybir.dt.float32r
ALU = mybir.AluOpType
ACT = mybir.ActivationFunctionType
AXX = mybir.AxisListType.X

P = 128
D = 1024
DEPTH = 2
SEQ = 1024
DEC = 64
PAST = 512
TOK = SEQ + DEC
NTILE = SEQ // P + 1
PADTOK = NTILE * P
SEGS = [(0, 364), (364, 364), (728, TOK - 728)]
STREAMS = [(0, 512), (512, 512), (SEQ, DEC)]
KC = D // P
EPS = 1e-6
N_BLOCKS = 77
FKEYS = SEQ + PAST + DEC
SCAN_OFF = SEQ + PAST
UW = 3 + SEQ + 3 + DEC
RAW = [(3, 512), (515, 512), (UW - DEC, DEC)]
PIECES = [(3, 0, SEQ), (UW - DEC, SEQ, DEC)]
RAW_SEGS = [[(3, 0, 364)], [(367, 0, 364)], [(731, 0, SEQ - 728), (UW - DEC, SEQ - 728, DEC)]]
LEVELS = [2, 4, 8, 16, 32, 64]
GAMMA = [1.0 - 2.0 ** (-5.0 - h) for h in range(4)]


def shape_constants():
    i = np.arange(P)
    ident = np.eye(P)
    incl = (i[:, None] <= i[None, :]).astype(float)
    strict = (i[:, None] < i[None, :]).astype(float)
    lev = []
    for s in [1] + LEVELS:
        same = (i[:, None] // (2 * s)) == (i[None, :] // (2 * s))
        lev.append((same & ((i[:, None] // s) % 2 == 0) & ((i[None, :] // s) % 2 == 1)).astype(float))
    causal = np.where(i[None, :] > i[:, None], 1e30, 0.0)
    swap = np.zeros((P, P))
    for r in range(P):
        swap[(r // 64) * 64 + (r + 32) % 64, r] = 1.0
    masks = np.stack([ident, np.ones((P, P)), incl, strict, causal, swap] + lev, axis=1)
    half = 32
    inv = np.float32(10000.0) ** (-np.arange(half, dtype=np.float32) / np.float32(half))
    pos = np.concatenate([np.arange(SEQ), PAST + np.arange(DEC)]).astype(np.float32)
    ang = (inv.astype(np.float32)[:, None] * pos[None, :]).astype(np.float32)
    cos = np.cos(ang.astype(np.float64))
    sin = np.sin(ang.astype(np.float64))
    rot = np.stack([np.tile(cos, (4, 1)), np.concatenate([-sin, sin, -sin, sin])], axis=1)
    ret = []
    for g in range(2):
        gam = GAMMA[2 * g:2 * g + 2]
        dist = np.abs(i[:, None] - i[None, :])
        seen = (i[:, None] // 64) <= (i[None, :] // 64)
        dt = np.concatenate([np.where(seen, 0.125 * x ** dist, 0.0) for x in gam], axis=1)
        per = np.repeat(gam, 64)
        dq = per[:, None] ** (i[None, :] + 1)
        kd = 0.125 * per[None, :] ** (P - 1 - i)[:, None]
        kds = 0.125 * per[None, :] ** np.maximum(DEC - 1 - i, 0)[:, None]
        dc = np.stack([per ** P, per ** DEC], axis=1)
        ret.append(np.concatenate([dt, dq, kd, kds, dc], axis=1))
    f = np.float32
    return masks.astype(f), rot.astype(f), np.stack(ret).astype(f)


RETC = 2 * P + P + 2 * P + 2


def build(nc, A, O):
    with ExitStack() as ctx:
        def sb(name, shape, dt=F32):
            return ctx.enter_context(nc.sbuf_tensor("sb_" + name, shape, dt))

        sems = []

        def sem(name):
            s = ctx.enter_context(nc.semaphore(name))
            sems.append(s)
            return s

        hs = sb("h_split", [P, 2, KC, TOK], F32R)
        ws = sb("w_split", [P, 2, 2, KC, P], F32R)
        wraw = sb("w_raw", [P, 6, KC, P])
        raw_qk = sb("raw_qk", [P, 2, UW])
        masks = sb("masks", [P, 13, P])
        cT = sb("cT", [P, KC, 2])
        consts = sb("consts", [P, 4])
        nwT = sb("nwT", [P, KC])
        adab = sb("adab", [P, 24])
        modT = sb("modT", [P, 24, 2])
        ident, ones, incl, strict = (masks[:, m, :] for m in range(4))
        causal, swap = masks[:, 4, :], masks[:, 5, :]
        eps_c, l2_c, one_c = consts[:, 0:1], consts[:, 1:2], consts[:, 2:3]
        ps = ctx.enter_context(nc.psum_tensor("ps", [P, 8, 512], F32))

        def scratch(name, shape):
            return nc.dram_tensor("scratch_" + name, shape, F32, kind="Internal").ap()

        dx = scratch("x", (KC, P, TOK))
        do = scratch("o", (12, P, TOK))
        dfk = scratch("fcum", (8, FKEYS))
        dg = scratch("g", (4, PADTOK))
        db = scratch("beta", (4, PADTOK))

        slot_loaded = [sem(f"slot_loaded_{i}") for i in range(6)]
        branch_loaded = [sem(f"branch_loaded_{i}") for i in range(4)]
        x_loaded = [sem(f"x_loaded_{i}") for i in range(3)]
        x_stored = [sem(f"x_stored_{i}") for i in range(3)]
        params_loaded = sem("params_loaded")
        hist_loaded = sem("hist_loaded")
        o_loaded = sem("o_loaded")
        split_hi = sem("split_hi")
        split_ready = sem("split_ready")
        branch_hi = sem("branch_hi")
        branch_ready = sem("branch_ready")
        proj_done = sem("proj_done")
        evacuated = sem("evacuated")
        bank_ready = sem("bank_ready")
        act_took = sem("act_took")
        dve_took = sem("dve_took")
        stored = sem("stored")
        act_step = sem("act_step")
        dve_step = sem("dve_step")
        squares = sem("squares")
        squares_used = sem("squares_used")
        roots = sem("roots")
        slot_used = sem("slot_used")
        h_scaled = sem("h_scaled")
        h_hi = sem("h_hi")
        h_ready = sem("h_ready")
        gates_raw = sem("gates_raw")
        tap_done = sem("tap_done")
        conv_done = sem("conv_done")
        silu_done = sem("silu_done")
        normed = sem("normed")
        decays = sem("decays")
        exps = sem("exps")
        level_mask = sem("level_mask")
        level_x = sem("level_x")
        state_ready = sem("state_ready")
        chain_pe = sem("chain_pe")
        rhs_ready = sem("rhs_ready")
        upd_ready = sem("upd_ready")
        out_pe = sem("out_pe")
        out_took = sem("out_took")
        out_done = sem("out_done")
        scores_pe = sem("scores_pe")
        logits = sem("logits")
        probs = sem("probs")
        merged = sem("merged")
        scaled = sem("scaled")
        gate_pe = sem("gate_pe")
        cleared = sem("cleared")
        nums = [s.num for s in sems]
        clear = range(min(nums), max(nums) + 1)
        assert len(clear) == len(sems)

        def barrier():
            nc.multi_engine_barrier(list(nc.engines), sems_to_clear=clear)

        def ln_chain(eng, ins, count, s):
            count[0] += 1
            ins.then_inc(s, 1)
            eng.wait_ge(s, count[0])

        class Ring:
            def __init__(self, owners, first, banks):
                self.owners, self.first, self.banks = owners, first, banks

            def bank(self, n):
                return self.first + n % self.banks

            def acquire(self, pe, n):
                m = n - self.banks
                if m >= 0 and not isinstance(self.owners[m], str):
                    pe.wait_ge(*self.owners[m])
                elif m >= 0:
                    who = self.owners[m]
                    pe.wait_ge(act_took if who == "act" else dve_took,
                               sum(o == who for o in self.owners[:m + 1]))

        def three(pe, out, w_hi, w_lo, x_hi, x_lo, first, last):
            pe.matmul(out, w_hi, x_hi, start=first, stop=False)
            pe.matmul(out, w_hi, x_lo, start=False, stop=False)
            return pe.matmul(out, w_lo, x_hi, start=False, stop=last)

        def project(pe, e, first_bank, banks, slot, done=None, src=None, after=None):
            for s, (a, w) in enumerate(SEGS):
                if e + s >= banks:
                    pe.wait_ge(evacuated, e + s - banks + 1)
                for k in range(KC):
                    if after is not None and s == 0:
                        pe.wait_ge(after, k + 1)
                    mm = three(pe, ps[:, first_bank + (e + s) % banks, 0:w], ws[:, slot, 0, k, :],
                               ws[:, slot, 1, k, :], hs[:, 0, k, a:a + w], hs[:, 1, k, a:a + w],
                               k == 0, k == KC - 1)
                    if k == KC - 1:
                        mm.then_inc(proj_done, 1)
                    yield

        def blocks(pe, todo, first_bank, banks):
            for e, b in todo:
                if b >= 2:
                    pe.wait_ge(split_ready, b - 1)
                yield from project(pe, e, first_bank, banks, b % 2)

        def turns(gen, n):
            for _ in range(n):
                next(gen, None)

        def take(act, e, first_bank, banks, dst, func=ACT.Copy):
            w = dst.shape[-1]
            act.wait_ge(proj_done, e + 1)
            act.activation(dst, ps[0:dst.shape[0], first_bank + e % banks, 0:w], func).then_inc(evacuated, 1)

        def take_into(act, e, s, first_bank, banks, buf):
            act.wait_ge(proj_done, e + 1)
            for u, c, w in RAW_SEGS[s]:
                ins = act.activation(buf[:, u:u + w], ps[:, first_bank + e % banks, c:c + w], ACT.Copy)
            ins.then_inc(evacuated, 1)

        def take_raw(act, e, e0, first_bank, banks):
            x, s = divmod(e - e0, 3)
            take_into(act, e, s, first_bank, banks, raw_qk[:, x, :])

        def split_block(pool, slot, to, n):
            pool.tensor_copy(ws[:, to, 0], wraw[:, slot]).then_inc(split_hi, 1)
            pool.wait_ge(split_hi, n)
            pool.tensor_tensor(ws[:, to, 1], wraw[:, slot], ws[:, to, 0].bitcast(F32), ALU.subtract)\
                .then_inc(split_ready, 1)

        def split_blocks(pool, last_entry):
            nb = len(last_entry)
            for b in range(2, nb + 2):
                pool.wait_ge(proj_done, last_entry[b - 2])
                if b >= nb:
                    pool.wait_ge(slot_loaded[b - nb], 16)
                split_block(pool, b % nb, b % 2, b - 1)

        def reload_weights(sp, base, count):
            for i in range(count):
                if i >= 2:
                    sp.wait_ge(split_ready, i - 1)
                sp.dma_start(wraw[:, i], row("wblk", base + i)).then_inc(slot_loaded[i], 16)

        def all_loaded(sp, count):
            for i in range(count):
                sp.wait_ge(slot_loaded[i], 16)

        def sum_features(pe, ring, n, sq):
            for s, (a, w) in enumerate(SEGS):
                ring.acquire(pe, n + s)
                pe.matmul(ps[:, ring.bank(n + s), 0:w], ones, sq[:, a:a + w],
                          start=True, stop=True).then_inc(bank_ready, 1)

        def row(name, idx):
            ap = A[name] if name in A else O[name]
            dims = " ".join("bcdef"[:len(ap.shape) - 2])
            return ap[bass.ds(idx, 1)].rearrange(f"a p {dims} -> (a p) {dims}" if dims else "a p -> (a p)")

        def Q4(ap):
            return ap.rearrange("p (t c) -> p t c", c=P)

        def tiles_of(mask):
            return mask.unsqueeze(1).to_broadcast([P, NTILE, P])

        G3 = [(0, 4), (4, 4), (8, 1)]

        with nc.Block() as block:
            @block.sync
            def _(sp):
                sp.dma_start(masks[:, :, :], A["masks"]).then_inc(params_loaded, 16)
                sp.dma_start(cT[:, :, :], A["cT"]).then_inc(params_loaded, 16)
                sp.dma_start(dx, A["xT"]).then_inc(stored, 16)
                for n in range(4):
                    sp.dma_start(wraw[:, n], A["adaw"][n]).then_inc(params_loaded, 16)
                sp.wait_ge(stored, 16)
                sp.wait_ge(params_loaded, 96)

            @block.scalar
            def _(act):
                act.wait_ge(params_loaded, 96)
                act.activation(cT[:, :, :], cT[:, :, :], ACT.Silu)

            @block.vector
            def _(dve):
                dve.memset(eps_c, EPS)
                dve.memset(l2_c, EPS * P)
                dve.memset(one_c, 1.0)
                dve.memset(raw_qk[:, :, 0:3], 0.0)
        barrier()

        def norm_phase(final, L, ph):
            work = ph.enter_context(nc.sbuf_tensor("sb_norm_" + ("last" if final else "layer"), [P, 14500], F32))
            x = work[:, 0:KC * TOK].rearrange("p (k t) -> p k t", k=KC)
            at = KC * TOK
            sq = work[:, at:at + 2 * TOK].rearrange("p (b t) -> p b t", b=2)
            at += 2 * TOK
            rstd = work[:, at:at + TOK]
            at += TOK
            lfx = work[0:8, at:at + FKEYS]
            at += FKEYS
            gcols, scw = work[0:96, at:at + 4], work[:, at + 4:at + 20].rearrange("p (k c) -> p k c", k=KC)
            gz, ga, gl, gre = (work[0:96, i * PADTOK:(i + 1) * PADTOK] for i in range(4))
            fre = work[0:8, 4 * PADTOK:4 * PADTOK + FKEYS]
            NADA = 16
            with nc.Block() as block:
                @block.sync
                def _(sp):
                    for c in range(4):
                        sp.dma_start(x[:, 2 * c:2 * c + 2, :], dx[2 * c:2 * c + 2].rearrange("k p t -> p k t"))\
                            .then_inc(branch_loaded[c], 16)
                    if final:
                        sp.dma_start(nwT[:, :], A["fnwT"]).then_inc(params_loaded, 16)
                        for k in range(KC):
                            sp.wait_ge(out_done, k + 1)
                            sp.dma_start(O["yT"][k], x[:, k, :]).then_inc(stored, 16)
                        sp.wait_ge(stored, 16 * KC)
                        return
                    sp.dma_start(nwT[:, :], row("nwT", L)).then_inc(params_loaded, 16)
                    sp.dma_start(adab[:, :], row("adabT", L)).then_inc(params_loaded, 16)
                    sp.dma_start(gcols, row("gcols", L)).then_inc(params_loaded, 16)
                    sp.dma_start(lfx[:, SEQ:SEQ + PAST], row("lfc", L)).then_inc(params_loaded, 16)
                    sp.dma_start(wraw[:, 4], row("wblk", L * N_BLOCKS)).then_inc(slot_loaded[4], 16)
                    sp.dma_start(wraw[:, 5], row("wblk", L * N_BLOCKS + 1)).then_inc(slot_loaded[5], 16)
                    for n in range(4, NADA):
                        sp.wait_ge(slot_used, n - 3)
                        sp.dma_start(wraw[:, n % 4], row("adaw", L * 24 + n)).then_inc(slot_loaded[n % 4], 16)
                    sp.wait_ge(split_ready, 1)
                    sp.dma_start(wraw[:, 4], row("wblk", L * N_BLOCKS + 2)).then_inc(slot_loaded[4], 16)
                    for i in range(4):
                        sp.wait_ge(slot_used, NADA - 3 + i)
                        sp.dma_start(wraw[:, i], row("wblk", L * N_BLOCKS + 3 + i)).then_inc(slot_loaded[i], 16)
                    sp.wait_ge(split_ready, 2)
                    sp.dma_start(wraw[:, 5], row("wblk", L * N_BLOCKS + 8)).then_inc(slot_loaded[5], 16)
                    sp.wait_ge(split_ready, 3)
                    sp.dma_start(wraw[:, 4], row("wblk", L * N_BLOCKS + 7)).then_inc(slot_loaded[4], 16)
                    sp.wait_ge(decays, 1)
                    sp.dma_start(row("p_logf", L), lfx[:, 0:SEQ]).then_inc(stored, 16)
                    sp.dma_start(row("s_logf", L), lfx[:, SCAN_OFF:FKEYS]).then_inc(stored, 16)
                    sp.wait_ge(decays, 2)
                    sp.dma_start(dfk, fre).then_inc(stored, 16)
                    sp.wait_ge(exps, 1)
                    sp.dma_start(db, gz[64:68, :]).then_inc(stored, 16)
                    sp.wait_ge(decays, 3)
                    sp.dma_start(dg, ga[32:36, :]).then_inc(stored, 16)
                    sp.wait_ge(stored, 80)
                    for i in range(4):
                        sp.wait_ge(slot_loaded[i], 64)
                    sp.wait_ge(slot_loaded[4], 48)
                    sp.wait_ge(slot_loaded[5], 32)

                @block.gpsimd
                def _(pool):
                    if final:
                        return
                    pool.wait_ge(slot_loaded[4], 16)
                    split_block(pool, 4, 1, 1)
                    pool.wait_ge(slot_loaded[5], 16)
                    split_block(pool, 5, 0, 2)
                    pool.wait_ge(slot_loaded[4], 32)
                    pool.wait_ge(gate_pe, 3)
                    split_block(pool, 4, 1, 3)
                    for i in range(2):
                        pool.wait_ge(slot_loaded[i], 64)
                        pool.wait_ge(proj_done, 3 * (i + 1))
                        split_block(pool, i, i, 4 + i)

                @block.tensor
                def _(pe):
                    for k in range(KC):
                        pe.wait_ge(squares, k + 1)
                        for s, (a, w) in enumerate(SEGS):
                            mm = pe.matmul(ps[:, s, 0:w], ones, sq[:, k % 2, a:a + w],
                                           start=(k == 0), stop=(k == KC - 1))
                        mm.then_inc(squares_used, 1)
                    if final:
                        return
                    for n in range(NADA):
                        if n >= 4:
                            pe.wait_ge(slot_loaded[n % 4], 16 * (n // 4))
                        for k in range(KC):
                            mm = pe.matmul(ps[:, 3, 2 * n:2 * n + 2], wraw[:, n % 4, k, :], cT[:, k, :],
                                           start=(k == 0), stop=(k == KC - 1))
                        mm.then_inc(slot_used, 1)
                    pe.wait_ge(split_ready, 1)
                    pe.wait_ge(roots, 3)
                    for s, (a, w) in enumerate(SEGS):
                        for k in range(KC):
                            if s == 0:
                                pe.wait_ge(h_ready, k + 1)
                            mm = three(pe, ps[:, s, 0:w], ws[:, 1, 0, k, :], ws[:, 1, 1, k, :],
                                       hs[:, 0, k, a:a + w], hs[:, 1, k, a:a + w], k == 0, k == KC - 1)
                        mm.then_inc(gate_pe, 1)
                    for x_ in range(2):
                        pe.wait_ge(split_ready, 2 + x_)
                        for _ in project(pe, 3 * x_, 4, 4, x_):
                            pass

                @block.scalar
                def _(act):
                    for k in range(KC):
                        if k % 2 == 0:
                            act.wait_ge(branch_loaded[k // 2], 16)
                        if k >= 2:
                            act.wait_ge(squares_used, k - 1)
                        act.activation(sq[:, k % 2, :], x[:, k, :], ACT.Square).then_inc(squares, 1)
                    act.wait_ge(squares_used, KC)
                    for s, (a, w) in enumerate(SEGS):
                        act.activation(rstd[:, a:a + w], ps[:, s, 0:w], ACT.Sqrt, bias=eps_c,
                                       scale=1.0 / D).then_inc(roots, 1)
                    if final:
                        return
                    for k in range(KC):
                        act.wait_ge(h_scaled, k + 1)
                        for c, (a, w) in enumerate(((0, SEQ), (SEQ, DEC))):
                            ins = act.activation(hs[:, 0, k, a:a + w], x[:, k, a:a + w], ACT.Identity,
                                                 bias=modT[:, k, c:c + 1])
                        ins.then_inc(h_hi, 1)
                    act.wait_ge(params_loaded, 64)
                    act.activation(gcols[:, 2:3], gcols[:, 1:2], ACT.Exp).then_inc(act_step, 1)
                    act.wait_ge(gates_raw, 4)
                    act.activation(gl, ga, ACT.Exp, scale=-1.0).then_inc(act_step, 1)
                    act.wait_ge(act_step, 2)
                    act.activation(gl, gl, ACT.Ln, bias=one_c[0:96]).then_inc(act_took, 1)
                    for e in range(3):
                        take_raw(act, e, 0, 4, 4)
                    act.wait_ge(conv_done, 1)
                    act.activation(gz[64:68, 0:TOK], gl[64:68, 0:TOK], ACT.Exp).then_inc(exps, 1)
                    for e in range(3, 6):
                        take_raw(act, e, 0, 4, 4)

                @block.vector
                def _(dve):
                    st = [0]

                    def link(ins):
                        ln_chain(dve, ins, st, dve_step)
                    if not final:
                        dve.wait_ge(params_loaded, 64)
                        dve.wait_ge(slot_used, NADA)
                        link(dve.tensor_tensor(modT[:, 0:16, :],
                                               ps[:, 3, 0:32].rearrange("p (n c) -> p n c", c=2),
                                               adab[:, 0:16].unsqueeze(2).to_broadcast([P, 16, 2]), ALU.add))
                        link(dve.tensor_scalar(scw, modT[:, 8:16, :], 1.0, None, ALU.add))
                        link(dve.tensor_tensor(scw, scw, nwT[:, :].unsqueeze(2).to_broadcast([P, KC, 2]),
                                               ALU.mult))
                    else:
                        dve.wait_ge(params_loaded, 16)
                    dve.wait_ge(roots, 3)
                    link(dve.reciprocal(rstd, rstd))

                    def scale(k):
                        for c, (a, w) in enumerate(((0, SEQ), (SEQ, DEC))):
                            col = nwT[:, k:k + 1] if final else scw[:, k, c:c + 1]
                            ins = dve.scalar_tensor_tensor(x[:, k, a:a + w], x[:, k, a:a + w], col,
                                                           rstd[:, a:a + w], ALU.mult, ALU.mult)
                        ins.then_inc(out_done if final else h_scaled, 1)

                    scale(0)
                    for k in range(KC):
                        if k + 1 < KC:
                            scale(k + 1)
                        if final:
                            continue
                        dve.wait_ge(h_hi, k + 1)
                        for c, (a, w) in enumerate(((0, SEQ), (SEQ, DEC))):
                            ins = dve.scalar_tensor_tensor(hs[:, 1, k, a:a + w], x[:, k, a:a + w],
                                                           modT[:, k, c:c + 1],
                                                           hs[:, 0, k, a:a + w].bitcast(F32),
                                                           ALU.add, ALU.subtract)
                        ins.then_inc(h_ready, 1)
                    if final:
                        return
                    dve.wait_ge(h_ready, KC)
                    dve.memset(ga[:, TOK:PADTOK], 0.0)
                    link(dve.memset(gz[:, TOK:PADTOK], 0.0))
                    for s, (a, w) in enumerate(SEGS):
                        dve.wait_ge(gate_pe, s + 1)
                        dve.tensor_scalar(gz[:, a:a + w], ps[0:96, s, 0:w], gcols[:, 0:1], None,
                                          ALU.add).then_inc(gates_raw, 1)
                    dve.wait_ge(gates_raw, 3)
                    dve.scalar_tensor_tensor(ga, gz, -1.0, gz, ALU.mult, ALU.max).then_inc(gates_raw, 1)
                    dve.memset(gre, 1.0).then_inc(cleared, 1)
                    dve.wait_ge(cleared, 1)
                    link(dve.memset(Q4(gre)[:, :, 0:1], 0.0))
                    link(dve.memset(fre, 1.0))
                    link(dve.memset(fre[:, SEQ:SEQ + 1], 0.0))
                    dve.wait_ge(act_took, 1)
                    dve.wait_ge(act_step, 2)
                    link(dve.scalar_tensor_tensor(ga, gz, 0.0, gl, ALU.max, ALU.add))
                    link(dve.tensor_scalar(ga, ga, gcols[:, 2:3], -1.0, ALU.mult, ALU.mult))
                    dve.scalar_tensor_tensor(gl, gz, 0.0, gl, ALU.min, ALU.subtract).then_inc(conv_done, 1)
                    dve.wait_ge(conv_done, 1)
                    link(dve.memset(ga[:, TOK:PADTOK], 0.0))
                    dve.tensor_copy(lfx[:, 0:SEQ], gl[0:8, 0:SEQ])
                    dve.tensor_copy(lfx[:, SCAN_OFF:FKEYS], gl[0:8, SEQ:TOK]).then_inc(decays, 1)
                    dve.wait_ge(decays, 1)
                    link(dve.tensor_tensor_scan(fre, fre, lfx, 0.0, ALU.mult, ALU.add))
                    dve.tensor_scalar(fre, fre, 8.0, None, ALU.mult).then_inc(decays, 1)
                    dve.tensor_tensor_scan(ga[32:36, :], gre[32:36, :], ga[32:36, :], 0.0, ALU.mult,
                                           ALU.add).then_inc(decays, 1)
            barrier()

        def root_pair(act, ring, n, r):
            for s, (a, w) in enumerate(SEGS):
                act.wait_ge(bank_ready, n + s + 1)
                act.activation(r[:, a:a + w], ps[:, ring.bank(n + s), 0:w], ACT.Sqrt, bias=eps_c,
                               scale=1.0 / P).then_inc(act_took, 1)

        def finish_head(dve, link, need, raw, r, w_col, z):
            dve.wait_ge(act_took, need)
            link(dve.reciprocal(r, r))
            link(dve.scalar_tensor_tensor(raw, raw, w_col, r, ALU.mult, ALU.mult))
            dve.tensor_tensor(z, z, raw, ALU.mult).then_inc(out_done, 1)

        def retention_group(L, g, ph):
            work = ph.enter_context(nc.sbuf_tensor("sb_ret", [P, 13 * PADTOK + 11 * P + RETC + 8 + 4096], F32))

            def slab(i):
                return work[:, i * PADTOK:(i + 1) * PADTOK]
            q, k_, V = slab(0), slab(1), work[:, 2 * PADTOK:4 * PADTOK].rearrange("p (t c) -> p t c", c=2 * P)
            cos, sin, tmp, Kd = slab(4)[:, 0:TOK], slab(5)[:, 0:TOK], slab(6), slab(7)
            AT = [slab(8), slab(9)]
            raw, sq, r = [slab(4), slab(5)], slab(6), [slab(7), slab(8)]
            zs = [slab(10)[:, 0:TOK], slab(11)[:, 0:TOK]]
            base = 13 * PADTOK
            S = work[:, base:base + 11 * P].rearrange("p (t c) -> p t c", c=P)
            base += 11 * P
            rc = work[:, base:base + RETC]
            DT = [rc[:, 0:P], rc[:, P:2 * P]]
            dq, kd = rc[:, 2 * P:3 * P], rc[:, 3 * P:5 * P]
            dc = rc[:, 5 * P:5 * P + 2]
            base += RETC
            nw = work[:, base:base + 2]
            ada = work[:, base + 8:base + 8 + 4096].rearrange("p (b k c) -> p b k c", b=4, k=KC)
            gi = L * 2 + g
            VN = [(0, 2), (2, 2), (4, 2), (6, 2), (8, 1)]
            owners = (["dve"] * 16 + [(state_ready, 4), (state_ready, 8), (state_ready, 9)]
                      + ["act"] * 12)
            ring = Ring(owners, 0, 5)
            B0, NB = 5, 3
            with nc.Block() as block:
                @block.sync
                def _(sp):
                    sp.dma_start(cos, A["rot"][:, 0, :]).then_inc(params_loaded, 16)
                    sp.dma_start(sin, A["rot"][:, 1, :]).then_inc(params_loaded, 16)
                    sp.dma_start(rc, row("retc", g)).then_inc(params_loaded, 16)
                    sp.dma_start(nw, row("rnwT", gi)).then_inc(params_loaded, 16)
                    sp.dma_start(S[:, 9, :], row("sret", gi)).then_inc(params_loaded, 16)
                    for n in range(4):
                        sp.dma_start(ada[:, n], row("adaw", L * 24 + 16 + 4 * g + n)).then_inc(o_loaded, 16)
                    reload_weights(sp, L * N_BLOCKS + 3 + g * 6 + 6, 6)
                    sp.wait_ge(state_ready, 9)
                    sp.dma_start(row("p_ret", gi), S[:, 8, :]).then_inc(stored, 16)
                    sp.dma_start(row("s_ret", gi), S[:, 10, :]).then_inc(stored, 16)
                    for h in range(2):
                        sp.wait_ge(out_done, h + 1)
                        sp.dma_start(do[bass.ds(2 * g + h, 1)].rearrange("a p t -> (a p) t"), zs[h])\
                            .then_inc(stored, 16)
                    sp.wait_ge(stored, 64)
                    all_loaded(sp, 6)

                @block.gpsimd
                def _(pool):
                    split_blocks(pool, [5, 5, 8, 11, 14, 17])

                @block.tensor
                def _(pe):
                    for x in range(2):
                        for s, (a, w) in enumerate(STREAMS):
                            ring.acquire(pe, 3 * x + s)
                            pe.matmul(ps[:, ring.bank(3 * x + s), 0:w], swap,
                                      raw_qk[:, x, RAW[s][0]:RAW[s][0] + w],
                                      start=True, stop=True).then_inc(bank_ready, 1)
                    for e, (t, c) in enumerate(VN):
                        if e >= NB:
                            pe.wait_ge(evacuated, e - NB + 1)
                        for j in range(c):
                            a = (t + j) * P if t + j < 8 else TOK - P
                            for k in range(KC):
                                mm = three(pe, ps[:, B0 + e % NB, 256 * j:256 * j + 256],
                                           hs[:, 0, k, a:a + P], hs[:, 1, k, a:a + P],
                                           ws[:, 0:2, 0, k, :], ws[:, 0:2, 1, k, :], k == 0, k == KC - 1)
                        mm.then_inc(proj_done, 1)
                    fill = blocks(pe, [(5, 2), (8, 3), (11, 4), (14, 5)], B0, NB)
                    pe.wait_ge(o_loaded, 64)
                    ring.acquire(pe, 6)
                    for n in range(4):
                        for k in range(KC):
                            mm = pe.matmul(ps[:, ring.bank(6), 2 * n:2 * n + 2], ada[:, n, k, :], cT[:, k, :],
                                           start=(k == 0), stop=(k == KC - 1))
                    mm.then_inc(bank_ready, 1)
                    pe.wait_ge(normed, 2)
                    for n, (t, c) in enumerate(G3):
                        ring.acquire(pe, 7 + n)
                        for j in range(c):
                            mm = pe.transpose(ps[:, ring.bank(7 + n), P * j:P * j + P],
                                              Q4(k_)[:, t + j, :], ident)
                        mm.then_inc(bank_ready, 1)
                        turns(fill, 4)
                    for h in range(2):
                        for n, (t, c) in enumerate(G3):
                            e = 10 + 3 * h + n
                            ring.acquire(pe, e)
                            for j in range(c):
                                mm = pe.matmul(ps[:, ring.bank(e), P * j:P * j + P],
                                               Q4(k_)[64 * h:64 * h + 64, t + j, :],
                                               Q4(q)[64 * h:64 * h + 64, t + j, :], start=True, stop=True)
                            mm.then_inc(bank_ready, 1)
                            turns(fill, 4)
                    pe.wait_ge(dve_took, 10)
                    pe.wait_ge(evacuated, 5)
                    pe.wait_ge(cleared, 2)
                    for n, (t, c) in enumerate(G3):
                        ring.acquire(pe, 16 + n)
                        for j in range(c):
                            for h in range(2):
                                mm = pe.matmul(ps[64 * h:64 * h + 64, ring.bank(16 + n), P * j:P * j + P],
                                               Q4(Kd)[:, t + j, 64 * h:64 * h + 64],
                                               V[:, t + j, P * h:P * h + P], start=True, stop=True)
                        mm.then_inc(bank_ready, 1)
                        turns(fill, 4)
                    for h in range(2):
                        pe.wait_ge(dve_took, 10 + 3 * (h + 1))
                        pe.wait_ge(conv_done, 1)
                        for n, (t, c) in enumerate(G3):
                            e = 19 + 3 * h + n
                            ring.acquire(pe, e)
                            pe.wait_ge(state_ready, t + c - 1 if t < 8 else 8)
                            for j in range(c):
                                tt = t + j
                                out = ps[:, ring.bank(e), P * j:P * j + P]
                                mm = pe.matmul(out, V[:, tt, P * h:P * h + P], Q4(AT[h])[:, tt, :],
                                               start=True, stop=(tt == 0))
                                if tt:
                                    mm = pe.matmul(out, S[64 * h:64 * h + 64, 9 if tt == 8 else tt, :],
                                                   Q4(q)[64 * h:64 * h + 64, tt, :], start=False, stop=True)
                            mm.then_inc(bank_ready, 1)
                            turns(fill, 4)
                    for h in range(2):
                        pe.wait_ge(squares, h + 1)
                        for s, (a, w) in enumerate(SEGS):
                            ring.acquire(pe, 25 + 3 * h + s)
                            pe.matmul(ps[:, ring.bank(25 + 3 * h + s), 0:w], ones, sq[:, a:a + w],
                                      start=True, stop=True).then_inc(bank_ready, 1)
                            turns(fill, 4)
                    turns(fill, 96)

                @block.scalar
                def _(act):
                    for e, (t, c) in enumerate(VN):
                        act.wait_ge(proj_done, e + 1)
                        lo = 0 if t < 8 else DEC
                        act.activation(V[0:P - lo, t:t + c, :],
                                       ps[lo:P, B0 + e % NB, 0:256 * c].rearrange("p (t c) -> p t c", t=c),
                                       ACT.Copy).then_inc(evacuated, 1)

                    def taken(m):
                        if m < 6:
                            a, w = SEGS[m % 3]
                            take(act, 5 + m, B0, NB, zs[m // 3][:, a:a + w], ACT.Silu)
                        else:
                            take_raw(act, 5 + m, 11, B0, NB)

                    def copy_out(j):
                        h, n = divmod(j, 3)
                        t, c = G3[n]
                        act.wait_ge(bank_ready, 20 + j)
                        act.activation(Q4(raw[h])[:, t:t + c, :], Q4(ps[:, ring.bank(19 + j), 0:P * c]),
                                       ACT.Copy).then_inc(act_took, 1)

                    def root(j):
                        h, s = divmod(j, 3)
                        a, w = SEGS[s]
                        act.wait_ge(bank_ready, 26 + j)
                        act.activation(r[h][:, a:a + w], ps[:, ring.bank(25 + j), 0:w], ACT.Sqrt, bias=eps_c,
                                       scale=1.0 / P).then_inc(act_took, 1)

                    def square(h):
                        act.wait_ge(act_took, 3 * (h + 1))
                        act.activation(sq, raw[h], ACT.Square).then_inc(squares, 1)

                    for m in range(6):
                        taken(m)
                    act.wait_ge(normed, 2)
                    copy_out(0)
                    copy_out(1)
                    taken(6)
                    copy_out(2)
                    copy_out(3)
                    taken(7)
                    copy_out(4)
                    copy_out(5)
                    taken(8)
                    square(0)
                    root(0)
                    root(1)
                    taken(9)
                    root(2)
                    square(1)
                    root(3)
                    taken(10)
                    root(4)
                    root(5)
                    taken(11)

                @block.vector
                def _(dve):
                    st = [0]

                    def link(ins):
                        ln_chain(dve, ins, st, dve_step)
                    dve.memset(V[64:128, 8, :], 0.0).then_inc(cleared, 1)
                    link(dve.memset(q[:, TOK:PADTOK], 0.0))
                    dve.memset(k_[:, TOK:PADTOK], 0.0).then_inc(cleared, 1)
                    dve.wait_ge(params_loaded, 80)
                    for x, dst in enumerate((q, k_)):
                        for s, (a, w) in enumerate(STREAMS):
                            dve.wait_ge(bank_ready, 1 + 3 * x + s)
                            dve.tensor_tensor(tmp[:, a:a + w], ps[:, ring.bank(3 * x + s), 0:w],
                                              sin[:, a:a + w], ALU.mult).then_inc(dve_took, 1)
                        for u, a, w in PIECES:
                            link(dve.tensor_tensor(dst[:, a:a + w], raw_qk[:, x, u:u + w], cos[:, a:a + w],
                                                   ALU.mult))
                        dve.wait_ge(dve_took, 3 * (x + 1))
                        dve.tensor_tensor(dst[:, 0:TOK], dst[:, 0:TOK], tmp[:, 0:TOK], ALU.add)\
                            .then_inc(normed, 1)
                        dve.wait_ge(normed, x + 1)
                    dve.wait_ge(bank_ready, 7)
                    dve.tensor_tensor(modT[:, bass.ds(16 + 4 * g, 4), :],
                                      ps[:, ring.bank(6), 0:8].rearrange("p (n c) -> p n c", c=2),
                                      adab[:, bass.ds(16 + 4 * g, 4)].unsqueeze(2).to_broadcast([P, 4, 2]),
                                      ALU.add).then_inc(dve_took, 1)
                    for n, (t, c) in enumerate(G3):
                        dve.wait_ge(bank_ready, 8 + n)
                        col = kd[:, 0:P] if t < 8 else kd[:, P:2 * P]
                        dve.tensor_tensor(Q4(Kd)[:, t:t + c, :], Q4(ps[:, ring.bank(7 + n), 0:P * c]),
                                          col.unsqueeze(1).to_broadcast([P, c, P]), ALU.mult)\
                            .then_inc(dve_took, 1)
                    for h in range(2):
                        for n, (t, c) in enumerate(G3):
                            e = 10 + 3 * h + n
                            dve.wait_ge(bank_ready, e + 1)
                            dve.tensor_tensor(Q4(AT[h])[:, t:t + c, :], Q4(ps[:, ring.bank(e), 0:P * c]),
                                              DT[h].unsqueeze(1).to_broadcast([P, c, P]), ALU.mult)\
                                .then_inc(dve_took, 1)
                    dve.tensor_tensor(Q4(q), Q4(q), tiles_of(dq), ALU.mult).then_inc(conv_done, 1)
                    for t in range(NTILE):
                        n = 16 + t // 4
                        dve.wait_ge(bank_ready, n + 1)
                        upd = ps[:, ring.bank(n), P * (t % 4):P * (t % 4) + P]
                        if t == 0:
                            ins = dve.tensor_copy(S[:, 1, :], upd)
                        elif t < 8:
                            ins = dve.scalar_tensor_tensor(S[:, t + 1, :], S[:, t, :], dc[:, 0:1], upd,
                                                           ALU.mult, ALU.add)
                        else:
                            ins = dve.scalar_tensor_tensor(S[:, 10, :], S[:, 9, :], dc[:, 1:2], upd,
                                                           ALU.mult, ALU.add)
                        ins.then_inc(state_ready, 1)
                        dve.wait_ge(state_ready, t + 1)
                    dve.wait_ge(evacuated, 11)
                    for h in range(2):
                        finish_head(dve, link, 9 + 3 * h, raw[h][:, 0:TOK], r[h][:, 0:TOK], nw[:, h:h + 1],
                                    zs[h])
            barrier()

        def fox_group(L, g, ph):
            work = ph.enter_context(nc.sbuf_tensor("sb_fox", [P, 16600], F32))
            qT = work[:, 0:TOK]
            at = TOK
            kT = work[:, at:at + FKEYS]
            at += FKEYS
            V = work[:, at:at + 13 * P].rearrange("p (t c) -> p t c", c=P)
            at += 13 * P
            fk = work[:, at:at + 2 * FKEYS].rearrange("p (h c) -> p h c", h=2)
            at += 2 * FKEYS
            fd = work[:, at:at + 2 * 9 * P].rearrange("p (h t c) -> p h t c", h=2, t=9)
            at += 18 * P
            lg = work[:, at:at + 2048].rearrange("p (b c) -> p b c", b=2)
            at += 2048
            PT = work[:, at:at + 2048].rearrange("p (b c) -> p b c", b=2)
            at += 2048
            otok = work[:, at:at + 2 * P].rearrange("p (b c) -> p b c", b=2)
            at += 2 * P
            mx = work[:, at:at + 18 * 5].rearrange("p (s c) -> p s c", c=5)
            at += 90
            zs, oo = work[:, at:at + TOK], work[:, at + TOK:at + 2 * TOK]
            vT = oo
            gi = L * 4 + g
            VN = [(0, 4), (4, 4), (8, 1)]
            B0, NB = 6, 2
            steps = [(t, h) for t in range(9) for h in range(2)]

            def blocks_of(t):
                if t < 8:
                    return [(P * b, P, b) for b in range(t + 1)]
                return [(SEQ + P * b, P, 8 + b) for b in range(4)] + [(SCAN_OFF, DEC, 12)]

            entry = {}
            order = 3
            for s, (t, h) in enumerate(steps):
                for c in range((len(blocks_of(t)) + 3) // 4):
                    entry[("p", s, c)] = order
                    order += 1
                if h == 0 and t:
                    entry[("o", t - 1)] = order
                    order += 1
                entry[("v", s)] = order
                order += 1
            entry[("o", 8)] = order
            last_p = [max(v for e, v in entry.items() if e[0] == "p" and e[1] == s) for s in range(18)]
            with nc.Block() as block:
                @block.sync
                def _(sp):
                    sp.dma_start(fk.rearrange("p h c -> p (h c)"),
                                 dfk[bass.ds(2 * g, 2), :].rearrange("a c -> (a c)").partition_broadcast(P))\
                        .then_inc(hist_loaded, 16)
                    sp.dma_start(kT[:, SEQ:SEQ + PAST], row("kcT", gi)).then_inc(params_loaded, 16)
                    sp.dma_start(V[:, 8:12, :], row("vc", gi)).then_inc(params_loaded, 16)
                    reload_weights(sp, L * N_BLOCKS + 15 + g * 4 + 4, 4)
                    sp.wait_ge(act_took, 4)
                    sp.dma_start(row("p_k", gi), kT[:, 0:SEQ]).then_inc(stored, 16)
                    sp.dma_start(row("s_k", gi), kT[:, SCAN_OFF:FKEYS]).then_inc(stored, 16)
                    sp.wait_ge(dve_took, 3)
                    sp.dma_start(row("p_v", gi), V[:, 0:8, :]).then_inc(stored, 16)
                    sp.dma_start(row("s_v", gi), V[0:DEC, 12, :]).then_inc(stored, 16)
                    sp.wait_ge(out_took, 1)
                    sp.dma_start(do[bass.ds(4 + g, 1)].rearrange("a p t -> (a p) t"), zs).then_inc(stored, 16)
                    sp.wait_ge(stored, 80)
                    all_loaded(sp, 4)

                @block.gpsimd
                def _(pool):
                    pool.wait_ge(hist_loaded, 16)
                    for h in range(2):
                        pool.tensor_tensor(fd[:, h, 0:8, :], Q4(fk[:, h, 0:SEQ]),
                                           causal.unsqueeze(1).to_broadcast([P, 8, P]), ALU.add)\
                            .then_inc(level_mask, 1)
                        pool.tensor_tensor(fd[:, h, 8, 0:DEC], fk[:, h, SCAN_OFF:FKEYS], causal[:, 0:DEC],
                                           ALU.add).then_inc(level_mask, 1)
                    split_blocks(pool, [3, 6, 9, 12])

                @block.tensor
                def _(pe):
                    for _ in project(pe, 0, B0, NB, 0):
                        pass
                    fill = blocks(pe, [(3, 1), (6, 2), (9, 3)], B0, NB)

                    def qk(s):
                        t, h = steps[s]
                        rows = P if t < 8 else DEC
                        blk = blocks_of(t)
                        lo, n = blk[0][0], sum(b[1] for b in blk)
                        if s >= 2:
                            pe.wait_ge(logits, s - 1)
                        for a in range(0, n, 512):
                            w = min(512, n - a)
                            mm = pe.matmul(ps[0:rows, 2 * (s % 2) + a // 512, 0:w],
                                           qT[64 * h:64 * h + 64, P * t:P * t + rows],
                                           kT[64 * h:64 * h + 64, lo + a:lo + a + w], start=True, stop=True)
                        mm.then_inc(scores_pe, 1)

                    def get(n):
                        if n >= 2:
                            pe.wait_ge(dve_took, n - 1)
                        return 4 + n % 2

                    def turn_out(t):
                        rows = P if t < 8 else DEC
                        b = get(entry[("o", t)])
                        pe.wait_ge(dve_took, entry[("v", 2 * t + 1)] + 1)
                        pe.transpose(ps[:, b, 0:rows], otok[0:rows, t % 2, :], ident[0:rows, 0:rows])\
                            .then_inc(bank_ready, 1)

                    pe.wait_ge(act_took, 4)
                    pe.wait_ge(params_loaded, 32)
                    qk(0)
                    turns(fill, 2)
                    for n, (t, c) in enumerate(VN):
                        pe.wait_ge(evacuated, 3)
                        b = get(n)
                        for j in range(c):
                            w = P if t < 8 else DEC
                            mm = pe.transpose(ps[0:w, b, P * j:P * j + P], vT[:, P * (t + j):P * (t + j) + w],
                                              ident)
                        mm.then_inc(bank_ready, 1)
                    for s, (t, h) in enumerate(steps):
                        if s + 1 < len(steps):
                            qk(s + 1)
                        turns(fill, 2 if s else 0)
                        rows = P if t < 8 else DEC
                        blk = blocks_of(t)
                        pe.wait_ge(probs, s + 1)
                        for c in range(0, len(blk), 4):
                            b = get(entry[("p", s, c // 4)])
                            for j, (col, w, _) in enumerate(blk[c:c + 4]):
                                mm = pe.transpose(ps[0:w, b, P * j:P * j + rows],
                                                  lg[0:rows, s % 2, (c + j) * P:(c + j) * P + w],
                                                  ident[0:rows, 0:rows])
                            mm.then_inc(bank_ready, 1)
                        if h == 0 and t:
                            turn_out(t - 1)
                        turns(fill, 2)
                        b = get(entry[("v", s)])
                        pe.wait_ge(dve_took, last_p[s] + 1)
                        for c, (col, w, vt) in enumerate(blk):
                            mm = pe.matmul(ps[0:rows, b, 0:64], PT[0:w, s % 2, P * c:P * c + rows],
                                           V[0:w, vt, 64 * h:64 * h + 64],
                                           start=(c == 0), stop=(c == len(blk) - 1))
                        mm.then_inc(bank_ready, 1)
                    turns(fill, 72)
                    turn_out(8)

                @block.scalar
                def _(act):
                    for x, dst in enumerate((qT, kT)):
                        for i, (u, a, w) in enumerate(PIECES):
                            b = SCAN_OFF if x == 1 and i == 1 else a
                            act.activation(dst[:, b:b + w], raw_qk[:, x, u:u + w], ACT.Copy).then_inc(act_took, 1)
                    for s, (a, w) in enumerate(SEGS):
                        take(act, s, B0, NB, vT[:, a:a + w])

                    def taken(m):
                        if m < 3:
                            a, w = SEGS[m]
                            take(act, 3 + m, B0, NB, zs[:, a:a + w], ACT.Silu)
                        else:
                            take_raw(act, 3 + m, 6, B0, NB)

                    for s, (t, h) in enumerate(steps):
                        rows = P if t < 8 else DEC
                        n = sum(b[1] for b in blocks_of(t))
                        act.wait_ge(exps, s + 1)
                        act.activation(lg[0:rows, s % 2, 0:n], lg[0:rows, s % 2, 0:n], ACT.Exp,
                                       bias=mx[0:rows, s, 2:3], accum_out=mx[0:rows, s, 3:4])\
                            .then_inc(probs, 1)
                        if s % 2 == 0 and s:
                            taken(s // 2 - 1)
                    taken(8)

                @block.vector
                def _(dve):
                    st = [0]

                    def link(ins):
                        ln_chain(dve, ins, st, dve_step)

                    def maxima(s):
                        t, h = steps[s]
                        rows = P if t < 8 else DEC
                        blk = blocks_of(t)
                        lo, w = blk[0][0], blk[-1][1]
                        n = P * (len(blk) - 1)
                        dve.wait_ge(scores_pe, s + 1)
                        if s >= 2:
                            dve.wait_ge(bank_ready, last_p[s - 2] + 1)
                        src = ps[0:rows, 2 * (s % 2):2 * (s % 2) + 2, :].rearrange("p b c -> p (b c)")
                        if n:
                            dve.tensor_tensor_reduce(out=lg[0:rows, s % 2, 0:n], in0=src[:, 0:n],
                                                     in1=fk[0:rows, h, lo:lo + n], scale=0.125, scalar=-3e38,
                                                     op0=ALU.subtract, op1=ALU.max,
                                                     accum_out=mx[0:rows, s, 0:1])
                        dve.tensor_tensor_reduce(out=lg[0:rows, s % 2, n:n + w], in0=src[:, n:n + w],
                                                 in1=fd[0:rows, h, t, 0:w], scale=0.125, scalar=-3e38,
                                                 op0=ALU.subtract, op1=ALU.max,
                                                 accum_out=mx[0:rows, s, 1:2]).then_inc(logits, 1)
                        dve.wait_ge(logits, s + 1)
                        other = mx[0:rows, s, 0:1] if n else mx[0:rows, s, 1:2]
                        dve.tensor_scalar(mx[0:rows, s, 2:3], mx[0:rows, s, 1:2], other, -1.0,
                                          ALU.max, ALU.mult).then_inc(exps, 1)

                    def keep(t):
                        n = entry[("o", t)]
                        rows = P if t < 8 else DEC
                        dve.wait_ge(bank_ready, n + 1)
                        dve.tensor_copy(oo[:, P * t:P * t + rows], ps[:, 4 + n % 2, 0:rows]).then_inc(dve_took, 1)

                    dve.wait_ge(hist_loaded, 16)
                    dve.wait_ge(level_mask, 4)
                    maxima(0)
                    for n, (t, c) in enumerate(VN):
                        dve.wait_ge(bank_ready, n + 1)
                        rows, to = (P, t) if t < 8 else (DEC, 12)
                        dve.tensor_copy(V[0:rows, to:to + c, :], Q4(ps[0:rows, 4 + n % 2, 0:P * c]))\
                            .then_inc(dve_took, 1)
                    for s, (t, h) in enumerate(steps):
                        if s + 1 < len(steps):
                            maxima(s + 1)
                        rows = P if t < 8 else DEC
                        blk = blocks_of(t)
                        if s >= 2:
                            dve.wait_ge(bank_ready, entry[("v", s - 2)] + 1)
                        for c in range(0, len(blk), 4):
                            part = blk[c:c + 4]
                            n = entry[("p", s, c // 4)]
                            full = sum(1 for b in part if b[1] == P)
                            dve.wait_ge(bank_ready, n + 1)
                            src = ps[:, 4 + n % 2, 0:P * len(part)].rearrange("p (b c) -> p b c", c=P)
                            dst = PT[:, s % 2, P * c:P * (c + len(part))].rearrange("p (b c) -> p b c", c=P)
                            if full:
                                ins = dve.tensor_copy(dst[:, 0:full, 0:rows], src[:, 0:full, 0:rows])
                            else:
                                ins = dve.tensor_copy(dst[0:DEC, 0, 0:rows], src[0:DEC, 0, 0:rows])
                            ins.then_inc(dve_took, 1)
                        if h == 0 and t:
                            keep(t - 1)
                        dve.wait_ge(probs, s + 1)
                        link(dve.reciprocal(mx[0:rows, s, 4:5], mx[0:rows, s, 3:4]))
                        n = entry[("v", s)]
                        dve.wait_ge(bank_ready, n + 1)
                        dve.tensor_scalar(otok[0:rows, t % 2, 64 * h:64 * h + 64], ps[0:rows, 4 + n % 2, 0:64],
                                          mx[0:rows, s, 4:5], None, ALU.mult).then_inc(dve_took, 1)
                    keep(8)
                    dve.wait_ge(dve_took, entry[("o", 8)] + 1)
                    dve.wait_ge(evacuated, 6)
                    dve.tensor_tensor(zs, zs, oo, ALU.mult).then_inc(out_took, 1)
            barrier()

        def delta_group(L, g, ph):
            work = ph.enter_context(nc.sbuf_tensor("sb_delta", [P, 13 * PADTOK + 1000], F32))

            def slab(i):
                return work[:, i * PADTOK:(i + 1) * PADTOK]
            ub = [raw_qk[:, 0, :], raw_qk[:, 1, :], work[:, 0:UW]]
            cv = [slab(2), slab(3), slab(4)]
            qT, kT, vT = cv
            AT = vT
            Grow, brow, E, LT, XT, Kd, Vb = (slab(i) for i in (5, 6, 7, 8, 9, 10, 11))
            X, T, LM = slab(6), slab(0), slab(1)
            sq = [slab(8), slab(9)]
            rt = [slab(10), slab(11)]
            raw, sqo, ro = slab(8), slab(0), slab(1)
            zs = slab(12)[:, 0:TOK]
            at = 13 * PADTOK
            gcol, bcol, nbg, kdc = (work[:, at + 9 * i:at + 9 * i + 9] for i in range(4))
            at += 36
            egl = work[:, at:at + 9]
            at += 9
            cw, nw = work[:, at:at + 12], work[:, at + 12:at + 13]
            at += 13
            S = work[:, 13 * 0 + at:at + 3 * P].rearrange("p (b c) -> p b c", b=3)
            R, U = LM[:, 0:4 * P], LM[:, 4 * P:8 * P]
            gi = L * 4 + g
            owners = ["act"] * 6 + ["dve"] * 12
            lev_first = []
            for i in range(len(LEVELS)):
                lev_first.append(len(owners))
                owners += ["act"] * 3 + ["dve"] * (6 if i < len(LEVELS) - 1 else 3)
            norm_first = len(owners)
            owners += ["act"] * 3
            ring = Ring(owners, 0, 5)
            B0, NB = 5, 3

            def taken(who, n):
                return sum(o == who for o in owners[:n + 1])

            def turned(n):
                return min(n // 8, 6)

            def level_out(eng, i, n):
                if i < 0:
                    eng.wait_ge(level_x, 1)
                else:
                    eng.wait_ge(dve_took, taken("dve", lev_first[i] + 3 + 2 * n + 1))

            with nc.Block() as block:
                @block.sync
                def _(sp):
                    for x in range(3):
                        sp.dma_start(ub[x][:, 3 + SEQ:6 + SEQ], row("hist", gi * 3 + x)).then_inc(hist_loaded, 16)
                    sp.dma_start(cw, row("cwT", gi)).then_inc(params_loaded, 16)
                    sp.dma_start(nw, row("gnwT", L)).then_inc(params_loaded, 16)
                    sp.dma_start(Grow, dg[bass.ds(g, 1), :].rearrange("a c -> (a c)").partition_broadcast(P))\
                        .then_inc(params_loaded, 16)
                    sp.dma_start(brow, db[bass.ds(g, 1), :].rearrange("a c -> (a c)").partition_broadcast(P))\
                        .then_inc(params_loaded, 16)
                    with nc.allow_non_contiguous_dma(reason="a small turn of gates"):
                        sp.dma_start(gcol, dg[bass.ds(g, 1), :].rearrange("a (t p) -> (a p) t", p=P))\
                            .then_inc(params_loaded, 16)
                        sp.dma_start(bcol, db[bass.ds(g, 1), :].rearrange("a (t p) -> (a p) t", p=P))\
                            .then_inc(params_loaded, 16)
                    sp.dma_start(S[:, 2, :], row("sgdn", gi)).then_inc(params_loaded, 16)
                    for x in range(3):
                        if x == 2:
                            sp.wait_ge(evacuated, 3)
                        sp.dma_start(row("p_conv", gi * 3 + x), ub[x][:, SEQ:SEQ + 3]).then_inc(stored, 16)
                        sp.dma_start(row("s_conv", gi * 3 + x), ub[x][:, UW - 3:UW]).then_inc(stored, 16)
                    reload_weights(sp, L * N_BLOCKS + 31 + g * 4 + 4, 4)
                    sp.wait_ge(state_ready, 9)
                    sp.dma_start(row("p_gdn", gi), S[:, 0, :]).then_inc(stored, 16)
                    sp.dma_start(row("s_gdn", gi), S[:, 2, :]).then_inc(stored, 16)
                    sp.wait_ge(out_done, 1)
                    sp.dma_start(do[bass.ds(8 + g, 1)].rearrange("a p t -> (a p) t"), zs).then_inc(stored, 16)
                    sp.wait_ge(stored, 144)
                    all_loaded(sp, 4)

                @block.gpsimd
                def _(pool):
                    split_blocks(pool, [3, 6, 9, 12])

                @block.tensor
                def _(pe):
                    for _ in project(pe, 0, B0, NB, 0):
                        pass
                    fill = blocks(pe, [(3, 1), (6, 2), (9, 3)], B0, NB)

                    def turn(first, src):
                        for n, (t, c) in enumerate(G3):
                            ring.acquire(pe, first + n)
                            for j in range(c):
                                mm = pe.transpose(ps[:, ring.bank(first + n), P * j:P * j + P],
                                                  Q4(src)[:, t + j, :], ident)
                            mm.then_inc(bank_ready, 1)

                    def products(first, lhs, rhs, group):
                        n, (t, c) = group, G3[group]
                        ring.acquire(pe, first + n)
                        for j in range(c):
                            mm = pe.matmul(ps[:, ring.bank(first + n), P * j:P * j + P],
                                           Q4(lhs)[:, t + j, :], Q4(rhs)[:, t + j, :], start=True, stop=True)
                        mm.then_inc(bank_ready, 1)

                    for x in range(2):
                        turns(fill, 8)
                        pe.wait_ge(squares, x + 1)
                        sum_features(pe, ring, 3 * x, sq[x])
                    turns(fill, 8)
                    pe.wait_ge(silu_done, 3)
                    turn(6, vT)
                    pe.wait_ge(normed, 2)
                    turn(9, kT)
                    for n in range(3):
                        products(12, kT, kT, n)
                    for n in range(3):
                        products(15, kT, qT, n)
                    for i in range(len(LEVELS)):
                        f = lev_first[i]
                        pe.wait_ge(level_mask, i + 1)
                        for n in range(3):
                            level_out(pe, i - 1, n)
                            products(f, LM, X, n)
                        turns(fill, 2)
                        for n in range(3):
                            pe.wait_ge(act_took, taken("act", f + n))
                            products(f + 3 + (n if i < len(LEVELS) - 1 else 0), T, XT, n)
                            if i < len(LEVELS) - 1:
                                products(f + 4 + n, XT, T, n)
                        turns(fill, 1)
                    pe.wait_ge(act_took, taken("act", norm_first - 1))
                    pe.wait_ge(dve_took, taken("dve", norm_first - 1))
                    pe.wait_ge(decays, 3)
                    for i, t in enumerate([8] + list(range(8))):
                        src = S[:, 2 if t == 8 else t % 2, :]
                        if i:
                            pe.wait_ge(state_ready, i)
                        else:
                            pe.wait_ge(params_loaded, 112)
                        pe.wait_ge(cleared, 6)
                        pe.matmul(ps[:, 0, 0:P], Q4(kT)[:, t, :], src, start=True, stop=True)\
                            .then_inc(chain_pe, 1)
                        turns(fill, 1)
                        pe.wait_ge(rhs_ready, i + 1)
                        pe.matmul(ps[:, 1, 0:P], Q4(XT)[:, t, :], R[:, P * (i % 4):P * (i % 4) + P],
                                  start=True, stop=True).then_inc(chain_pe, 1)
                        if i >= 2:
                            pe.wait_ge(out_took, i - 1)
                        pe.matmul(ps[:, 3 + i % 2, 0:P], src, Q4(qT)[:, t, :], start=True, stop=False)
                        turns(fill, 1)
                        pe.wait_ge(upd_ready, i + 1)
                        Ui = U[:, P * (i % 4):P * (i % 4) + P]
                        pe.matmul(ps[:, 2, 0:P], Q4(Kd)[:, t, :], Ui, start=True, stop=True)\
                            .then_inc(chain_pe, 1)
                        pe.matmul(ps[:, 3 + i % 2, 0:P], Ui, Q4(AT)[:, t, :], start=False, stop=True)\
                            .then_inc(out_pe, 1)
                        turns(fill, 1)
                    turns(fill, 72)
                    pe.wait_ge(squares, 3)
                    pe.wait_ge(state_ready, 9)
                    sum_features(pe, ring, norm_first, sqo)

                @block.scalar
                def _(act):
                    def tap(x):
                        for u, a, w in ((0, 0, SEQ), (3 + SEQ, SEQ, DEC)):
                            ins = act.activation(cv[x][:, a:a + w], ub[x][:, u:u + w], ACT.Copy,
                                                 scale=cw[:, 4 * x:4 * x + 1])
                        ins.then_inc(tap_done, 1)

                    def silu(x):
                        act.wait_ge(conv_done, x + 1)
                        act.activation(cv[x][:, 0:TOK], cv[x][:, 0:TOK], ACT.Silu).then_inc(silu_done, 1)

                    def square(x):
                        act.wait_ge(silu_done, x + 1)
                        act.activation(sq[x][:, 0:TOK], cv[x][:, 0:TOK], ACT.Square).then_inc(squares, 1)

                    def z(s):
                        a, w = SEGS[s]
                        take(act, 3 + s, B0, NB, zs[:, a:a + w], ACT.Silu)

                    act.wait_ge(hist_loaded, 48)
                    act.wait_ge(params_loaded, 112)
                    tap(0)
                    tap(1)
                    for s in range(3):
                        take_into(act, s, s, B0, NB, ub[2])
                    act.wait_ge(evacuated, 3)
                    act.wait_ge(cleared, 6)
                    tap(2)
                    silu(0)
                    square(0)
                    z(0)
                    silu(1)
                    square(1)
                    z(1)
                    def roots_of(x):
                        for s, (a, w) in enumerate(SEGS):
                            n = 3 * x + s
                            act.wait_ge(bank_ready, n + 1)
                            act.activation(rt[x][:, a:a + w], ps[:, ring.bank(n), 0:w], ACT.Sqrt,
                                           bias=l2_c if x == 0 else eps_c,
                                           scale=float(P) if x == 0 else 1.0).then_inc(act_took, 1)

                    roots_of(0)
                    roots_of(1)
                    z(2)
                    silu(2)
                    act.wait_ge(decays, 1)
                    act.activation(E, E, ACT.Exp).then_inc(exps, 1)
                    act.activation(kdc, kdc, ACT.Exp).then_inc(exps, 1)
                    act.activation(Grow, Grow, ACT.Exp).then_inc(exps, 1)
                    act.activation(gcol, gcol, ACT.Exp).then_inc(exps, 1)
                    for i in range(len(LEVELS)):
                        if i == 0:
                            act.wait_ge(conv_done, 3)
                            act.wait_ge(stored, 96)
                        for n, (t, c) in enumerate(G3):
                            e = lev_first[i] + n
                            act.wait_ge(bank_ready, e + 1)
                            act.activation(Q4(T)[:, t:t + c, :], Q4(ps[:, ring.bank(e), 0:P * c]), ACT.Copy)\
                                .then_inc(act_took, 1)
                        for m in range(6):
                            if turned(3 * (i - 1) + 2) <= m < turned(3 * i + 2):
                                take_raw(act, 6 + m, 6, B0, NB)
                    for i, t in enumerate([8] + list(range(8))):
                        act.wait_ge(out_pe, i + 1)
                        if i == 0:
                            act.wait_ge(level_mask, len(LEVELS))
                        act.activation(Q4(raw)[:, t, :], ps[:, 3 + i % 2, 0:P], ACT.Copy).then_inc(out_took, 1)
                        for m in range(6):
                            if turned(18 + 3 * i if i else 17) <= m < turned(18 + 3 * (i + 1)):
                                take_raw(act, 6 + m, 6, B0, NB)
                    for m in range(turned(45), 6):
                        take_raw(act, 6 + m, 6, B0, NB)
                    act.wait_ge(out_took, 9)
                    act.activation(sqo, raw, ACT.Square).then_inc(squares, 1)
                    root_pair(act, ring, norm_first, ro)

                @block.vector
                def _(dve):
                    st = [0]

                    def link(ins):
                        ln_chain(dve, ins, st, dve_step)
                    dve.memset(ub[2][:, 0:3], 0.0).then_inc(cleared, 1)
                    dve.memset(S[:, 1, :], 0.0).then_inc(cleared, 1)
                    dve.memset(qT[:, TOK:PADTOK], 0.0).then_inc(cleared, 1)
                    dve.memset(kT[:, TOK:PADTOK], 0.0).then_inc(cleared, 1)
                    dve.memset(vT[:, TOK:PADTOK], 0.0).then_inc(cleared, 1)
                    dve.memset(S[:, 0, :], 0.0).then_inc(cleared, 1)
                    dve.wait_ge(cleared, 6)
                    dve.wait_ge(params_loaded, 112)
                    def conv(x):
                        u, c = ub[x], cv[x]
                        dve.wait_ge(tap_done, x + 1)
                        for j in range(1, 4):
                            for a, b, w in ((0, 0, SEQ), (3 + SEQ, SEQ, DEC)):
                                ins = dve.scalar_tensor_tensor(c[:, b:b + w], u[:, a + j:a + j + w],
                                                               cw[:, 4 * x + j:4 * x + j + 1], c[:, b:b + w],
                                                               ALU.mult, ALU.add)
                            if j == 3:
                                ins.then_inc(conv_done, 1)
                                dve.wait_ge(conv_done, x + 1)
                            else:
                                link(ins)

                    conv(0)
                    conv(1)
                    link(dve.tensor_tensor(Q4(E), Q4(Grow), gcol.unsqueeze(2).to_broadcast([P, NTILE, P]),
                                           ALU.subtract))
                    link(dve.tensor_tensor(kdc.unsqueeze(2), Q4(Grow)[:, :, P - 1:P], gcol.unsqueeze(2),
                                           ALU.subtract))
                    dve.tensor_scalar(E, E, 0.0, None, ALU.min).then_inc(decays, 1)
                    conv(2)
                    for x in range(2):
                        dve.wait_ge(act_took, 3 * (x + 1))
                        r = rt[x][:, 0:TOK]
                        link(dve.reciprocal(r, r))
                        dve.tensor_tensor(cv[x][:, 0:TOK], cv[x][:, 0:TOK], r, ALU.mult).then_inc(normed, 1)
                        dve.wait_ge(normed, x + 1)
                    for n, (t, c) in enumerate(G3):
                        dve.wait_ge(bank_ready, 7 + n)
                        dve.tensor_tensor(Q4(Vb)[:, t:t + c, :], Q4(ps[:, ring.bank(6 + n), 0:P * c]),
                                          bcol[:, t:t + c].unsqueeze(2).to_broadcast([P, c, P]), ALU.mult)\
                            .then_inc(dve_took, 1)
                    dve.wait_ge(exps, 4)
                    link(dve.tensor_tensor(Q4(E), Q4(E), incl.unsqueeze(1).to_broadcast([P, NTILE, P]), ALU.mult))
                    link(dve.tensor_copy(egl.unsqueeze(2), Q4(Grow)[:, :, P - 1:P]))
                    link(dve.scalar_tensor_tensor(nbg, bcol, -1.0, gcol, ALU.mult, ALU.mult))
                    for n, (t, c) in enumerate(G3):
                        dve.wait_ge(bank_ready, 10 + n)
                        dve.tensor_tensor(Q4(Kd)[:, t:t + c, :], Q4(ps[:, ring.bank(9 + n), 0:P * c]),
                                          kdc[:, t:t + c].unsqueeze(2).to_broadcast([P, c, P]), ALU.mult)\
                            .then_inc(dve_took, 1)
                    link(dve.tensor_tensor(Q4(brow), Q4(brow), strict.unsqueeze(1).to_broadcast([P, NTILE, P]),
                                           ALU.mult))
                    for x, dst in enumerate((LT, AT)):
                        for n, (t, c) in enumerate(G3):
                            e = 12 + 3 * x + n
                            dve.wait_ge(bank_ready, e + 1)
                            dve.tensor_tensor(Q4(dst)[:, t:t + c, :], Q4(ps[:, ring.bank(e), 0:P * c]),
                                              Q4(E)[:, t:t + c, :], ALU.mult).then_inc(dve_took, 1)
                    dve.wait_ge(dve_took, taken("dve", 17))
                    link(dve.tensor_tensor(LT, LT, brow, ALU.mult))
                    link(dve.tensor_tensor(Q4(XT), Q4(LT), masks[:, 6, :].unsqueeze(1).to_broadcast([P, NTILE, P]),
                                           ALU.mult))
                    link(dve.tensor_tensor(Q4(XT), ident.unsqueeze(1).to_broadcast([P, NTILE, P]), Q4(XT),
                                           ALU.subtract))
                    dve.transpose(X, XT).then_inc(level_x, 1)
                    dve.tensor_tensor(qT, qT, Grow, ALU.mult).then_inc(decays, 2)
                    for i in range(len(LEVELS)):
                        f = lev_first[i]
                        if i:
                            dve.wait_ge(bank_ready, lev_first[i - 1] + 3)
                        dve.tensor_tensor(Q4(LM), Q4(LT),
                                          masks[:, 7 + i, :].unsqueeze(1).to_broadcast([P, NTILE, P]),
                                          ALU.mult).then_inc(level_mask, 1)
                        last = i == len(LEVELS) - 1
                        for n, (t, c) in enumerate(G3):
                            e = f + 3 + (n if last else 2 * n)
                            dve.wait_ge(bank_ready, e + (1 if last else 2))
                            ins = dve.tensor_tensor(Q4(XT)[:, t:t + c, :], Q4(XT)[:, t:t + c, :],
                                                    Q4(ps[:, ring.bank(e), 0:P * c]), ALU.subtract)
                            ins.then_inc(dve_took, 1)
                            if not last:
                                ins = dve.tensor_tensor(Q4(X)[:, t:t + c, :], Q4(X)[:, t:t + c, :],
                                                        Q4(ps[:, ring.bank(e + 1), 0:P * c]), ALU.subtract)
                                ins.then_inc(dve_took, 1)
                        dve.wait_ge(dve_took, taken("dve", f + (5 if last else 8)))
                    for i, t in enumerate([8] + list(range(8))):
                        Ri, Ui = (b[:, P * (i % 4):P * (i % 4) + P] for b in (R, U))
                        dve.wait_ge(chain_pe, 3 * i + 1)
                        dve.scalar_tensor_tensor(Ri, ps[:, 0, 0:P], nbg[:, t:t + 1], Q4(Vb)[:, t, :],
                                                 ALU.mult, ALU.add).then_inc(rhs_ready, 1)
                        dve.wait_ge(chain_pe, 3 * i + 2)
                        if i >= 4:
                            dve.wait_ge(out_pe, i - 3)
                        dve.tensor_copy(Ui, ps[:, 1, 0:P]).then_inc(upd_ready, 1)
                        src = S[:, 2 if t == 8 else t % 2, :]
                        dst = S[:, 2 if t == 8 else (t + 1) % 2, :]
                        dve.wait_ge(chain_pe, 3 * i + 3)
                        if t == 8:
                            dve.wait_ge(out_pe, 1)
                        elif i >= 2:
                            dve.wait_ge(out_pe, i)
                        dve.scalar_tensor_tensor(dst, src, egl[:, t:t + 1], ps[:, 2, 0:P], ALU.mult, ALU.add)\
                            .then_inc(state_ready, 1)
                        dve.wait_ge(state_ready, i + 1)
                    finish_head(dve, link, taken("act", norm_first + 2), raw[:, 0:TOK], ro[:, 0:TOK], nw, zs)
            barrier()

        def merge(L, ph):
            NU = 24
            work = ph.enter_context(nc.sbuf_tensor("sb_merged", [P, KC * TOK + TOK], F32))
            mg = work[:, 0:KC * TOK].rearrange("p (k t) -> p k t", k=KC)
            os = ph.enter_context(nc.sbuf_tensor("sb_o_split", [P, 2, 4, TOK], F32R))
            wbs = ph.enter_context(nc.sbuf_tensor("sb_wb_split", [P, 2, 2, 4, P], F32R))
            extra = work[:, KC * TOK:KC * TOK + TOK]

            def gate(u, s):
                if u < 2:
                    return [(raw_qk[:, u, b:b + w], c, w) for b, c, w in RAW_SEGS[s]]
                a, w = SEGS[s]
                return [((raw_qk[:, 0], raw_qk[:, 1], extra)[u % 3][:, a:a + w], 0, w)]

            def wb_raw(u):
                return wraw[:, 4 + (u % 4) // 2, 4 * (u % 2):4 * (u % 2) + 4, :]

            def xbuf(j):
                return (raw_qk[:, 0, 0:TOK], raw_qk[:, 1, 0:TOK], extra)[j % 3]

            NBLK = 22 + KC
            first = L * N_BLOCKS + 47
            with nc.Block() as block:
                @block.sync
                def _(sp):
                    def load_o(n):
                        for k in range(4):
                            sp.dma_start(os[:, 1, k, :].bitcast(F32), do[4 * n + k]).then_inc(o_loaded, 16)

                    def load_wb(u):
                        sp.dma_start(wb_raw(u), row("wbr", L * NU + u)).then_inc(branch_loaded[u % 4], 16)

                    def load_block(b):
                        sp.dma_start(wraw[:, b % 4], row("wblk", first + b)).then_inc(slot_loaded[b % 4], 16)

                    def load_x(j):
                        sp.dma_start(xbuf(j), dx[j]).then_inc(x_loaded[j % 3], 16)

                    load_o(0)
                    for u in range(4):
                        load_wb(u)
                    load_block(4)
                    load_block(5)
                    for u in range(NU):
                        if u == NU - 2:
                            for j in range(3):
                                sp.wait_ge(merged, 3 * (14 + j))
                                load_x(j)
                        sp.wait_ge(split_ready, u + 1)
                        load_block(u + 6)
                        if u + 6 < NU:
                            if u == 0:
                                sp.wait_ge(branch_ready, 1)
                                load_wb(4)
                                sp.wait_ge(branch_ready, 2)
                                load_wb(5)
                            sp.wait_ge(branch_ready, u + 3)
                            load_wb(u + 6)
                        if u in (7, 15):
                            sp.wait_ge(bank_ready, 3 * (u + 1))
                            load_o((u + 1) // 8)
                    for j in range(KC):
                        sp.wait_ge(dve_took, 3 * (j + 1))
                        sp.dma_start(dx[j], xbuf(j)).then_inc(x_stored[j % 3], 16)
                        if j + 3 < KC:
                            sp.wait_ge(x_stored[j % 3], 16 * (j // 3 + 1))
                            load_x(j + 3)
                        if j == 5:
                            sp.wait_ge(split_ready, NBLK - 2)
                            for n in range(4):
                                sp.dma_start(wraw[:, n], row("adaw", L * 24 + 24 + n)).then_inc(params_loaded, 16)
                    for i in range(3):
                        sp.wait_ge(x_stored[i], 16 * len(range(i, KC, 3)))
                    sp.wait_ge(params_loaded, 64)

                @block.gpsimd
                def _(pool):
                    def split_wb(u):
                        pool.wait_ge(branch_loaded[u % 4], 16 * (u // 4 + 1))
                        pool.tensor_copy(wbs[:, u % 2, 0], wb_raw(u)).then_inc(branch_hi, 1)
                        pool.wait_ge(branch_hi, u + 1)
                        pool.tensor_tensor(wbs[:, u % 2, 1], wb_raw(u), wbs[:, u % 2, 0].bitcast(F32),
                                           ALU.subtract).then_inc(branch_ready, 1)

                    split_wb(0)
                    split_wb(1)
                    for b in range(2, NBLK):
                        if b < 24:
                            pool.wait_ge(proj_done, 3 * (b - 1))
                        else:
                            pool.wait_ge(bank_ready, 3 * NU + 3 * (b - 23))
                        if b >= 4:
                            pool.wait_ge(slot_loaded[b % 4], 16 * (b // 4))
                        split_block(pool, b % 4, b % 2, b - 1)
                        if b < NU:
                            pool.wait_ge(bank_ready, 3 * (b - 1))
                            split_wb(b)

                @block.tensor
                def _(pe):
                    for u in range(NU):
                        if u + 2 < NU:
                            if u >= 2:
                                pe.wait_ge(split_ready, u - 1)
                            for _ in project(pe, 3 * u, 0, 4, u % 2):
                                pass
                        pe.wait_ge(branch_ready, u + 1)
                        if u % 8 == 0:
                            pe.wait_ge(h_ready, 4 * (u // 8 + 1))
                        for s, (a, w) in enumerate(SEGS):
                            f = 3 * u + s
                            if f >= 4:
                                pe.wait_ge(scaled, f - 3)
                            for k in range(4):
                                mm = three(pe, ps[:, 4 + f % 4, 0:w], wbs[:, u % 2, 0, k, :],
                                           wbs[:, u % 2, 1, k, :], os[:, 0, k, a:a + w], os[:, 1, k, a:a + w],
                                           k == 0, k == 3)
                            mm.then_inc(bank_ready, 1)
                    for j in range(KC):
                        b = 22 + j
                        pe.wait_ge(split_ready, b - 1)
                        for s, (a, w) in enumerate(SEGS):
                            f = 3 * (NU + j) + s
                            m = f - 4
                            pe.wait_ge(*((scaled, m + 1) if m < 3 * NU else (dve_took, m + 1 - 3 * NU)))
                            for k in range(KC):
                                if j == 0 and s == 0:
                                    pe.wait_ge(normed, k + 1)
                                mm = three(pe, ps[:, 4 + f % 4, 0:w], ws[:, b % 2, 0, k, :],
                                           ws[:, b % 2, 1, k, :], hs[:, 0, k, a:a + w], hs[:, 1, k, a:a + w],
                                           k == 0, k == KC - 1)
                            mm.then_inc(bank_ready, 1)

                @block.scalar
                def _(act):
                    for u in range(2):
                        for s in range(3):
                            for dst, _, _ in gate(u, s):
                                ins = act.activation(dst, dst, ACT.Sigmoid)
                        ins.then_inc(probs, 1)
                    for u in range(NU):
                        if u % 8 == 0:
                            act.wait_ge(o_loaded, 64 * (u // 8 + 1))
                            for k in range(4):
                                act.activation(os[:, 0, k, :], os[:, 1, k, :].bitcast(F32), ACT.Copy)\
                                    .then_inc(h_hi, 1)
                        if u + 2 < NU:
                            if u:
                                act.wait_ge(scaled if u <= 8 else merged, 3 * u if u <= 8 else 3 * (u - 8))
                            for s in range(3):
                                take(act, 3 * u + s, 0, 4, gate(u + 2, s)[0][0], ACT.Sigmoid)
                    act.wait_ge(proj_done, 3 * 22)
                    for k in range(KC):
                        act.wait_ge(merged, 3 * (9 + k))
                        act.activation(hs[:, 0, k, :], mg[:, k, :], ACT.Copy).then_inc(level_x, 1)

                @block.vector
                def _(dve):
                    def low(k):
                        dve.wait_ge(level_x, k + 1)
                        dve.tensor_tensor(hs[:, 1, k, :], mg[:, k, :], hs[:, 0, k, :].bitcast(F32),
                                          ALU.subtract).then_inc(normed, 1)

                    for u in range(NU):
                        br, c = divmod(u, 8)
                        if c == 0:
                            for k in range(4):
                                dve.wait_ge(h_hi, 4 * br + k + 1)
                                dve.tensor_tensor(os[:, 1, k, :], os[:, 1, k, :].bitcast(F32),
                                                  os[:, 0, k, :].bitcast(F32), ALU.subtract).then_inc(h_ready, 1)
                        if u < 2:
                            dve.wait_ge(probs, u + 1)
                        for s, (a, w) in enumerate(SEGS):
                            f = 3 * u + s
                            if u >= 2:
                                dve.wait_ge(evacuated, 3 * (u - 2) + s + 1)
                            dve.wait_ge(bank_ready, f + 1)
                            for g_, b, n in gate(u, s):
                                ins = dve.tensor_tensor(g_ if br else mg[:, c, a + b:a + b + n],
                                                        ps[:, 4 + f % 4, b:b + n], g_, ALU.mult)
                            ins.then_inc(scaled, 1)
                            if br:
                                dve.wait_ge(scaled, f + 1)
                                dve.tensor_tensor(mg[:, c, a:a + w], mg[:, c, a:a + w], g_, ALU.add)\
                                    .then_inc(merged, 1)
                        if u == 21:
                            for k in range(6):
                                low(k)
                        elif u > 21:
                            low(u - 16)
                    for j in range(KC):
                        dve.wait_ge(x_loaded[j % 3], 16 * (j // 3 + 1))
                        for s, (a, w) in enumerate(SEGS):
                            f = 3 * (NU + j) + s
                            dve.wait_ge(bank_ready, f + 1)
                            for c, (_, b, n) in enumerate(RAW_SEGS[s]):
                                ins = dve.scalar_tensor_tensor(xbuf(j)[:, a + b:a + b + n],
                                                               ps[:, 4 + f % 4, b:b + n],
                                                               modT[:, 16 + j, c:c + 1],
                                                               xbuf(j)[:, a + b:a + b + n],
                                                               ALU.mult, ALU.add)
                            ins.then_inc(dve_took, 1)
            with nc.Block() as block:
                @block.vector
                def _(dve):
                    dve.memset(raw_qk[:, :, 0:3], 0.0)
            barrier()

        with nc.Fori(0, DEPTH) as L:
            with ExitStack() as ph:
                norm_phase(False, L, ph)
            with nc.Fori(0, 2) as g, ExitStack() as ph:
                retention_group(L, g, ph)
            with nc.Fori(0, 4) as g, ExitStack() as ph:
                fox_group(L, g, ph)
            with nc.Fori(0, 4) as g, ExitStack() as ph:
                delta_group(L, g, ph)
            with ExitStack() as ph:
                merge(L, ph)
        with ExitStack() as ph:
            norm_phase(True, None, ph)


OUTS = {
    "yT": (KC, P, TOK),
    "p_k": (8, P, SEQ), "p_v": (8, P, 8, P), "p_logf": (2, 8, SEQ), "p_ret": (4, P, P), "p_gdn": (8, P, P),
    "p_conv": (24, P, 3),
    "s_k": (8, P, DEC), "s_v": (8, DEC, P), "s_logf": (2, 8, DEC), "s_ret": (4, P, P), "s_gdn": (8, P, P),
    "s_conv": (24, P, 3),
}


def column_blocks():
    ret, fox, gdn, gates = 0, 1536, 3592, 5648
    own, qk = [], []
    for g in range(2):
        qk.append([ret + g * 128, ret + 256 + g * 128])
        own.append([ret + c + g * 256 for c in (512, 640, 1024, 1152)])
    for first in (fox, gdn):
        for g in range(4):
            qk.append([first + g * 128, first + 512 + g * 128])
            own.append([first + 1024 + g * 128, first + 1544 + g * 128])
    units = [gates + n * 1024 + d * 128 for n in range(3) for d in range(8)]
    qk.append(units[:2])
    cols = list(qk[0])
    for g, c in enumerate(own):
        cols += c + qk[g + 1]
    return cols + units[2:]


def kernel(**inputs):
    import concourse.bacc as _bacc
    from concourse.bass_utils import run_bass_kernel_spmd as _run

    a = {n: np.asarray(v) for n, v in inputs.items()}
    w_in = a["w_in"]

    def blocked(w):
        return w.reshape(KC, P, -1, P).transpose(2, 1, 0, 3)

    wsm = np.zeros((DEPTH, D, P), np.float32)
    wsm[:, :, 0:8] = w_in[:, :, 3072:3080]
    wsm[:, :, 32:36] = w_in[:, :, 5128:5132]
    wsm[:, :, 64:68] = w_in[:, :, 5132:5136]
    stream = [np.concatenate([blocked(wsm[l])] + [blocked(w_in[l][:, c:c + P]) for c in column_blocks()]
                             + [blocked(a["w_out"][l])]) for l in range(DEPTH)]
    gcols = np.zeros((DEPTH, 96, 4), np.float32)
    gcols[:, 0:8, 0] = a["fox_f_bias"]
    gcols[:, 32:36, 0] = a["gdn_dt_bias"]
    gcols[:, 32:36, 1] = a["gdn_a_log"]
    masks, rot, retc = shape_constants()
    x = np.concatenate([a["x_prompt"][0], a["x_sample"][0]])
    cvec = np.stack([a["c_prompt"][0], a["c_sample"][0]])
    conv_w = a["gdn_conv_w"].reshape(DEPTH, 4, 3, 4, P).transpose(0, 3, 4, 2, 1)
    hist = a["state_gdn_conv"].reshape(DEPTH, 3, 3, 4, P).transpose(0, 3, 2, 4, 1)
    arrays = {
        "xT": x.T.reshape(KC, P, TOK),
        "cT": cvec.T.reshape(KC, P, 2).transpose(1, 0, 2),
        "masks": masks, "rot": rot, "retc": retc,
        "wblk": np.concatenate(stream),
        "wbr": a["w_branch"].reshape(DEPTH, 3, 4, P, 8, P).transpose(0, 1, 4, 3, 2, 5).reshape(48, P, 4, P),
        "adaw": np.concatenate([blocked(a["ada_w"][l]) for l in range(DEPTH)] + [np.zeros((4, P, KC, P), np.float32)]),
        "adabT": a["ada_b"].reshape(DEPTH, 24, P).transpose(0, 2, 1),
        "nwT": a["norm_w"].reshape(DEPTH, KC, P).transpose(0, 2, 1),
        "fnwT": a["final_norm_w"].reshape(KC, P).T,
        "gcols": gcols,
        "lfc": a["cache_fox_logf"][:, 0],
        "rnwT": a["ret_norm_w"].reshape(DEPTH * 2, 2, P).transpose(0, 2, 1),
        "gnwT": a["gdn_norm_w"].reshape(DEPTH, P, 1),
        "sret": a["state_ret"].reshape(DEPTH * 2, P, P),
        "sgdn": a["state_gdn"].reshape(DEPTH * 4, P, P),
        "kcT": a["cache_fox_k"].reshape(DEPTH * 4, 2, PAST, 64).transpose(0, 1, 3, 2).reshape(8, P, PAST),
        "vc": a["cache_fox_v"].reshape(DEPTH * 4, 2, 4, P, 64).transpose(0, 3, 2, 1, 4).reshape(8, P, 4, P),
        "cwT": conv_w.reshape(8, P, 12),
        "hist": hist.reshape(24, P, 3),
    }
    arrays = {n: np.ascontiguousarray(v) for n, v in arrays.items()}
    nc = _bacc.Bacc("TRN2", target_bir_lowering=False, num_devices=1)
    A = {n: nc.dram_tensor("in_" + n, v.shape, F32, kind="ExternalInput").ap() for n, v in arrays.items()}
    O = {n: nc.dram_tensor("out_" + n, s, F32, kind="ExternalOutput").ap() for n, s in OUTS.items()}
    build(nc, A, O)
    r = _run(nc, [{"in_" + n: v for n, v in arrays.items()}], core_ids=[0])
    o = {n: np.asarray(r.results[0]["out_" + n]) for n in OUTS}
    y = o["yT"].reshape(D, TOK).T

    def heads_k(v, n):
        return v.reshape(DEPTH, 1, 8, 64, n).transpose(0, 1, 2, 4, 3)

    def conv(v):
        return v.reshape(DEPTH, 4, 3, P, 3).transpose(0, 4, 2, 1, 3).reshape(DEPTH, 1, 3, 1536)

    p_v = o["p_v"].reshape(DEPTH, 4, P, 8, 2, 64).transpose(0, 1, 4, 3, 2, 5).reshape(DEPTH, 1, 8, SEQ, 64)
    s_v = o["s_v"].reshape(DEPTH, 4, DEC, 2, 64).transpose(0, 1, 3, 2, 4).reshape(DEPTH, 1, 8, DEC, 64)
    out = (y[None, :SEQ], y[None, SEQ:],
           heads_k(o["p_k"], SEQ), p_v, o["p_logf"].reshape(DEPTH, 1, 8, SEQ),
           o["p_ret"].reshape(DEPTH, 1, 4, 64, P), o["p_gdn"].reshape(DEPTH, 1, 4, P, P), conv(o["p_conv"]),
           heads_k(o["s_k"], DEC), s_v, o["s_logf"].reshape(DEPTH, 1, 8, DEC),
           o["s_ret"].reshape(DEPTH, 1, 4, 64, P), o["s_gdn"].reshape(DEPTH, 1, 4, P, P), conv(o["s_conv"]))
    return tuple(np.ascontiguousarray(v) for v in out)
```

```python
from contextlib import ExitStack

import numpy as np
import concourse.bass as bass
from concourse import mybir

F32 = mybir.dt.float32
F32R = mybir.dt.float32r
ALU = mybir.AluOpType
ACT = mybir.ActivationFunctionType
AXX = mybir.AxisListType.X

P = 128
D = 1024
DEPTH = 2
SEQ = 1024
DEC = 64
PAST = 512
TOK = SEQ + DEC
NTILE = SEQ // P + 1
PADTOK = NTILE * P
SEGS = [(0, 364), (364, 364), (728, TOK - 728)]
STREAMS = [(0, 512), (512, 512), (SEQ, DEC)]
KC = D // P
EPS = 1e-6
N_BLOCKS = 77
FKEYS = SEQ + PAST + DEC
SCAN_OFF = SEQ + PAST
UW = 3 + SEQ + 3 + DEC
RAW = [(3, 512), (515, 512), (UW - DEC, DEC)]
PIECES = [(3, 0, SEQ), (UW - DEC, SEQ, DEC)]
RAW_SEGS = [[(3, 0, 364)], [(367, 0, 364)], [(731, 0, SEQ - 728), (UW - DEC, SEQ - 728, DEC)]]
LEVELS = [2, 4, 8, 16, 32, 64]
GAMMA = [1.0 - 2.0 ** (-5.0 - h) for h in range(4)]


def shape_constants():
    i = np.arange(P)
    ident = np.eye(P)
    future = np.where(i[:, None] > i[None, :], 1e30, 0.0)
    strict = (i[:, None] < i[None, :]).astype(float)
    lev = []
    for s in [1] + LEVELS:
        same = (i[:, None] // (2 * s)) == (i[None, :] // (2 * s))
        lev.append((same & ((i[:, None] // s) % 2 == 0) & ((i[None, :] // s) % 2 == 1)).astype(float))
    causal = np.where(i[None, :] > i[:, None], 1e30, 0.0)
    swap = np.zeros((P, P))
    for r in range(P):
        swap[(r // 64) * 64 + (r + 32) % 64, r] = 1.0
    masks = np.stack([ident, np.ones((P, P)), future, strict, causal, swap] + lev, axis=1)
    half = 32
    inv = np.float32(10000.0) ** (-np.arange(half, dtype=np.float32) / np.float32(half))
    pos = np.concatenate([np.arange(SEQ), PAST + np.arange(DEC)]).astype(np.float32)
    ang = (inv.astype(np.float32)[:, None] * pos[None, :]).astype(np.float32)
    cos = np.cos(ang.astype(np.float64))
    sin = np.sin(ang.astype(np.float64))
    rot = np.stack([np.tile(cos, (4, 1)), np.concatenate([-sin, sin, -sin, sin])], axis=1)
    ret = []
    for g in range(2):
        gam = GAMMA[2 * g:2 * g + 2]
        dist = np.abs(i[:, None] - i[None, :])
        seen = (i[:, None] // 64) <= (i[None, :] // 64)
        dt = np.concatenate([np.where(seen, 0.125 * x ** dist, 0.0) for x in gam], axis=1)
        per = np.repeat(gam, 64)
        dq = per[:, None] ** (i[None, :] + 1)
        kd = 0.125 * per[None, :] ** (P - 1 - i)[:, None]
        kds = 0.125 * per[None, :] ** np.maximum(DEC - 1 - i, 0)[:, None]
        dc = np.stack([per ** P, per ** DEC], axis=1)
        ret.append(np.concatenate([dt, dq, kd, kds, dc], axis=1))
    f = np.float32
    return masks.astype(f), rot.astype(f), np.stack(ret).astype(f)


RETC = 2 * P + P + 2 * P + 2


def build(nc, A, O):
    with ExitStack() as ctx:
        def sb(name, shape, dt=F32):
            return ctx.enter_context(nc.sbuf_tensor("sb_" + name, shape, dt))

        sems = []

        def sem(name):
            s = ctx.enter_context(nc.semaphore(name))
            sems.append(s)
            return s

        hs = sb("h_split", [P, 2, KC, TOK], F32R)
        ws = sb("w_split", [P, 2, 2, KC, P], F32R)
        wraw = sb("w_raw", [P, 6, KC, P])
        raw_qk = sb("raw_qk", [P, 2, UW])
        masks = sb("masks", [P, 13, P])
        cT = sb("cT", [P, KC, 2])
        consts = sb("consts", [P, 4])
        nwT = sb("nwT", [P, KC])
        adab = sb("adab", [P, 24])
        modT = sb("modT", [P, 24, 2])
        ident, ones, future, strict = (masks[:, m, :] for m in range(4))
        causal, swap = masks[:, 4, :], masks[:, 5, :]
        eps_c, l2_c, one_c = consts[:, 0:1], consts[:, 1:2], consts[:, 2:3]
        ps = ctx.enter_context(nc.psum_tensor("ps", [P, 8, 512], F32))

        def scratch(name, shape):
            return nc.dram_tensor("scratch_" + name, shape, F32, kind="Internal").ap()

        dx = scratch("x", (KC, P, TOK))
        do = scratch("o", (12, P, TOK))
        dfk = scratch("fcum", (8, FKEYS))
        dg = scratch("g", (4, PADTOK))
        db = scratch("beta", (4, PADTOK))

        slot_loaded = [sem(f"slot_loaded_{i}") for i in range(6)]
        branch_loaded = [sem(f"branch_loaded_{i}") for i in range(4)]
        x_loaded = [sem(f"x_loaded_{i}") for i in range(3)]
        x_stored = [sem(f"x_stored_{i}") for i in range(3)]
        params_loaded = sem("params_loaded")
        hist_loaded = sem("hist_loaded")
        o_loaded = sem("o_loaded")
        split_hi = sem("split_hi")
        split_ready = sem("split_ready")
        branch_hi = sem("branch_hi")
        branch_ready = sem("branch_ready")
        proj_done = sem("proj_done")
        evacuated = sem("evacuated")
        bank_ready = sem("bank_ready")
        act_took = sem("act_took")
        dve_took = sem("dve_took")
        stored = sem("stored")
        act_step = sem("act_step")
        dve_step = sem("dve_step")
        squares = sem("squares")
        squares_used = sem("squares_used")
        roots = sem("roots")
        inverse = sem("inverse")
        slot_used = sem("slot_used")
        h_scaled = sem("h_scaled")
        h_hi = sem("h_hi")
        h_ready = sem("h_ready")
        gates_raw = sem("gates_raw")
        tap_done = sem("tap_done")
        conv_done = sem("conv_done")
        silu_done = sem("silu_done")
        normed = sem("normed")
        decays = sem("decays")
        exps = sem("exps")
        level_mask = sem("level_mask")
        level_x = sem("level_x")
        state_ready = sem("state_ready")
        chain_pe = sem("chain_pe")
        rhs_ready = sem("rhs_ready")
        upd_ready = sem("upd_ready")
        out_pe = sem("out_pe")
        out_took = sem("out_took")
        out_done = sem("out_done")
        scores_pe = sem("scores_pe")
        beta_decay = sem("beta_decay")
        norm_sums = sem("norm_sums")
        logits = sem("logits")
        probs = sem("probs")
        merged = sem("merged")
        scaled = sem("scaled")
        gate_pe = sem("gate_pe")
        cleared = sem("cleared")
        nums = [s.num for s in sems]
        clear = range(min(nums), max(nums) + 1)
        assert len(clear) == len(sems)

        def barrier():
            nc.multi_engine_barrier(list(nc.engines), sems_to_clear=clear)

        def wait_own(eng, ins, count, s):
            count[0] += 1
            ins.then_inc(s, 1)
            eng.wait_ge(s, count[0])

        class Ring:
            def __init__(self, owners, first, banks):
                self.owners, self.first, self.banks = owners, first, banks

            def bank(self, n):
                return self.first + n % self.banks

            def acquire(self, pe, n):
                m = n - self.banks
                if m >= 0 and not isinstance(self.owners[m], str):
                    pe.wait_ge(*self.owners[m])
                elif m >= 0:
                    who = self.owners[m]
                    pe.wait_ge(act_took if who == "act" else dve_took,
                               sum(o == who for o in self.owners[:m + 1]))

        def three(pe, out, w_hi, w_lo, x_hi, x_lo, first, last):
            pe.matmul(out, w_hi, x_hi, start=first, stop=False)
            pe.matmul(out, w_hi, x_lo, start=False, stop=False)
            return pe.matmul(out, w_lo, x_hi, start=False, stop=last)

        def project(pe, e, first_bank, banks, slot):
            for s, (a, w) in enumerate(SEGS):
                if e + s >= banks:
                    pe.wait_ge(evacuated, e + s - banks + 1)
                for k in range(KC):
                    mm = three(pe, ps[:, first_bank + (e + s) % banks, 0:w], ws[:, slot, 0, k, :],
                               ws[:, slot, 1, k, :], hs[:, 0, k, a:a + w], hs[:, 1, k, a:a + w],
                               k == 0, k == KC - 1)
                    if k == KC - 1:
                        mm.then_inc(proj_done, 1)
                    yield

        def blocks(pe, todo, first_bank, banks):
            for e, b in todo:
                if b >= 2:
                    pe.wait_ge(split_ready, b - 1)
                yield from project(pe, e, first_bank, banks, b % 2)

        def turns(gen, n):
            for _ in range(n):
                next(gen, None)

        def take(act, e, first_bank, banks, dst, func=ACT.Copy):
            w = dst.shape[-1]
            act.wait_ge(proj_done, e + 1)
            act.activation(dst, ps[0:dst.shape[0], first_bank + e % banks, 0:w], func).then_inc(evacuated, 1)

        def take_into(act, e, s, first_bank, banks, buf):
            act.wait_ge(proj_done, e + 1)
            for u, c, w in RAW_SEGS[s]:
                ins = act.activation(buf[:, u:u + w], ps[:, first_bank + e % banks, c:c + w], ACT.Copy)
            ins.then_inc(evacuated, 1)

        def take_raw(act, e, e0, first_bank, banks):
            x, s = divmod(e - e0, 3)
            take_into(act, e, s, first_bank, banks, raw_qk[:, x, :])

        def split_block(pool, slot, to, n):
            pool.tensor_copy(ws[:, to, 0], wraw[:, slot]).then_inc(split_hi, 1)
            pool.wait_ge(split_hi, n)
            pool.tensor_tensor(ws[:, to, 1], wraw[:, slot], ws[:, to, 0].bitcast(F32), ALU.subtract)\
                .then_inc(split_ready, 1)

        def split_blocks(pool, last_entry):
            nb = len(last_entry)
            for b in range(2, nb + 2):
                pool.wait_ge(proj_done, last_entry[b - 2])
                if b >= nb:
                    pool.wait_ge(slot_loaded[b - nb], 16)
                split_block(pool, b % nb, b % 2, b - 1)

        def reload_weights(sp, base, count):
            for i in range(count):
                if i >= 2:
                    sp.wait_ge(split_ready, i - 1)
                sp.dma_start(wraw[:, i], row("wblk", base + i)).then_inc(slot_loaded[i], 16)

        def all_loaded(sp, count):
            for i in range(count):
                sp.wait_ge(slot_loaded[i], 16)

        def sum_features(pe, ring, n, sq):
            for s, (a, w) in enumerate(SEGS):
                ring.acquire(pe, n + s)
                pe.matmul(ps[:, ring.bank(n + s), 0:w], ones, sq[:, a:a + w],
                          start=True, stop=True).then_inc(bank_ready, 1)

        def row(name, idx):
            ap = A[name] if name in A else O[name]
            dims = " ".join("bcdef"[:len(ap.shape) - 2])
            return ap[bass.ds(idx, 1)].rearrange(f"a p {dims} -> (a p) {dims}" if dims else "a p -> (a p)")

        def Q4(ap):
            return ap.rearrange("p (t c) -> p t c", c=P)

        def tiles_of(mask):
            return mask.unsqueeze(1).to_broadcast([P, NTILE, P])

        G3 = [(0, 4), (4, 4), (8, 1)]

        with nc.Block() as block:
            @block.sync
            def _(sp):
                sp.dma_start(masks[:, :, :], A["masks"]).then_inc(params_loaded, 16)
                sp.dma_start(cT[:, :, :], A["cT"]).then_inc(params_loaded, 16)
                sp.dma_start(dx, A["xT"]).then_inc(stored, 16)
                for n in range(4):
                    sp.dma_start(wraw[:, n], A["adaw"][n]).then_inc(params_loaded, 16)
                sp.wait_ge(stored, 16)
                sp.wait_ge(params_loaded, 96)

            @block.scalar
            def _(act):
                act.wait_ge(params_loaded, 96)
                act.activation(cT[:, :, :], cT[:, :, :], ACT.Silu)

            @block.vector
            def _(dve):
                dve.memset(eps_c, EPS)
                dve.memset(l2_c, EPS * P)
                dve.memset(one_c, 1.0)
                dve.memset(raw_qk[:, :, 0:3], 0.0)
        barrier()

        def norm_phase(final, L, ph):
            work = ph.enter_context(nc.sbuf_tensor("sb_norm_" + ("last" if final else "layer"), [P, 14500], F32))
            x = work[:, 0:KC * TOK].rearrange("p (k t) -> p k t", k=KC)
            at = KC * TOK
            sq = work[:, at:at + 2 * TOK].rearrange("p (b t) -> p b t", b=2)
            mrow = work[0:2, at:at + 2 * D]
            at += 2 * TOK
            rstd = work[:, at:at + TOK]
            at += TOK
            lfx = work[0:8, at:at + FKEYS]
            at += FKEYS
            gcols, scw = work[0:96, at:at + 4], work[:, at + 4:at + 20].rearrange("p (k c) -> p k c", k=KC)
            gz, ga, gl, gre = (work[0:96, i * PADTOK:(i + 1) * PADTOK] for i in range(4))
            fre = work[0:8, 4 * PADTOK:4 * PADTOK + FKEYS]
            NADA = 16
            ada = None if final else ph.enter_context(nc.sbuf_tensor("sb_ada", [P, 6, KC, P], F32))
            with nc.Block() as block:
                @block.sync
                def _(sp):
                    for c in range(4):
                        sp.dma_start(x[:, 2 * c:2 * c + 2, :], dx[2 * c:2 * c + 2].rearrange("k p t -> p k t"))\
                            .then_inc(branch_loaded[c], 16)
                    if final:
                        sp.dma_start(nwT[:, :], A["fnwT"]).then_inc(params_loaded, 16)
                        for k in range(KC):
                            sp.wait_ge(out_done, k + 1)
                            sp.dma_start(O["yT"][k], x[:, k, :]).then_inc(stored, 16)
                        sp.wait_ge(stored, 16 * KC)
                        return
                    sp.dma_start(nwT[:, :], row("nwT", L)).then_inc(params_loaded, 16)
                    sp.dma_start(adab[:, :], row("adabT", L)).then_inc(params_loaded, 16)
                    sp.dma_start(gcols, row("gcols", L)).then_inc(params_loaded, 16)
                    sp.dma_start(lfx[:, SEQ:SEQ + PAST], row("lfc", L)).then_inc(params_loaded, 16)
                    sp.dma_start(wraw[:, 4], row("wblk", L * N_BLOCKS)).then_inc(slot_loaded[4], 16)
                    sp.dma_start(wraw[:, 5], row("wblk", L * N_BLOCKS + 1)).then_inc(slot_loaded[5], 16)
                    def load_ada(first, count, to, s):
                        sp.dma_start(ada[:, to:to + count], A["adaw"][bass.ds(L * 24 + first, count)]
                                     .rearrange("b p k c -> p b k c")).then_inc(s, 16)

                    load_ada(4, 3, 0, x_loaded[0])
                    load_ada(7, 3, 3, x_loaded[1])
                    sp.wait_ge(slot_used, 4)
                    for i in range(4):
                        sp.dma_start(wraw[:, i], row("adaw", L * 24 + 10 + i)).then_inc(slot_loaded[i], 16)
                    sp.wait_ge(slot_used, 8)
                    load_ada(14, 2, 0, x_loaded[2])
                    sp.wait_ge(split_ready, 1)
                    sp.dma_start(wraw[:, 4], row("wblk", L * N_BLOCKS + 2)).then_inc(slot_loaded[4], 16)
                    for i in range(4):
                        sp.wait_ge(slot_used, 12 + i // 2 * 2)
                        sp.dma_start(wraw[:, i], row("wblk", L * N_BLOCKS + 3 + i)).then_inc(slot_loaded[i], 16)
                    sp.wait_ge(split_ready, 2)
                    sp.dma_start(wraw[:, 5], row("wblk", L * N_BLOCKS + 8)).then_inc(slot_loaded[5], 16)
                    sp.wait_ge(split_ready, 3)
                    sp.dma_start(wraw[:, 4], row("wblk", L * N_BLOCKS + 7)).then_inc(slot_loaded[4], 16)
                    sp.wait_ge(decays, 1)
                    sp.dma_start(row("p_logf", L), lfx[:, 0:SEQ]).then_inc(stored, 16)
                    sp.dma_start(row("s_logf", L), lfx[:, SCAN_OFF:FKEYS]).then_inc(stored, 16)
                    sp.wait_ge(decays, 2)
                    sp.dma_start(dfk, fre).then_inc(stored, 16)
                    sp.wait_ge(exps, 1)
                    sp.dma_start(db, gz[64:68, :]).then_inc(stored, 16)
                    sp.wait_ge(decays, 3)
                    sp.dma_start(dg, ga[32:36, :]).then_inc(stored, 16)
                    sp.wait_ge(stored, 80)
                    for i in range(4):
                        sp.wait_ge(slot_loaded[i], 32)
                    sp.wait_ge(slot_loaded[4], 48)
                    sp.wait_ge(slot_loaded[5], 32)

                @block.gpsimd
                def _(pool):
                    if final:
                        return
                    pool.wait_ge(slot_loaded[4], 16)
                    split_block(pool, 4, 1, 1)
                    pool.wait_ge(slot_loaded[5], 16)
                    split_block(pool, 5, 0, 2)
                    pool.wait_ge(slot_loaded[4], 32)
                    pool.wait_ge(gate_pe, 3)
                    split_block(pool, 4, 1, 3)
                    for i in range(2):
                        pool.wait_ge(slot_loaded[i], 32)
                        pool.wait_ge(proj_done, 3 * (i + 1))
                        split_block(pool, i, i, 4 + i)

                @block.tensor
                def _(pe):
                    def modulation(n, count):
                        if n < 4 or 10 <= n < 14:
                            w_ = wraw[:, n % 10:n % 10 + count]
                        else:
                            w_ = ada[:, (n - 4) % 10:(n - 4) % 10 + count]
                        at_ = P * (n % 4)
                        for k in range(KC):
                            mm = pe.matmul(ps[0:2, 3 + n // 4, at_:at_ + P * count], cT[:, k, :],
                                           w_[:, :, k, :], start=(k == 0), stop=(k == KC - 1))
                        mm.then_inc(slot_used, count)

                    if not final:
                        modulation(0, 4)
                    for k in range(KC):
                        pe.wait_ge(squares, k + 1)
                        for s, (a, w) in enumerate(SEGS):
                            mm = pe.matmul(ps[:, s, 0:w], ones, sq[:, k % 2, a:a + w],
                                           start=(k == 0), stop=(k == KC - 1))
                        mm.then_inc(squares_used, 1)
                    if final:
                        return
                    pe.wait_ge(x_loaded[0], 16)
                    pe.wait_ge(x_loaded[1], 16)
                    modulation(4, 4)
                    modulation(8, 2)
                    for n in (10, 12):
                        pe.wait_ge(slot_loaded[n - 10], 16)
                        pe.wait_ge(slot_loaded[n - 9], 16)
                        modulation(n, 2)
                    pe.wait_ge(x_loaded[2], 16)
                    modulation(14, 2)
                    for n in range(NADA):
                        if n % 4 == 0:
                            pe.wait_ge(upd_ready, n // 4 + 1)
                        mm = pe.transpose(ps[:, 7, 2 * n:2 * n + 2], mrow[:, P * n:P * n + P], ident[0:2, 0:2])
                    mm.then_inc(chain_pe, 1)
                    pe.wait_ge(split_ready, 1)
                    pe.wait_ge(roots, 3)
                    for s, (a, w) in enumerate(SEGS):
                        for k in range(KC):
                            if s == 0:
                                pe.wait_ge(*((level_x, k // 2 + 1) if k % 2 else (h_ready, k // 2 + 1)))
                            mm = three(pe, ps[:, s, 0:w], ws[:, 1, 0, k, :], ws[:, 1, 1, k, :],
                                       hs[:, 0, k, a:a + w], hs[:, 1, k, a:a + w], k == 0, k == KC - 1)
                        mm.then_inc(gate_pe, 1)
                    for x_ in range(2):
                        pe.wait_ge(split_ready, 2 + x_)
                        for _ in project(pe, 3 * x_, 4, 4, x_):
                            pass

                @block.scalar
                def _(act):
                    for k in range(KC):
                        if k % 2 == 0:
                            act.wait_ge(branch_loaded[k // 2], 16)
                        if k >= 2:
                            act.wait_ge(squares_used, k - 1)
                        act.activation(sq[:, k % 2, :], x[:, k, :], ACT.Square).then_inc(squares, 1)
                    act.wait_ge(squares_used, KC)
                    for s, (a, w) in enumerate(SEGS):
                        act.activation(rstd[:, a:a + w], ps[:, s, 0:w], ACT.Ln, bias=eps_c,
                                       scale=1.0 / D).then_inc(roots, 1)
                    act.wait_ge(roots, 3)
                    act.activation(rstd, rstd, ACT.Exp, scale=-0.5).then_inc(inverse, 1)
                    if final:
                        return
                    for i in range(4):
                        act.wait_ge(slot_used, 4 * (i + 1))
                        act.activation(mrow[:, 512 * i:512 * i + 512], ps[0:2, 3 + i, :], ACT.Copy)\
                            .then_inc(upd_ready, 1)
                    act.wait_ge(scaled, 2)
                    def low_part(k):
                        act.wait_ge(conv_done, k // 2 + 1)
                        for c, (a, w) in enumerate(((0, SEQ), (SEQ, DEC))):
                            ins = act.activation(hs[:, 1, k, a:a + w], x[:, k, a:a + w], ACT.Identity,
                                                 bias=modT[:, k, c:c + 1])
                        ins.then_inc(level_x, 1)

                    for k in range(KC):
                        if k in (3, 5, 7):
                            low_part(k - 2)
                        act.wait_ge(h_scaled, k + 1)
                        for c, (a, w) in enumerate(((0, SEQ), (SEQ, DEC))):
                            ins = act.activation(hs[:, 0, k, a:a + w], x[:, k, a:a + w], ACT.Identity,
                                                 bias=modT[:, k, c:c + 1], scale=scw[:, k, c:c + 1])
                        ins.then_inc(h_hi, 1)
                    low_part(7)
                    act.wait_ge(params_loaded, 64)
                    act.activation(gcols[:, 2:3], gcols[:, 1:2], ACT.Exp).then_inc(act_step, 1)
                    act.wait_ge(gates_raw, 4)
                    act.activation(gl, ga, ACT.Exp, scale=-1.0).then_inc(act_step, 1)
                    act.wait_ge(act_step, 2)
                    act.activation(gl, gl, ACT.Ln, bias=one_c[0:96]).then_inc(act_took, 1)
                    for e in range(3):
                        take_raw(act, e, 0, 4, 4)
                    act.wait_ge(conv_done, 5)
                    act.activation(gz[64:68, 0:TOK], gl[64:68, 0:TOK], ACT.Exp).then_inc(exps, 1)
                    for e in range(3, 6):
                        take_raw(act, e, 0, 4, 4)

                @block.vector
                def _(dve):
                    st = [0]

                    def link(ins):
                        wait_own(dve, ins, st, dve_step)
                    dve.wait_ge(inverse, 1)
                    if final:
                        dve.wait_ge(params_loaded, 16)
                        for k in range(KC):
                            dve.scalar_tensor_tensor(x[:, k, :], x[:, k, :], nwT[:, k:k + 1], rstd,
                                                     ALU.mult, ALU.mult).then_inc(out_done, 1)
                        return
                    for k in range(KC):
                        dve.tensor_tensor(x[:, k, :], x[:, k, :], rstd, ALU.mult).then_inc(h_scaled, 1)
                    dve.wait_ge(params_loaded, 64)
                    dve.wait_ge(chain_pe, 1)
                    dve.tensor_tensor(modT[:, 0:16, :], ps[:, 7, 0:32].rearrange("p (n c) -> p n c", c=2),
                                      adab[:, 0:16].unsqueeze(2).to_broadcast([P, 16, 2]), ALU.add)\
                        .then_inc(scaled, 1)
                    dve.wait_ge(scaled, 1)
                    link(dve.tensor_scalar(scw, modT[:, 8:16, :], 1.0, None, ALU.add))
                    dve.tensor_tensor(scw, scw, nwT[:, :].unsqueeze(2).to_broadcast([P, KC, 2]),
                                      ALU.mult).then_inc(scaled, 1)
                    dve.wait_ge(scaled, 2)
                    for k in range(KC):
                        dve.wait_ge(h_hi, k + 1)
                        for c, (a, w) in enumerate(((0, SEQ), (SEQ, DEC))):
                            ins = dve.scalar_tensor_tensor(x[:, k, a:a + w], x[:, k, a:a + w],
                                                           scw[:, k, c:c + 1],
                                                           hs[:, 0, k, a:a + w].bitcast(F32),
                                                           ALU.mult, ALU.subtract)
                        if k % 2:
                            ins.then_inc(conv_done, 1)
                            continue
                        link(ins)
                        for c, (a, w) in enumerate(((0, SEQ), (SEQ, DEC))):
                            ins = dve.tensor_scalar(hs[:, 1, k, a:a + w], x[:, k, a:a + w],
                                                    modT[:, k, c:c + 1], None, ALU.add)
                        ins.then_inc(h_ready, 1)
                    dve.wait_ge(level_x, KC // 2)
                    dve.memset(ga[:, TOK:PADTOK], 0.0)
                    link(dve.memset(gz[:, TOK:PADTOK], 0.0))
                    for s, (a, w) in enumerate(SEGS):
                        dve.wait_ge(gate_pe, s + 1)
                        dve.tensor_scalar(gz[:, a:a + w], ps[0:96, s, 0:w], gcols[:, 0:1], None,
                                          ALU.add).then_inc(gates_raw, 1)
                    dve.wait_ge(gates_raw, 3)
                    dve.scalar_tensor_tensor(ga, gz, -1.0, gz, ALU.mult, ALU.max).then_inc(gates_raw, 1)
                    dve.memset(gre, 1.0).then_inc(cleared, 1)
                    dve.wait_ge(cleared, 1)
                    link(dve.memset(Q4(gre)[:, :, 0:1], 0.0))
                    link(dve.memset(fre, 1.0))
                    link(dve.memset(fre[:, SEQ:SEQ + 1], 0.0))
                    dve.wait_ge(act_took, 1)
                    dve.wait_ge(act_step, 2)
                    link(dve.scalar_tensor_tensor(ga, gz, 0.0, gl, ALU.max, ALU.add))
                    link(dve.tensor_scalar(ga, ga, gcols[:, 2:3], -1.0, ALU.mult, ALU.mult))
                    dve.scalar_tensor_tensor(gl, gz, 0.0, gl, ALU.min, ALU.subtract).then_inc(conv_done, 1)
                    dve.wait_ge(conv_done, 5)
                    link(dve.memset(ga[:, TOK:PADTOK], 0.0))
                    dve.tensor_copy(lfx[:, 0:SEQ], gl[0:8, 0:SEQ])
                    dve.tensor_copy(lfx[:, SCAN_OFF:FKEYS], gl[0:8, SEQ:TOK]).then_inc(decays, 1)
                    dve.wait_ge(decays, 1)
                    link(dve.tensor_tensor_scan(fre, fre, lfx, 0.0, ALU.mult, ALU.add))
                    dve.tensor_scalar(fre, fre, 8.0, None, ALU.mult).then_inc(decays, 1)
                    dve.tensor_tensor_scan(ga[32:36, :], gre[32:36, :], ga[32:36, :], 0.0, ALU.mult,
                                           ALU.add).then_inc(decays, 1)
            barrier()

        def finish_head(dve, link, need, raw, r, w_col, z):
            dve.wait_ge(inverse, need)
            link(dve.scalar_tensor_tensor(raw, raw, w_col, r, ALU.mult, ALU.mult))
            dve.tensor_tensor(z, z, raw, ALU.mult).then_inc(out_done, 1)

        def retention_group(L, g, ph):
            work = ph.enter_context(nc.sbuf_tensor("sb_ret", [P, 13 * PADTOK + 11 * P + RETC + 8 + 4096], F32))

            def slab(i):
                return work[:, i * PADTOK:(i + 1) * PADTOK]
            q, k_, V = slab(0), slab(1), work[:, 2 * PADTOK:4 * PADTOK].rearrange("p (t c) -> p t c", c=2 * P)
            cos, sin, tmp, Kd = slab(4)[:, 0:TOK], slab(5)[:, 0:TOK], slab(6), slab(7)
            AT = [slab(8), slab(9)]
            raw, sq, r = [slab(4), slab(5)], slab(6), [slab(7), slab(8)]
            zs = [slab(10)[:, 0:TOK], slab(11)[:, 0:TOK]]
            mrow = slab(12)[0:2, 0:4 * P]
            base = 13 * PADTOK
            S = work[:, base:base + 11 * P].rearrange("p (t c) -> p t c", c=P)
            base += 11 * P
            rc = work[:, base:base + RETC]
            DT = [rc[:, 0:P], rc[:, P:2 * P]]
            dq, kd = rc[:, 2 * P:3 * P], rc[:, 3 * P:5 * P]
            dc = rc[:, 5 * P:5 * P + 2]
            base += RETC
            nw = work[:, base:base + 2]
            ada = work[:, base + 8:base + 8 + 4096].rearrange("p (b k c) -> p b k c", b=4, k=KC)
            gi = L * 2 + g
            VN = [(0, 2), (2, 2), (4, 2), (6, 2), (8, 1)]
            OUT, NORM = [[19, 20, 21], [22, 26, 27]], [23, 28]
            owners = (["dve"] * 16 + [(state_ready, 4), (state_ready, 8), (state_ready, 9)]
                      + ["act"] * 12)
            ring = Ring(owners, 0, 5)
            B0, NB = 5, 3
            with nc.Block() as block:
                @block.sync
                def _(sp):
                    sp.dma_start(cos, A["rot"][:, 0, :]).then_inc(params_loaded, 16)
                    sp.dma_start(sin, A["rot"][:, 1, :]).then_inc(params_loaded, 16)
                    sp.dma_start(rc, row("retc", g)).then_inc(params_loaded, 16)
                    sp.dma_start(nw, row("rnwT", gi)).then_inc(params_loaded, 16)
                    sp.dma_start(S[:, 9, :], row("sret", gi)).then_inc(params_loaded, 16)
                    for n in range(4):
                        sp.dma_start(ada[:, n], row("adaw", L * 24 + 16 + 4 * g + n)).then_inc(o_loaded, 16)
                    reload_weights(sp, L * N_BLOCKS + 3 + g * 6 + 6, 6)
                    sp.wait_ge(state_ready, 9)
                    sp.dma_start(row("p_ret", gi), S[:, 8, :]).then_inc(stored, 16)
                    sp.dma_start(row("s_ret", gi), S[:, 10, :]).then_inc(stored, 16)
                    for h in range(2):
                        sp.wait_ge(out_done, (1, 4)[h])
                        sp.dma_start(do[bass.ds(2 * g + h, 1)].rearrange("a p t -> (a p) t"), zs[h])\
                            .then_inc(stored, 16)
                    sp.wait_ge(stored, 64)
                    all_loaded(sp, 6)

                @block.gpsimd
                def _(pool):
                    split_blocks(pool, [5, 5, 8, 11, 14, 17])

                @block.tensor
                def _(pe):
                    for x in range(2):
                        for s, (a, w) in enumerate(STREAMS):
                            ring.acquire(pe, 3 * x + s)
                            pe.matmul(ps[:, ring.bank(3 * x + s), 0:w], swap,
                                      raw_qk[:, x, RAW[s][0]:RAW[s][0] + w],
                                      start=True, stop=True).then_inc(bank_ready, 1)
                    for e, (t, c) in enumerate(VN):
                        if e >= NB:
                            pe.wait_ge(evacuated, e - NB + 1)
                        for j in range(c):
                            a = (t + j) * P if t + j < 8 else TOK - P
                            for k in range(KC):
                                mm = three(pe, ps[:, B0 + e % NB, 256 * j:256 * j + 256],
                                           hs[:, 0, k, a:a + P], hs[:, 1, k, a:a + P],
                                           ws[:, 0:2, 0, k, :], ws[:, 0:2, 1, k, :], k == 0, k == KC - 1)
                        mm.then_inc(proj_done, 1)
                    fill = blocks(pe, [(5, 2), (8, 3), (11, 4), (14, 5)], B0, NB)
                    pe.wait_ge(o_loaded, 64)
                    ring.acquire(pe, 6)
                    for k in range(KC):
                        mm = pe.matmul(ps[0:2, ring.bank(6), :], cT[:, k, :], ada[:, :, k, :],
                                       start=(k == 0), stop=(k == KC - 1))
                    mm.then_inc(gate_pe, 1)
                    pe.wait_ge(gates_raw, 1)
                    for n in range(4):
                        mm = pe.transpose(ps[:, ring.bank(6), 2 * n:2 * n + 2], mrow[:, P * n:P * n + P],
                                          ident[0:2, 0:2])
                    mm.then_inc(bank_ready, 1)
                    pe.wait_ge(normed, 2)
                    for n, (t, c) in enumerate(G3):
                        ring.acquire(pe, 7 + n)
                        for j in range(c):
                            mm = pe.transpose(ps[:, ring.bank(7 + n), P * j:P * j + P],
                                              Q4(k_)[:, t + j, :], ident)
                        mm.then_inc(bank_ready, 1)
                        turns(fill, 4)
                    for h in range(2):
                        for n, (t, c) in enumerate(G3):
                            e = 10 + 3 * h + n
                            ring.acquire(pe, e)
                            for j in range(c):
                                mm = pe.matmul(ps[:, ring.bank(e), P * j:P * j + P],
                                               Q4(k_)[64 * h:64 * h + 64, t + j, :],
                                               Q4(q)[64 * h:64 * h + 64, t + j, :], start=True, stop=True)
                            mm.then_inc(bank_ready, 1)
                            turns(fill, 4)
                    pe.wait_ge(dve_took, 10)
                    pe.wait_ge(evacuated, 5)
                    pe.wait_ge(cleared, 2)
                    for n, (t, c) in enumerate(G3):
                        ring.acquire(pe, 16 + n)
                        for j in range(c):
                            for h in range(2):
                                mm = pe.matmul(ps[64 * h:64 * h + 64, ring.bank(16 + n), P * j:P * j + P],
                                               Q4(Kd)[:, t + j, 64 * h:64 * h + 64],
                                               V[:, t + j, P * h:P * h + P], start=True, stop=True)
                        mm.then_inc(bank_ready, 1)
                        turns(fill, 5)
                    def output(h, n):
                        (t, c), e = G3[n], OUT[h][n]
                        ring.acquire(pe, e)
                        pe.wait_ge(state_ready, t + c - 1 if t < 8 else 8)
                        for j in range(c):
                            tt = t + j
                            out = ps[:, ring.bank(e), P * j:P * j + P]
                            mm = pe.matmul(out, V[:, tt, P * h:P * h + P], Q4(AT[h])[:, tt, :],
                                           start=True, stop=(tt == 0))
                            if tt:
                                mm = pe.matmul(out, S[64 * h:64 * h + 64, 9 if tt == 8 else tt, :],
                                               Q4(q)[64 * h:64 * h + 64, tt, :], start=False, stop=True)
                        mm.then_inc(bank_ready, 1)

                    def norm_sum(h, s):
                        a, w = SEGS[s]
                        e = NORM[h] + s
                        ring.acquire(pe, e)
                        pe.matmul(ps[:, ring.bank(e), 0:w], ones, sq[:, a:a + w],
                                  start=True, stop=True).then_inc(bank_ready, 1)

                    pe.wait_ge(dve_took, 16)
                    pe.wait_ge(conv_done, 1)
                    for n in range(3):
                        output(0, n)
                        turns(fill, 5)
                    output(1, 0)
                    turns(fill, 5)
                    pe.wait_ge(squares, 1)
                    for s in range(3):
                        norm_sum(0, s)
                        turns(fill, 5)
                    for n in (1, 2):
                        output(1, n)
                        turns(fill, 5)
                    pe.wait_ge(squares, 2)
                    for s in range(3):
                        norm_sum(1, s)

                @block.scalar
                def _(act):
                    for e, (t, c) in enumerate(VN):
                        act.wait_ge(proj_done, e + 1)
                        lo = 0 if t < 8 else DEC
                        act.activation(V[0:P - lo, t:t + c, :],
                                       ps[lo:P, B0 + e % NB, 0:256 * c].rearrange("p (t c) -> p t c", t=c),
                                       ACT.Copy).then_inc(evacuated, 1)

                    def taken(m):
                        if m < 6:
                            a, w = SEGS[m % 3]
                            take(act, 5 + m, B0, NB, zs[m // 3][:, a:a + w], ACT.Silu)
                        else:
                            take_raw(act, 5 + m, 11, B0, NB)

                    def copy_out(h, n):
                        (t, c), e = G3[n], OUT[h][n]
                        act.wait_ge(bank_ready, e + 1)
                        act.activation(Q4(raw[h])[:, t:t + c, :], Q4(ps[:, ring.bank(e), 0:P * c]),
                                       ACT.Copy).then_inc(act_took, 1)

                    def root(h, s):
                        (a, w), e = SEGS[s], NORM[h] + s
                        act.wait_ge(bank_ready, e + 1)
                        act.activation(r[h][:, a:a + w], ps[:, ring.bank(e), 0:w], ACT.Ln, bias=eps_c,
                                       scale=1.0 / P).then_inc(act_took, 1)

                    def invert(h, a, w, own):
                        act.wait_ge(act_took, own)
                        act.activation(r[h][:, a:a + w], r[h][:, a:a + w], ACT.Exp, scale=-0.5)\
                            .then_inc(inverse, 1)

                    def square(h):
                        act.wait_ge(act_took, 3 if h == 0 else 9)
                        act.activation(sq, raw[h], ACT.Square).then_inc(squares, 1)

                    for m in range(6):
                        taken(m)
                    act.wait_ge(normed, 2)
                    copy_out(0, 0)
                    taken(6)
                    copy_out(0, 1)
                    copy_out(0, 2)
                    square(0)
                    taken(7)
                    copy_out(1, 0)
                    root(0, 0)
                    taken(8)
                    root(0, 1)
                    root(0, 2)
                    invert(0, 0, TOK, 7)
                    taken(9)
                    copy_out(1, 1)
                    taken(10)
                    copy_out(1, 2)
                    square(1)
                    for s in range(3):
                        root(1, s)
                    for s, (a, w) in enumerate(SEGS):
                        invert(1, a, w, 10 + s)
                    taken(11)

                @block.vector
                def _(dve):
                    st = [0]

                    def link(ins):
                        wait_own(dve, ins, st, dve_step)
                    dve.memset(V[64:128, 8, :], 0.0).then_inc(cleared, 1)
                    link(dve.memset(q[:, TOK:PADTOK], 0.0))
                    dve.memset(k_[:, TOK:PADTOK], 0.0).then_inc(cleared, 1)
                    dve.wait_ge(params_loaded, 80)
                    for x, dst in enumerate((q, k_)):
                        for s, (a, w) in enumerate(STREAMS):
                            dve.wait_ge(bank_ready, 1 + 3 * x + s)
                            dve.tensor_tensor(tmp[:, a:a + w], ps[:, ring.bank(3 * x + s), 0:w],
                                              sin[:, a:a + w], ALU.mult).then_inc(dve_took, 1)
                        for u, a, w in PIECES:
                            link(dve.tensor_tensor(dst[:, a:a + w], raw_qk[:, x, u:u + w], cos[:, a:a + w],
                                                   ALU.mult))
                        dve.wait_ge(dve_took, 3 * (x + 1))
                        dve.tensor_tensor(dst[:, 0:TOK], dst[:, 0:TOK], tmp[:, 0:TOK], ALU.add)\
                            .then_inc(normed, 1)
                        dve.wait_ge(normed, x + 1)
                    dve.wait_ge(gate_pe, 1)
                    dve.tensor_copy(mrow, ps[0:2, ring.bank(6), :]).then_inc(gates_raw, 1)
                    dve.wait_ge(bank_ready, 7)
                    dve.tensor_tensor(modT[:, bass.ds(16 + 4 * g, 4), :],
                                      ps[:, ring.bank(6), 0:8].rearrange("p (n c) -> p n c", c=2),
                                      adab[:, bass.ds(16 + 4 * g, 4)].unsqueeze(2).to_broadcast([P, 4, 2]),
                                      ALU.add).then_inc(dve_took, 1)
                    for n, (t, c) in enumerate(G3):
                        dve.wait_ge(bank_ready, 8 + n)
                        col = kd[:, 0:P] if t < 8 else kd[:, P:2 * P]
                        dve.tensor_tensor(Q4(Kd)[:, t:t + c, :], Q4(ps[:, ring.bank(7 + n), 0:P * c]),
                                          col.unsqueeze(1).to_broadcast([P, c, P]), ALU.mult)\
                            .then_inc(dve_took, 1)
                    for h in range(2):
                        for n, (t, c) in enumerate(G3):
                            e = 10 + 3 * h + n
                            dve.wait_ge(bank_ready, e + 1)
                            dve.tensor_tensor(Q4(AT[h])[:, t:t + c, :], Q4(ps[:, ring.bank(e), 0:P * c]),
                                              DT[h].unsqueeze(1).to_broadcast([P, c, P]), ALU.mult)\
                                .then_inc(dve_took, 1)
                    dve.tensor_tensor(Q4(q), Q4(q), tiles_of(dq), ALU.mult).then_inc(conv_done, 1)
                    for t in range(NTILE):
                        n = 16 + t // 4
                        dve.wait_ge(bank_ready, n + 1)
                        upd = ps[:, ring.bank(n), P * (t % 4):P * (t % 4) + P]
                        if t == 0:
                            ins = dve.tensor_copy(S[:, 1, :], upd)
                        elif t < 8:
                            ins = dve.scalar_tensor_tensor(S[:, t + 1, :], S[:, t, :], dc[:, 0:1], upd,
                                                           ALU.mult, ALU.add)
                        else:
                            ins = dve.scalar_tensor_tensor(S[:, 10, :], S[:, 9, :], dc[:, 1:2], upd,
                                                           ALU.mult, ALU.add)
                        ins.then_inc(state_ready, 1)
                        dve.wait_ge(state_ready, t + 1)
                    dve.wait_ge(evacuated, 11)
                    finish_head(dve, link, 1, raw[0][:, 0:TOK], r[0][:, 0:TOK], nw[:, 0:1], zs[0])
                    for s, (a, w) in enumerate(SEGS):
                        finish_head(dve, link, 2 + s, raw[1][:, a:a + w], r[1][:, a:a + w], nw[:, 1:2],
                                    zs[1][:, a:a + w])
            barrier()

        def fox_group(L, g, ph):
            work = ph.enter_context(nc.sbuf_tensor("sb_fox", [P, 16600], F32))
            qT = work[:, 0:TOK]
            at = TOK
            kT = work[:, at:at + FKEYS]
            at += FKEYS
            V = work[:, at:at + 13 * P].rearrange("p (t c) -> p t c", c=P)
            at += 13 * P
            fk = work[:, at:at + 2 * FKEYS].rearrange("p (h c) -> p h c", h=2)
            at += 2 * FKEYS
            fd = work[:, at:at + 2 * 9 * P].rearrange("p (h t c) -> p h t c", h=2, t=9)
            at += 18 * P
            lg = work[:, at:at + 2048].rearrange("p (b c) -> p b c", b=2)
            at += 2048
            PT = work[:, at:at + 2048].rearrange("p (b c) -> p b c", b=2)
            at += 2048
            otok = work[:, at:at + 2 * P].rearrange("p (b c) -> p b c", b=2)
            at += 2 * P
            mx = work[:, at:at + 18 * 5].rearrange("p (s c) -> p s c", c=5)
            at += 90
            zs, oo = work[:, at:at + TOK], work[:, at + TOK:at + 2 * TOK]
            vT = oo
            gi = L * 4 + g
            VN = [(0, 4), (4, 4), (8, 1)]
            B0, NB = 6, 2
            steps = [(t, h) for t in range(9) for h in range(2)]

            def blocks_of(t):
                if t < 8:
                    return [(P * b, P, b) for b in range(t + 1)]
                return [(SEQ + P * b, P, 8 + b) for b in range(4)] + [(SCAN_OFF, DEC, 12)]

            entry = {}
            order = 3
            for s, (t, h) in enumerate(steps):
                for c in range((len(blocks_of(t)) + 3) // 4):
                    entry[("p", s, c)] = order
                    order += 1
                if h == 0 and t:
                    entry[("o", t - 1)] = order
                    order += 1
                entry[("v", s)] = order
                order += 1
            entry[("o", 8)] = order
            last_p = [max(v for e, v in entry.items() if e[0] == "p" and e[1] == s) for s in range(18)]
            with nc.Block() as block:
                @block.sync
                def _(sp):
                    sp.dma_start(fk.rearrange("p h c -> p (h c)"),
                                 dfk[bass.ds(2 * g, 2), :].rearrange("a c -> (a c)").partition_broadcast(P))\
                        .then_inc(hist_loaded, 16)
                    sp.dma_start(kT[:, SEQ:SEQ + PAST], row("kcT", gi)).then_inc(params_loaded, 16)
                    sp.dma_start(V[:, 8:12, :], row("vc", gi)).then_inc(params_loaded, 16)
                    reload_weights(sp, L * N_BLOCKS + 15 + g * 4 + 4, 4)
                    sp.wait_ge(act_took, 4)
                    sp.dma_start(row("p_k", gi), kT[:, 0:SEQ]).then_inc(stored, 16)
                    sp.dma_start(row("s_k", gi), kT[:, SCAN_OFF:FKEYS]).then_inc(stored, 16)
                    sp.wait_ge(dve_took, 3)
                    sp.dma_start(row("p_v", gi), V[:, 0:8, :]).then_inc(stored, 16)
                    sp.dma_start(row("s_v", gi), V[0:DEC, 12, :]).then_inc(stored, 16)
                    out = do[bass.ds(4 + g, 1)].rearrange("a p t -> (a p) t")
                    for i, (a, z) in enumerate(((0, SEQ), (SEQ, TOK))):
                        sp.wait_ge(out_took, i + 1)
                        sp.dma_start(out[:, a:z], zs[:, a:z]).then_inc(stored, 16)
                    sp.wait_ge(stored, 96)
                    all_loaded(sp, 4)

                @block.gpsimd
                def _(pool):
                    pool.wait_ge(hist_loaded, 16)
                    for h in range(2):
                        pool.tensor_tensor(fd[:, h, 0:8, :], Q4(fk[:, h, 0:SEQ]),
                                           causal.unsqueeze(1).to_broadcast([P, 8, P]), ALU.add)\
                            .then_inc(level_mask, 1)
                        pool.tensor_tensor(fd[:, h, 8, 0:DEC], fk[:, h, SCAN_OFF:FKEYS], causal[:, 0:DEC],
                                           ALU.add).then_inc(level_mask, 1)
                    split_blocks(pool, [3, 6, 9, 12])

                @block.tensor
                def _(pe):
                    for _ in project(pe, 0, B0, NB, 0):
                        pass
                    fill = blocks(pe, [(3, 1), (6, 2), (9, 3)], B0, NB)

                    def qk(s):
                        t, h = steps[s]
                        rows = P if t < 8 else DEC
                        blk = blocks_of(t)
                        lo, n = blk[0][0], sum(b[1] for b in blk)
                        if s >= 2:
                            pe.wait_ge(logits, s - 1)
                        for a in range(0, n, 512):
                            w = min(512, n - a)
                            mm = pe.matmul(ps[0:rows, 2 * (s % 2) + a // 512, 0:w],
                                           qT[64 * h:64 * h + 64, P * t:P * t + rows],
                                           kT[64 * h:64 * h + 64, lo + a:lo + a + w], start=True, stop=True)
                        mm.then_inc(scores_pe, 1)

                    def get(n):
                        if n >= 2:
                            pe.wait_ge(dve_took, n - 1)
                        return 4 + n % 2

                    def turn_out(t):
                        rows = P if t < 8 else DEC
                        b = get(entry[("o", t)])
                        pe.wait_ge(dve_took, entry[("v", 2 * t + 1)] + 1)
                        pe.transpose(ps[:, b, 0:rows], otok[0:rows, t % 2, :], ident[0:rows, 0:rows])\
                            .then_inc(bank_ready, 1)

                    pe.wait_ge(act_took, 4)
                    pe.wait_ge(params_loaded, 32)
                    qk(0)
                    turns(fill, 2)
                    for n, (t, c) in enumerate(VN):
                        pe.wait_ge(evacuated, 3)
                        b = get(n)
                        for j in range(c):
                            w = P if t < 8 else DEC
                            mm = pe.transpose(ps[0:w, b, P * j:P * j + P], vT[:, P * (t + j):P * (t + j) + w],
                                              ident)
                        mm.then_inc(bank_ready, 1)
                    for s, (t, h) in enumerate(steps):
                        if s + 1 < len(steps):
                            qk(s + 1)
                        turns(fill, 2 if s else 0)
                        rows = P if t < 8 else DEC
                        blk = blocks_of(t)
                        pe.wait_ge(probs, s + 1)
                        for c in range(0, len(blk), 4):
                            b = get(entry[("p", s, c // 4)])
                            for j, (col, w, _) in enumerate(blk[c:c + 4]):
                                mm = pe.transpose(ps[0:w, b, P * j:P * j + rows],
                                                  lg[0:rows, s % 2, (c + j) * P:(c + j) * P + w],
                                                  ident[0:rows, 0:rows])
                            mm.then_inc(bank_ready, 1)
                        if h == 0 and t:
                            turn_out(t - 1)
                        turns(fill, 3 if 1 <= s <= 4 else 2)
                        b = get(entry[("v", s)])
                        pe.wait_ge(dve_took, last_p[s] + 1)
                        for c, (col, w, vt) in enumerate(blk):
                            mm = pe.matmul(ps[0:rows, b, 0:64], PT[0:w, s % 2, P * c:P * c + rows],
                                           V[0:w, vt, 64 * h:64 * h + 64],
                                           start=(c == 0), stop=(c == len(blk) - 1))
                        mm.then_inc(bank_ready, 1)
                    turns(fill, 72)
                    turn_out(8)

                @block.scalar
                def _(act):
                    for x, dst in enumerate((qT, kT)):
                        for i, (u, a, w) in enumerate(PIECES):
                            b = SCAN_OFF if x == 1 and i == 1 else a
                            act.activation(dst[:, b:b + w], raw_qk[:, x, u:u + w], ACT.Copy).then_inc(act_took, 1)
                    for s, (a, w) in enumerate(SEGS):
                        take(act, s, B0, NB, vT[:, a:a + w])

                    def taken(m):
                        if m < 3:
                            a, w = SEGS[m]
                            take(act, 3 + m, B0, NB, zs[:, a:a + w], ACT.Silu)
                        else:
                            take_raw(act, 3 + m, 6, B0, NB)

                    for s, (t, h) in enumerate(steps):
                        rows = P if t < 8 else DEC
                        n = sum(b[1] for b in blocks_of(t))
                        act.wait_ge(exps, s + 1)
                        act.activation(lg[0:rows, s % 2, 0:n], lg[0:rows, s % 2, 0:n], ACT.Exp,
                                       bias=mx[0:rows, s, 2:3], accum_out=mx[0:rows, s, 3:4])\
                            .then_inc(probs, 1)
                        if s % 2 == 0 and s:
                            taken(s // 2 - 1)
                    taken(8)

                @block.vector
                def _(dve):
                    st = [0]

                    def link(ins):
                        wait_own(dve, ins, st, dve_step)

                    def maxima(s):
                        t, h = steps[s]
                        rows = P if t < 8 else DEC
                        blk = blocks_of(t)
                        lo, w = blk[0][0], blk[-1][1]
                        n = P * (len(blk) - 1)
                        dve.wait_ge(scores_pe, s + 1)
                        if s >= 2:
                            dve.wait_ge(bank_ready, last_p[s - 2] + 1)
                        src = ps[0:rows, 2 * (s % 2):2 * (s % 2) + 2, :].rearrange("p b c -> p (b c)")
                        if n:
                            dve.tensor_tensor_reduce(out=lg[0:rows, s % 2, 0:n], in0=src[:, 0:n],
                                                     in1=fk[0:rows, h, lo:lo + n], scale=0.125, scalar=-3e38,
                                                     op0=ALU.subtract, op1=ALU.max,
                                                     accum_out=mx[0:rows, s, 0:1])
                        dve.tensor_tensor_reduce(out=lg[0:rows, s % 2, n:n + w], in0=src[:, n:n + w],
                                                 in1=fd[0:rows, h, t, 0:w], scale=0.125, scalar=-3e38,
                                                 op0=ALU.subtract, op1=ALU.max,
                                                 accum_out=mx[0:rows, s, 1:2]).then_inc(logits, 1)
                        dve.wait_ge(logits, s + 1)
                        other = mx[0:rows, s, 0:1] if n else mx[0:rows, s, 1:2]
                        dve.tensor_scalar(mx[0:rows, s, 2:3], mx[0:rows, s, 1:2], other, -1.0,
                                          ALU.max, ALU.mult).then_inc(exps, 1)

                    def keep(t):
                        n = entry[("o", t)]
                        rows = P if t < 8 else DEC
                        dve.wait_ge(bank_ready, n + 1)
                        dve.tensor_copy(oo[:, P * t:P * t + rows], ps[:, 4 + n % 2, 0:rows]).then_inc(dve_took, 1)

                    dve.wait_ge(hist_loaded, 16)
                    dve.wait_ge(level_mask, 4)
                    maxima(0)
                    for n, (t, c) in enumerate(VN):
                        dve.wait_ge(bank_ready, n + 1)
                        rows, to = (P, t) if t < 8 else (DEC, 12)
                        dve.tensor_copy(V[0:rows, to:to + c, :], Q4(ps[0:rows, 4 + n % 2, 0:P * c]))\
                            .then_inc(dve_took, 1)
                    for s, (t, h) in enumerate(steps):
                        if s + 1 < len(steps):
                            maxima(s + 1)
                        rows = P if t < 8 else DEC
                        blk = blocks_of(t)
                        if s >= 2:
                            dve.wait_ge(bank_ready, entry[("v", s - 2)] + 1)
                        for c in range(0, len(blk), 4):
                            part = blk[c:c + 4]
                            n = entry[("p", s, c // 4)]
                            full = sum(1 for b in part if b[1] == P)
                            dve.wait_ge(bank_ready, n + 1)
                            src = ps[:, 4 + n % 2, 0:P * len(part)].rearrange("p (b c) -> p b c", c=P)
                            dst = PT[:, s % 2, P * c:P * (c + len(part))].rearrange("p (b c) -> p b c", c=P)
                            if full:
                                ins = dve.tensor_copy(dst[:, 0:full, 0:rows], src[:, 0:full, 0:rows])
                            else:
                                ins = dve.tensor_copy(dst[0:DEC, 0, 0:rows], src[0:DEC, 0, 0:rows])
                            ins.then_inc(dve_took, 1)
                        if h == 0 and t:
                            keep(t - 1)
                        dve.wait_ge(probs, s + 1)
                        link(dve.reciprocal(mx[0:rows, s, 4:5], mx[0:rows, s, 3:4]))
                        n = entry[("v", s)]
                        dve.wait_ge(bank_ready, n + 1)
                        dve.tensor_scalar(otok[0:rows, t % 2, 64 * h:64 * h + 64], ps[0:rows, 4 + n % 2, 0:64],
                                          mx[0:rows, s, 4:5], None, ALU.mult).then_inc(dve_took, 1)
                        if s == len(steps) - 2:
                            dve.wait_ge(evacuated, 6)
                            dve.wait_ge(dve_took, entry[("o", 7)] + 1)
                            dve.tensor_tensor(zs[:, 0:SEQ], zs[:, 0:SEQ], oo[:, 0:SEQ], ALU.mult)\
                                .then_inc(out_took, 1)
                    keep(8)
                    dve.wait_ge(dve_took, entry[("o", 8)] + 1)
                    dve.tensor_tensor(zs[:, SEQ:TOK], zs[:, SEQ:TOK], oo[:, SEQ:TOK], ALU.mult)\
                        .then_inc(out_took, 1)
            barrier()

        def delta_group(L, g, ph):
            work = ph.enter_context(nc.sbuf_tensor("sb_delta", [P, 16 * PADTOK + 1000], F32))

            def slab(i):
                return work[:, i * PADTOK:(i + 1) * PADTOK]
            ub = [raw_qk[:, 0, :], raw_qk[:, 1, :], work[:, 0:UW]]
            cv = [slab(2), slab(3), slab(4)]
            qT, kT, vT = cv
            Grow, brow, E, LT, XT, Kd, Vb = (slab(i) for i in (5, 6, 7, 8, 9, 10, 11))
            X, T, LM = brow, slab(0), [slab(1), slab(14)]
            AT = slab(13)
            sq = [slab(8), slab(9)]
            rt = [slab(13), slab(14)]
            raw, sqo, ro = slab(8), slab(0), slab(1)
            zs = slab(12)[:, 0:TOK]
            at = 16 * PADTOK
            gcol, bcol, nbg, kdc = (work[:, at + 9 * i:at + 9 * i + 9] for i in range(4))
            at += 36
            cw, nw = work[:, at:at + 12], work[:, at + 12:at + 13]
            at += 13
            S = work[:, at:at + 3 * P].rearrange("p (b c) -> p b c", b=3)
            R, U = slab(15)[:, 0:4 * P], slab(15)[:, 4 * P:8 * P]
            gi = L * 4 + g
            owners = ["act"] * 6 + ["dve"] * 6 + ["act"] * 6
            lev_first = []
            for s in LEVELS:
                lev_first.append(len(owners))
                owners += ["act"] * 3 + ["dve"] * (6 if s == 32 else 3)
            norm_first = len(owners)
            ring = Ring(owners, 0, 5)
            B0, NB, SUM_BANK = 5, 2, 7
            CHAIN = [8] + list(range(8))
            PARTS = [(0, 384), (384, 384), (768, TOK - 768)]

            def taken(who, n):
                return sum(o == who for o in owners[:n + 1])

            def turned(n):
                return min(n // 8, 6)

            def level_entry(i, n):
                return lev_first[i] + 3 + (2 * n if LEVELS[i] == 32 else n)

            level_turns = [2] * 4 + [1] * 2
            step_turns = [5] * 6 + [4] * 2 + [0]
            turns_before = [sum(level_turns) + sum(step_turns[:i]) for i in range(10)]

            with nc.Block() as block:
                @block.sync
                def _(sp):
                    for x in range(3):
                        sp.dma_start(ub[x][:, 3 + SEQ:6 + SEQ], row("hist", gi * 3 + x)).then_inc(hist_loaded, 16)
                    sp.dma_start(cw, row("cwT", gi)).then_inc(hist_loaded, 16)
                    sp.dma_start(nw, row("gnwT", L)).then_inc(params_loaded, 16)
                    sp.dma_start(Grow, dg[bass.ds(g, 1), :].rearrange("a c -> (a c)").partition_broadcast(P))\
                        .then_inc(params_loaded, 16)
                    sp.dma_start(brow, db[bass.ds(g, 1), :].rearrange("a c -> (a c)").partition_broadcast(P))\
                        .then_inc(params_loaded, 16)
                    with nc.allow_non_contiguous_dma(reason="a small turn of gates"):
                        sp.dma_start(gcol, dg[bass.ds(g, 1), :].rearrange("a (t p) -> (a p) t", p=P))\
                            .then_inc(params_loaded, 16)
                        sp.dma_start(bcol, db[bass.ds(g, 1), :].rearrange("a (t p) -> (a p) t", p=P))\
                            .then_inc(params_loaded, 16)
                    sp.dma_start(S[:, 2, :], row("sgdn", gi)).then_inc(params_loaded, 16)
                    for x in range(3):
                        if x == 2:
                            sp.wait_ge(evacuated, 3)
                        sp.dma_start(row("p_conv", gi * 3 + x), ub[x][:, SEQ:SEQ + 3]).then_inc(stored, 16)
                        sp.dma_start(row("s_conv", gi * 3 + x), ub[x][:, UW - 3:UW]).then_inc(stored, 16)
                    reload_weights(sp, L * N_BLOCKS + 31 + g * 4 + 4, 4)
                    sp.wait_ge(state_ready, 9)
                    sp.dma_start(row("p_gdn", gi), S[:, 0, :]).then_inc(stored, 16)
                    sp.dma_start(row("s_gdn", gi), S[:, 2, :]).then_inc(stored, 16)
                    out = do[bass.ds(8 + g, 1)].rearrange("a p t -> (a p) t")
                    sp.wait_ge(out_done, 2)
                    sp.dma_start(out[:, 0:768], zs[:, 0:768]).then_inc(stored, 16)
                    sp.wait_ge(out_done, 3)
                    sp.dma_start(out[:, 768:TOK], zs[:, 768:TOK]).then_inc(stored, 16)
                    sp.wait_ge(stored, 160)
                    all_loaded(sp, 4)

                @block.gpsimd
                def _(pool):
                    pool.wait_ge(params_loaded, 96)
                    pool.tensor_tensor(Q4(E), Q4(Grow), gcol.unsqueeze(2).to_broadcast([P, NTILE, P]),
                                       ALU.subtract).then_inc(beta_decay, 1)
                    pool.tensor_tensor(kdc.unsqueeze(2), Q4(Grow)[:, :, P - 1:P], gcol.unsqueeze(2),
                                       ALU.subtract)
                    pool.wait_ge(beta_decay, 1)
                    pool.tensor_tensor(Q4(E), Q4(E), tiles_of(future), ALU.subtract).then_inc(decays, 1)
                    pool.tensor_tensor(Q4(brow), Q4(brow), tiles_of(strict), ALU.mult).then_inc(beta_decay, 1)
                    pool.wait_ge(proj_done, 3)
                    split_block(pool, 2, 0, 1)
                    pool.wait_ge(exps, 1)
                    pool.wait_ge(beta_decay, 2)
                    pool.tensor_tensor(brow, brow, E, ALU.mult).then_inc(beta_decay, 1)
                    pool.wait_ge(dve_took, 3)
                    for i in range(len(LEVELS)):
                        if i >= 2:
                            pool.wait_ge(bank_ready, lev_first[i - 2] + 3)
                        pool.tensor_tensor(Q4(LM[i % 2]), Q4(LT), tiles_of(masks[:, 7 + i, :]), ALU.mult)\
                            .then_inc(level_mask, 1)
                        if i == 1:
                            pool.wait_ge(bank_ready, 12)
                            pool.wait_ge(exps, 3)
                            pool.tensor_tensor(qT, qT, Grow, ALU.mult).then_inc(decays, 1)
                    pool.wait_ge(proj_done, 6)
                    split_block(pool, 3, 1, 2)
                    for i in range(2):
                        pool.wait_ge(slot_loaded[i], 16)
                        pool.wait_ge(proj_done, 9 + 3 * i)
                        split_block(pool, i, i, 3 + i)

                @block.tensor
                def _(pe):
                    for _ in project(pe, 0, B0, NB, 0):
                        pass
                    fill = blocks(pe, [(3, 1), (6, 2), (9, 3)], B0, NB)

                    def turn(first, src):
                        for n, (t, c) in enumerate(G3):
                            ring.acquire(pe, first + n)
                            for j in range(c):
                                mm = pe.transpose(ps[:, ring.bank(first + n), P * j:P * j + P],
                                                  Q4(src)[:, t + j, :], ident)
                            mm.then_inc(bank_ready, 1)

                    def products(e, lhs, rhs, n):
                        t, c = G3[n]
                        ring.acquire(pe, e)
                        for j in range(c):
                            mm = pe.matmul(ps[:, ring.bank(e), P * j:P * j + P],
                                           Q4(lhs)[:, t + j, :], Q4(rhs)[:, t + j, :], start=True, stop=True)
                        mm.then_inc(bank_ready, 1)

                    def part_sums(p):
                        a, w = PARTS[p]
                        pe.wait_ge(squares, 3 + p)
                        if p:
                            pe.wait_ge(roots, p)
                        pe.matmul(ps[:, SUM_BANK, 0:w], ones, sqo[:, a:a + w], start=True, stop=True)\
                            .then_inc(norm_sums, 1)

                    turns(fill, 8)
                    pe.wait_ge(squares, 1)
                    sum_features(pe, ring, 0, sq[1])
                    turns(fill, 4)
                    pe.wait_ge(squares, 2)
                    sum_features(pe, ring, 3, sq[0])
                    turns(fill, 4)
                    pe.wait_ge(normed, 1)
                    for n in range(3):
                        products(6 + n, kT, kT, n)
                    turns(fill, 4)
                    pe.wait_ge(normed, 2)
                    for n in range(3):
                        products(9 + n, kT, qT, n)
                    turns(fill, 4)
                    turn(12, kT)
                    pe.wait_ge(silu_done, 3)
                    turn(15, vT)
                    for i in range(len(LEVELS)):
                        pe.wait_ge(level_mask, i + 1)
                        for n in range(3):
                            if i and LEVELS[i - 1] == 32:
                                pe.wait_ge(dve_took, taken("dve", level_entry(i - 1, n) + 1))
                            else:
                                pe.wait_ge(level_x, 3 * i + n + 1)
                            products(lev_first[i] + n, LM[i % 2], X, n)
                        turns(fill, level_turns[i])
                        for n in range(3):
                            pe.wait_ge(act_took, taken("act", lev_first[i] + n))
                            products(level_entry(i, n), T, XT, n)
                            if LEVELS[i] == 32:
                                products(level_entry(i, n) + 1, XT, T, n)
                    pe.wait_ge(act_took, taken("act", norm_first - 1))
                    pe.wait_ge(dve_took, taken("dve", norm_first - 1))
                    pe.wait_ge(decays, 2)
                    for i, t in enumerate(CHAIN):
                        src = S[:, 2 if t == 8 else t % 2, :]
                        if i:
                            pe.wait_ge(state_ready, i)
                        else:
                            pe.wait_ge(params_loaded, 96)
                            pe.wait_ge(cleared, 6)
                        pe.matmul(ps[:, 0, 0:P], Q4(kT)[:, t, :], src, start=True, stop=True)\
                            .then_inc(chain_pe, 1)
                        turns(fill, 2)
                        pe.wait_ge(rhs_ready, i + 1)
                        pe.matmul(ps[:, 1, 0:P], Q4(XT)[:, t, :], R[:, P * (i % 4):P * (i % 4) + P],
                                  start=True, stop=True).then_inc(chain_pe, 1)
                        if i >= 2:
                            pe.wait_ge(out_took, i - 1)
                        pe.matmul(ps[:, 3 + i % 2, 0:P], src, Q4(qT)[:, t, :], start=True, stop=False)
                        if i in (5, 7):
                            part_sums(i // 7)
                        turns(fill, 1)
                        pe.wait_ge(upd_ready, i + 1)
                        Ui = U[:, P * (i % 4):P * (i % 4) + P]
                        pe.matmul(ps[:, 2, 0:P], Q4(Kd)[:, t, :], Ui, start=True, stop=True)\
                            .then_inc(chain_pe, 1)
                        pe.matmul(ps[:, 3 + i % 2, 0:P], Ui, Q4(AT)[:, t, :], start=False, stop=True)\
                            .then_inc(out_pe, 1)
                        turns(fill, step_turns[i] - 3)
                    part_sums(2)

                @block.scalar
                def _(act):
                    def tap(x):
                        for u, a, w in ((0, 0, SEQ), (3 + SEQ, SEQ, DEC)):
                            ins = act.activation(cv[x][:, a:a + w], ub[x][:, u:u + w], ACT.Copy,
                                                 scale=cw[:, 4 * x:4 * x + 1])
                        ins.then_inc(tap_done, 1)

                    def silu(x, n):
                        act.wait_ge(conv_done, n)
                        act.activation(cv[x][:, 0:TOK], cv[x][:, 0:TOK], ACT.Silu).then_inc(silu_done, 1)

                    def square(x, n):
                        act.wait_ge(silu_done, n)
                        act.activation(sq[x][:, 0:TOK], cv[x][:, 0:TOK], ACT.Square).then_inc(squares, 1)

                    def z(s):
                        a, w = SEGS[s]
                        take(act, 3 + s, B0, NB, zs[:, a:a + w], ACT.Silu)

                    def roots_of(x, first):
                        for s, (a, w) in enumerate(SEGS):
                            act.wait_ge(bank_ready, first + s + 1)
                            act.activation(rt[x][:, a:a + w], ps[:, ring.bank(first + s), 0:w], ACT.Ln,
                                           bias=l2_c if x == 0 else eps_c,
                                           scale=float(P) if x == 0 else 1.0).then_inc(act_took, 1)

                    def tiles_out(dst, first, col):
                        for n, (t, c) in enumerate(G3):
                            act.wait_ge(bank_ready, first + n + 1)
                            for j in range(c):
                                ins = act.activation(Q4(dst)[:, t + j, :],
                                                     ps[:, ring.bank(first + n), P * j:P * j + P],
                                                     ACT.Copy, scale=col[:, t + j:t + j + 1])
                            ins.then_inc(act_took, 1)

                    def part_square(p):
                        a, w = PARTS[p]
                        act.wait_ge(out_took, (4, 7, 9)[p])
                        act.activation(sqo[:, a:a + w], raw[:, a:a + w], ACT.Square).then_inc(squares, 1)

                    def part_root(p):
                        a, w = PARTS[p]
                        act.wait_ge(norm_sums, p + 1)
                        act.activation(ro[:, a:a + w], ps[:, SUM_BANK, 0:w], ACT.Ln, bias=eps_c,
                                       scale=1.0 / P).then_inc(roots, 1)

                    def part_invert(p):
                        a, w = PARTS[p]
                        act.wait_ge(roots, p + 1)
                        act.activation(ro[:, a:a + w], ro[:, a:a + w], ACT.Exp, scale=-0.5)\
                            .then_inc(inverse, 1)

                    act.wait_ge(hist_loaded, 64)
                    tap(1)
                    tap(0)
                    for s in range(2):
                        take_into(act, s, s, B0, NB, ub[2])
                    silu(1, 1)
                    square(1, 1)
                    take_into(act, 2, 2, B0, NB, ub[2])
                    act.wait_ge(evacuated, 3)
                    act.wait_ge(cleared, 6)
                    tap(2)
                    silu(0, 2)
                    square(0, 2)
                    roots_of(1, 0)
                    roots_of(0, 3)
                    for n, x in enumerate((1, 0)):
                        act.wait_ge(act_took, 3 * (n + 1))
                        act.activation(rt[x][:, 0:TOK], rt[x][:, 0:TOK], ACT.Exp, scale=-0.5)\
                            .then_inc(inverse, 1)
                        if n == 0:
                            act.wait_ge(decays, 1)
                            act.activation(E, E, ACT.Exp).then_inc(exps, 1)
                    act.activation(kdc, kdc, ACT.Exp).then_inc(exps, 1)
                    act.activation(Grow, Grow, ACT.Exp).then_inc(exps, 1)
                    act.activation(gcol, gcol, ACT.Exp).then_inc(exps, 1)
                    z(0)
                    z(1)
                    silu(2, 3)
                    z(2)
                    act.wait_ge(exps, 2)
                    act.wait_ge(params_loaded, 96)
                    tiles_out(Kd, 12, kdc)
                    tiles_out(Vb, 15, bcol)
                    act.wait_ge(stored, 96)
                    for i in range(len(LEVELS)):
                        for n, (t, c) in enumerate(G3):
                            e = lev_first[i] + n
                            act.wait_ge(bank_ready, e + 1)
                            act.activation(Q4(T)[:, t:t + c, :], Q4(ps[:, ring.bank(e), 0:P * c]), ACT.Copy)\
                                .then_inc(act_took, 1)
                    for i, t in enumerate(CHAIN):
                        act.wait_ge(out_pe, i + 1)
                        act.activation(Q4(raw)[:, t, :], ps[:, 3 + i % 2, 0:P], ACT.Copy).then_inc(out_took, 1)
                        if i in (3, 6):
                            part_square(i // 5)
                        if i == 5:
                            part_root(0)
                            part_invert(0)
                        if i == 7:
                            part_root(1)
                        if i == 8:
                            part_square(2)
                            part_root(2)
                            part_invert(1)
                            part_invert(2)
                        for m in range(6):
                            if (turned(turns_before[i]) if i else 0) <= m < turned(turns_before[i + 1]):
                                take_raw(act, 6 + m, 6, B0, NB)

                @block.vector
                def _(dve):
                    st = [0]

                    def link(ins):
                        wait_own(dve, ins, st, dve_step)
                    dve.memset(ub[2][:, 0:3], 0.0).then_inc(cleared, 1)
                    dve.memset(S[:, 1, :], 0.0).then_inc(cleared, 1)
                    dve.memset(qT[:, TOK:PADTOK], 0.0).then_inc(cleared, 1)
                    dve.memset(kT[:, TOK:PADTOK], 0.0).then_inc(cleared, 1)
                    dve.memset(vT[:, TOK:PADTOK], 0.0).then_inc(cleared, 1)
                    dve.memset(S[:, 0, :], 0.0).then_inc(cleared, 1)
                    dve.wait_ge(cleared, 6)
                    dve.wait_ge(hist_loaded, 64)

                    def conv(x, n):
                        u, c = ub[x], cv[x]
                        dve.wait_ge(tap_done, n)
                        for j in range(1, 4):
                            for a, b, w in ((0, 0, SEQ), (3 + SEQ, SEQ, DEC)):
                                ins = dve.scalar_tensor_tensor(c[:, b:b + w], u[:, a + j:a + j + w],
                                                               cw[:, 4 * x + j:4 * x + j + 1], c[:, b:b + w],
                                                               ALU.mult, ALU.add)
                            if j == 3:
                                ins.then_inc(conv_done, 1)
                            else:
                                link(ins)

                    conv(1, 1)
                    conv(0, 2)
                    conv(2, 3)
                    for n, x in enumerate((1, 0)):
                        dve.wait_ge(inverse, n + 1)
                        dve.tensor_tensor(cv[x][:, 0:TOK], cv[x][:, 0:TOK], rt[x][:, 0:TOK], ALU.mult)\
                            .then_inc(normed, 1)
                    dve.wait_ge(params_loaded, 96)
                    dve.wait_ge(beta_decay, 3)
                    for n, (t, c) in enumerate(G3):
                        a, w = P * t, P * c
                        dve.wait_ge(bank_ready, 7 + n)
                        dve.tensor_tensor(LT[:, a:a + w], ps[:, ring.bank(6 + n), 0:w], brow[:, a:a + w],
                                          ALU.mult).then_inc(dve_took, 1)
                        dve.wait_ge(dve_took, n + 1)
                        link(dve.tensor_tensor(Q4(XT)[:, t:t + c, :], Q4(LT)[:, t:t + c, :],
                                               masks[:, 6, :].unsqueeze(1).to_broadcast([P, c, P]), ALU.mult))
                        link(dve.tensor_tensor(Q4(XT)[:, t:t + c, :],
                                               ident.unsqueeze(1).to_broadcast([P, c, P]),
                                               Q4(XT)[:, t:t + c, :], ALU.subtract))
                        dve.transpose(X[:, a:a + w], XT[:, a:a + w]).then_inc(level_x, 1)
                    for n, (t, c) in enumerate(G3):
                        dve.wait_ge(bank_ready, 10 + n)
                        dve.tensor_tensor(Q4(AT)[:, t:t + c, :], Q4(ps[:, ring.bank(9 + n), 0:P * c]),
                                          Q4(E)[:, t:t + c, :], ALU.mult).then_inc(dve_took, 1)
                    dve.wait_ge(exps, 4)
                    link(dve.scalar_tensor_tensor(nbg, bcol, -1.0, gcol, ALU.mult, ALU.mult))
                    for i, half in enumerate(LEVELS):
                        for n, (t, c) in enumerate(G3):
                            e, a, w = level_entry(i, n), P * t, P * c
                            dve.wait_ge(bank_ready, e + (2 if half == 32 else 1))
                            dve.tensor_tensor(XT[:, a:a + w], XT[:, a:a + w], ps[:, ring.bank(e), 0:w],
                                              ALU.subtract).then_inc(dve_took, 1)
                            dve.wait_ge(dve_took, taken("dve", e))
                            if half < 32:
                                dve.transpose(X[:, a:a + w], XT[:, a:a + w]).then_inc(level_x, 1)
                            elif half == 32:
                                dve.wait_ge(level_x, 3 * i + n + 1)
                                dve.tensor_tensor(X[:, a:a + w], X[:, a:a + w], ps[:, ring.bank(e + 1), 0:w],
                                                  ALU.subtract).then_inc(dve_took, 1)
                    dve.wait_ge(dve_took, taken("dve", norm_first - 1))

                    def finish(p, step):
                        a, w = PARTS[p]
                        r, o, gate = ro[:, a:a + w], raw[:, a:a + w], zs[:, a:a + w]
                        if step == 0:
                            dve.wait_ge(inverse, 3 + p)
                            link(dve.scalar_tensor_tensor(o, o, nw, r, ALU.mult, ALU.mult))
                        else:
                            dve.tensor_tensor(gate, gate, o, ALU.mult).then_inc(out_done, 1)

                    for i, t in enumerate(CHAIN):
                        Ri, Ui = (b[:, P * (i % 4):P * (i % 4) + P] for b in (R, U))
                        dve.wait_ge(chain_pe, 3 * i + 1)
                        dve.scalar_tensor_tensor(Ri, ps[:, 0, 0:P], nbg[:, t:t + 1], Q4(Vb)[:, t, :],
                                                 ALU.mult, ALU.add).then_inc(rhs_ready, 1)
                        dve.wait_ge(chain_pe, 3 * i + 2)
                        if i >= 4:
                            dve.wait_ge(out_pe, i - 3)
                        dve.tensor_copy(Ui, ps[:, 1, 0:P]).then_inc(upd_ready, 1)
                        src = S[:, 2 if t == 8 else t % 2, :]
                        dst = S[:, 2 if t == 8 else (t + 1) % 2, :]
                        dve.wait_ge(chain_pe, 3 * i + 3)
                        if t == 8:
                            dve.wait_ge(out_pe, 1)
                        elif i >= 2:
                            dve.wait_ge(out_pe, i)
                        dve.scalar_tensor_tensor(dst, src, Q4(Grow)[:, t, P - 1:P], ps[:, 2, 0:P],
                                                 ALU.mult, ALU.add).then_inc(state_ready, 1)
                        dve.wait_ge(state_ready, i + 1)
                        if i in (6, 7):
                            finish(0, i - 6)
                    for p in (1, 2):
                        finish(p, 0)
                        finish(p, 1)
            barrier()

        def merge(L, ph):
            NU = 24
            work = ph.enter_context(nc.sbuf_tensor("sb_merged", [P, KC * TOK + TOK], F32))
            mg = work[:, 0:KC * TOK].rearrange("p (k t) -> p k t", k=KC)
            os = ph.enter_context(nc.sbuf_tensor("sb_o_split", [P, 2, 4, TOK], F32R))
            wbs = ph.enter_context(nc.sbuf_tensor("sb_wb_split", [P, 2, 2, 4, P], F32R))
            extra = work[:, KC * TOK:KC * TOK + TOK]

            def gate(u, s):
                if u < 2:
                    return [(raw_qk[:, u, b:b + w], c, w) for b, c, w in RAW_SEGS[s]]
                a, w = SEGS[s]
                return [((raw_qk[:, 0], raw_qk[:, 1], extra)[u % 3][:, a:a + w], 0, w)]

            def wb_raw(u):
                return wraw[:, 4 + (u % 4) // 2, 4 * (u % 2):4 * (u % 2) + 4, :]

            def xbuf(j):
                return (raw_qk[:, 0, 0:TOK], raw_qk[:, 1, 0:TOK], extra)[j % 3]

            NBLK = 22 + KC
            first = L * N_BLOCKS + 47
            with nc.Block() as block:
                @block.sync
                def _(sp):
                    def load_o(n):
                        for k in range(4):
                            sp.dma_start(os[:, 1, k, :].bitcast(F32), do[4 * n + k]).then_inc(o_loaded, 16)

                    def load_wb(u):
                        sp.dma_start(wb_raw(u), row("wbr", L * NU + u)).then_inc(branch_loaded[u % 4], 16)

                    def load_block(b):
                        sp.dma_start(wraw[:, b % 4], row("wblk", first + b)).then_inc(slot_loaded[b % 4], 16)

                    def load_x(j):
                        sp.dma_start(xbuf(j), dx[j]).then_inc(x_loaded[j % 3], 16)

                    load_o(0)
                    for u in range(4):
                        load_wb(u)
                    load_block(4)
                    load_block(5)
                    for u in range(NU):
                        if u == NU - 2:
                            for j in range(3):
                                sp.wait_ge(merged, 3 * (14 + j))
                                load_x(j)
                        sp.wait_ge(split_ready, u + 1)
                        load_block(u + 6)
                        if u in (7, 15):
                            sp.wait_ge(bank_ready, 3 * (u + 1))
                            load_o((u + 1) // 8)
                        if u + 6 < NU:
                            if u == 0:
                                sp.wait_ge(branch_ready, 1)
                                load_wb(4)
                                sp.wait_ge(branch_ready, 2)
                                load_wb(5)
                            sp.wait_ge(branch_ready, u + 3)
                            load_wb(u + 6)
                    for j in range(KC):
                        sp.wait_ge(dve_took, 3 * (j + 1))
                        sp.dma_start(dx[j], xbuf(j)).then_inc(x_stored[j % 3], 16)
                        if j + 3 < KC:
                            sp.wait_ge(x_stored[j % 3], 16 * (j // 3 + 1))
                            load_x(j + 3)
                        if j == 5:
                            sp.wait_ge(split_ready, NBLK - 2)
                            for n in range(4):
                                sp.dma_start(wraw[:, n], row("adaw", L * 24 + 24 + n)).then_inc(params_loaded, 16)
                    for i in range(3):
                        sp.wait_ge(x_stored[i], 16 * len(range(i, KC, 3)))
                    sp.wait_ge(params_loaded, 64)

                @block.gpsimd
                def _(pool):
                    def split_wb(u):
                        pool.wait_ge(branch_loaded[u % 4], 16 * (u // 4 + 1))
                        pool.tensor_copy(wbs[:, u % 2, 0], wb_raw(u)).then_inc(branch_hi, 1)
                        pool.wait_ge(branch_hi, u + 1)
                        pool.tensor_tensor(wbs[:, u % 2, 1], wb_raw(u), wbs[:, u % 2, 0].bitcast(F32),
                                           ALU.subtract).then_inc(branch_ready, 1)

                    split_wb(0)
                    split_wb(1)
                    for b in range(2, NBLK):
                        if b < 24:
                            pool.wait_ge(proj_done, 3 * (b - 1))
                        else:
                            pool.wait_ge(bank_ready, 3 * NU + 3 * (b - 23))
                        if b >= 4:
                            pool.wait_ge(slot_loaded[b % 4], 16 * (b // 4))
                        split_block(pool, b % 4, b % 2, b - 1)
                        if b < NU:
                            pool.wait_ge(bank_ready, 3 * (b - 1))
                            split_wb(b)

                @block.tensor
                def _(pe):
                    for u in range(NU):
                        if u + 2 < NU:
                            if u >= 2:
                                pe.wait_ge(split_ready, u - 1)
                            for _ in project(pe, 3 * u, 0, 4, u % 2):
                                pass
                        pe.wait_ge(branch_ready, u + 1)
                        for s, (a, w) in enumerate(SEGS):
                            f = 3 * u + s
                            if f >= 4:
                                pe.wait_ge(scaled, f - 3)
                            for k in range(4):
                                if u % 8 == 0 and s == 0:
                                    pe.wait_ge(h_ready, 4 * (u // 8) + k + 1)
                                mm = three(pe, ps[:, 4 + f % 4, 0:w], wbs[:, u % 2, 0, k, :],
                                           wbs[:, u % 2, 1, k, :], os[:, 0, k, a:a + w], os[:, 1, k, a:a + w],
                                           k == 0, k == 3)
                            mm.then_inc(bank_ready, 1)
                    for j in range(KC):
                        b = 22 + j
                        pe.wait_ge(split_ready, b - 1)
                        for s, (a, w) in enumerate(SEGS):
                            f = 3 * (NU + j) + s
                            m = f - 4
                            pe.wait_ge(*((scaled, m + 1) if m < 3 * NU else (dve_took, m + 1 - 3 * NU)))
                            for k in range(KC):
                                if j == 0 and s == 0:
                                    pe.wait_ge(normed, k + 1)
                                mm = three(pe, ps[:, 4 + f % 4, 0:w], ws[:, b % 2, 0, k, :],
                                           ws[:, b % 2, 1, k, :], hs[:, 0, k, a:a + w], hs[:, 1, k, a:a + w],
                                           k == 0, k == KC - 1)
                            mm.then_inc(bank_ready, 1)

                @block.scalar
                def _(act):
                    for u in range(2):
                        for s in range(3):
                            for dst, _, _ in gate(u, s):
                                ins = act.activation(dst, dst, ACT.Sigmoid)
                        ins.then_inc(probs, 1)
                    for u in range(NU):
                        if u % 8 == 0:
                            act.wait_ge(o_loaded, 64 * (u // 8 + 1))
                            for k in range(4):
                                act.activation(os[:, 0, k, :], os[:, 1, k, :].bitcast(F32), ACT.Copy)\
                                    .then_inc(h_hi, 1)
                        if u + 2 < NU:
                            if u:
                                act.wait_ge(scaled if u <= 8 else merged, 3 * u if u <= 8 else 3 * (u - 8))
                            for s in range(3):
                                take(act, 3 * u + s, 0, 4, gate(u + 2, s)[0][0], ACT.Sigmoid)
                    act.wait_ge(proj_done, 3 * 22)
                    for k in range(KC):
                        act.wait_ge(merged, 3 * (9 + k))
                        act.activation(hs[:, 0, k, :], mg[:, k, :], ACT.Copy).then_inc(level_x, 1)

                @block.vector
                def _(dve):
                    def low(k):
                        dve.wait_ge(level_x, k + 1)
                        dve.tensor_tensor(hs[:, 1, k, :], mg[:, k, :], hs[:, 0, k, :].bitcast(F32),
                                          ALU.subtract).then_inc(normed, 1)

                    for u in range(NU):
                        br, c = divmod(u, 8)
                        if c == 0:
                            for k in range(4):
                                dve.wait_ge(h_hi, 4 * br + k + 1)
                                dve.tensor_tensor(os[:, 1, k, :], os[:, 1, k, :].bitcast(F32),
                                                  os[:, 0, k, :].bitcast(F32), ALU.subtract).then_inc(h_ready, 1)
                        if u < 2:
                            dve.wait_ge(probs, u + 1)
                        for s, (a, w) in enumerate(SEGS):
                            f = 3 * u + s
                            if u >= 2:
                                dve.wait_ge(evacuated, 3 * (u - 2) + s + 1)
                            dve.wait_ge(bank_ready, f + 1)
                            for g_, b, n in gate(u, s):
                                ins = dve.tensor_tensor(g_ if br else mg[:, c, a + b:a + b + n],
                                                        ps[:, 4 + f % 4, b:b + n], g_, ALU.mult)
                            ins.then_inc(scaled, 1)
                            if br:
                                dve.wait_ge(scaled, f + 1)
                                dve.tensor_tensor(mg[:, c, a:a + w], mg[:, c, a:a + w], g_, ALU.add)\
                                    .then_inc(merged, 1)
                        if u == 21:
                            for k in range(6):
                                low(k)
                        elif u > 21:
                            low(u - 16)
                    for j in range(KC):
                        dve.wait_ge(x_loaded[j % 3], 16 * (j // 3 + 1))
                        for s, (a, w) in enumerate(SEGS):
                            f = 3 * (NU + j) + s
                            dve.wait_ge(bank_ready, f + 1)
                            for c, (_, b, n) in enumerate(RAW_SEGS[s]):
                                ins = dve.scalar_tensor_tensor(xbuf(j)[:, a + b:a + b + n],
                                                               ps[:, 4 + f % 4, b:b + n],
                                                               modT[:, 16 + j, c:c + 1],
                                                               xbuf(j)[:, a + b:a + b + n],
                                                               ALU.mult, ALU.add)
                            ins.then_inc(dve_took, 1)
            with nc.Block() as block:
                @block.vector
                def _(dve):
                    dve.memset(raw_qk[:, :, 0:3], 0.0)
            barrier()

        with nc.Fori(0, DEPTH) as L:
            with ExitStack() as ph:
                norm_phase(False, L, ph)
            with nc.Fori(0, 2) as g, ExitStack() as ph:
                retention_group(L, g, ph)
            with nc.Fori(0, 4) as g, ExitStack() as ph:
                fox_group(L, g, ph)
            with nc.Fori(0, 4) as g, ExitStack() as ph:
                delta_group(L, g, ph)
            with ExitStack() as ph:
                merge(L, ph)
        with ExitStack() as ph:
            norm_phase(True, None, ph)


OUTS = {
    "yT": (KC, P, TOK),
    "p_k": (8, P, SEQ), "p_v": (8, P, 8, P), "p_logf": (2, 8, SEQ), "p_ret": (4, P, P), "p_gdn": (8, P, P),
    "p_conv": (24, P, 3),
    "s_k": (8, P, DEC), "s_v": (8, DEC, P), "s_logf": (2, 8, DEC), "s_ret": (4, P, P), "s_gdn": (8, P, P),
    "s_conv": (24, P, 3),
}


def column_blocks():
    ret, fox, gdn, gates = 0, 1536, 3592, 5648
    own, qk = [], []
    for g in range(2):
        qk.append([ret + g * 128, ret + 256 + g * 128])
        own.append([ret + c + g * 256 for c in (512, 640, 1024, 1152)])
    for first in (fox, gdn):
        for g in range(4):
            qk.append([first + g * 128, first + 512 + g * 128])
            own.append([first + 1024 + g * 128, first + 1544 + g * 128])
    units = [gates + n * 1024 + d * 128 for n in range(3) for d in range(8)]
    qk.append(units[:2])
    cols = list(qk[0])
    for g, c in enumerate(own):
        cols += c + qk[g + 1]
    return cols + units[2:]


def kernel(**inputs):
    import concourse.bacc as _bacc
    from concourse.bass_utils import run_bass_kernel_spmd as _run

    a = {n: np.asarray(v) for n, v in inputs.items()}
    w_in = a["w_in"]

    def blocked(w):
        return w.reshape(KC, P, -1, P).transpose(2, 1, 0, 3)

    wsm = np.zeros((DEPTH, D, P), np.float32)
    wsm[:, :, 0:8] = w_in[:, :, 3072:3080]
    wsm[:, :, 32:36] = w_in[:, :, 5128:5132]
    wsm[:, :, 64:68] = w_in[:, :, 5132:5136]
    stream = [np.concatenate([blocked(wsm[l])] + [blocked(w_in[l][:, c:c + P]) for c in column_blocks()]
                             + [blocked(a["w_out"][l])]) for l in range(DEPTH)]
    gcols = np.zeros((DEPTH, 96, 4), np.float32)
    gcols[:, 0:8, 0] = a["fox_f_bias"]
    gcols[:, 32:36, 0] = a["gdn_dt_bias"]
    gcols[:, 32:36, 1] = a["gdn_a_log"]
    masks, rot, retc = shape_constants()
    x = np.concatenate([a["x_prompt"][0], a["x_sample"][0]])
    cvec = np.stack([a["c_prompt"][0], a["c_sample"][0]])
    conv_w = a["gdn_conv_w"].reshape(DEPTH, 4, 3, 4, P).transpose(0, 3, 4, 2, 1)
    hist = a["state_gdn_conv"].reshape(DEPTH, 3, 3, 4, P).transpose(0, 3, 2, 4, 1)
    arrays = {
        "xT": x.T.reshape(KC, P, TOK),
        "cT": cvec.T.reshape(KC, P, 2).transpose(1, 0, 2),
        "masks": masks, "rot": rot, "retc": retc,
        "wblk": np.concatenate(stream),
        "wbr": a["w_branch"].reshape(DEPTH, 3, 4, P, 8, P).transpose(0, 1, 4, 3, 2, 5).reshape(48, P, 4, P),
        "adaw": np.concatenate([blocked(a["ada_w"][l]) for l in range(DEPTH)] + [np.zeros((4, P, KC, P), np.float32)]),
        "adabT": a["ada_b"].reshape(DEPTH, 24, P).transpose(0, 2, 1),
        "nwT": a["norm_w"].reshape(DEPTH, KC, P).transpose(0, 2, 1),
        "fnwT": a["final_norm_w"].reshape(KC, P).T,
        "gcols": gcols,
        "lfc": a["cache_fox_logf"][:, 0],
        "rnwT": a["ret_norm_w"].reshape(DEPTH * 2, 2, P).transpose(0, 2, 1),
        "gnwT": a["gdn_norm_w"].reshape(DEPTH, P, 1),
        "sret": a["state_ret"].reshape(DEPTH * 2, P, P),
        "sgdn": a["state_gdn"].reshape(DEPTH * 4, P, P),
        "kcT": a["cache_fox_k"].reshape(DEPTH * 4, 2, PAST, 64).transpose(0, 1, 3, 2).reshape(8, P, PAST),
        "vc": a["cache_fox_v"].reshape(DEPTH * 4, 2, 4, P, 64).transpose(0, 3, 2, 1, 4).reshape(8, P, 4, P),
        "cwT": conv_w.reshape(8, P, 12),
        "hist": hist.reshape(24, P, 3),
    }
    arrays = {n: np.ascontiguousarray(v) for n, v in arrays.items()}
    nc = _bacc.Bacc("TRN2", target_bir_lowering=False, num_devices=1)
    A = {n: nc.dram_tensor("in_" + n, v.shape, F32, kind="ExternalInput").ap() for n, v in arrays.items()}
    O = {n: nc.dram_tensor("out_" + n, s, F32, kind="ExternalOutput").ap() for n, s in OUTS.items()}
    build(nc, A, O)
    r = _run(nc, [{"in_" + n: v for n, v in arrays.items()}], core_ids=[0])
    o = {n: np.asarray(r.results[0]["out_" + n]) for n in OUTS}
    y = o["yT"].reshape(D, TOK).T

    def heads_k(v, n):
        return v.reshape(DEPTH, 1, 8, 64, n).transpose(0, 1, 2, 4, 3)

    def conv(v):
        return v.reshape(DEPTH, 4, 3, P, 3).transpose(0, 4, 2, 1, 3).reshape(DEPTH, 1, 3, 1536)

    p_v = o["p_v"].reshape(DEPTH, 4, P, 8, 2, 64).transpose(0, 1, 4, 3, 2, 5).reshape(DEPTH, 1, 8, SEQ, 64)
    s_v = o["s_v"].reshape(DEPTH, 4, DEC, 2, 64).transpose(0, 1, 3, 2, 4).reshape(DEPTH, 1, 8, DEC, 64)
    out = (y[None, :SEQ], y[None, SEQ:],
           heads_k(o["p_k"], SEQ), p_v, o["p_logf"].reshape(DEPTH, 1, 8, SEQ),
           o["p_ret"].reshape(DEPTH, 1, 4, 64, P), o["p_gdn"].reshape(DEPTH, 1, 4, P, P), conv(o["p_conv"]),
           heads_k(o["s_k"], DEC), s_v, o["s_logf"].reshape(DEPTH, 1, 8, DEC),
           o["s_ret"].reshape(DEPTH, 1, 4, 64, P), o["s_gdn"].reshape(DEPTH, 1, 4, P, P), conv(o["s_conv"]))
    return tuple(np.ascontiguousarray(v) for v in out)
```
